# Optimizing a Trainium2 kernel written in Bass

```python
import math
import jax, jax.numpy as jnp
from jax import lax
import numpy as np

D_MODEL = 1024
BATCH = 1
SEQ = 256
DEPTH = 2

GRID_W = 64
N_HEADS = 16
N_KV_HEADS = 4
HEAD_DIM = D_MODEL // N_HEADS
GROUP = N_HEADS // N_KV_HEADS
Q_BLOCK = 128
ROPE_THETA = 10000.0
ATTN_QKV = N_HEADS * HEAD_DIM + 2 * N_KV_HEADS * HEAD_DIM
GLA_HEADS = 4
GLA_DK = D_MODEL // 2 // GLA_HEADS
GLA_DV = D_MODEL // GLA_HEADS
GLA_QK = GLA_HEADS * GLA_DK
GLA_V = GLA_HEADS * GLA_DV
GATE_RANK = 16
GATE_TAU = 16.0
GLA_CHUNK = 64
GLA_IN = 2 * GLA_QK + 2 * GLA_V + 2 * GATE_RANK
D_FF = 4 * D_MODEL
N_MIXERS = 2
N_ATTN = (DEPTH + 1) // 2
N_GLA = DEPTH // 2
EPS = 1e-6


def rmsnorm(x, g):
    x32 = x.astype(jnp.float32)
    y = x32 * lax.rsqrt(jnp.mean(x32 * x32, axis=-1, keepdims=True) + EPS)
    return (y * g.astype(jnp.float32)).astype(x.dtype)

def rope_angles(pos, dim):
    inv = ROPE_THETA ** (-jnp.arange(0, dim, 2, dtype=jnp.float32) / dim)
    ang = pos.astype(jnp.float32)[:, None] * inv[None, :]
    return jnp.cos(ang), jnp.sin(ang)

def apply_rot(x, cos, sin):
    half = x.shape[-1] // 2
    x32 = x.astype(jnp.float32)
    x1, x2 = x32[..., :half], x32[..., half:]
    c = cos[None, :, None, :]
    s = sin[None, :, None, :]
    return jnp.concatenate([x1 * c - x2 * s, x2 * c + x1 * s], axis=-1).astype(x.dtype)

def axial_rope(x, rope):
    cr, sr, cc, sc = rope
    half = HEAD_DIM // 2
    return jnp.concatenate([apply_rot(x[..., :half], cr, sr), apply_rot(x[..., half:], cc, sc)], axis=-1)

def attention_mixer(h, w_qkv, q_g, k_g, w_o, rope):
    B, S, _ = h.shape
    qkv = h @ w_qkv
    q, k, v = jnp.split(qkv, [N_HEADS * HEAD_DIM, (N_HEADS + N_KV_HEADS) * HEAD_DIM], axis=-1)
    q = rmsnorm(q.reshape(B, S, N_HEADS, HEAD_DIM), q_g)
    k = rmsnorm(k.reshape(B, S, N_KV_HEADS, HEAD_DIM), k_g)
    v = v.reshape(B, S, N_KV_HEADS, HEAD_DIM)
    q = axial_rope(q, rope)
    k = axial_rope(k, rope)
    n_blk = S // Q_BLOCK
    qb = jnp.moveaxis(q.reshape(B, n_blk, Q_BLOCK, N_KV_HEADS, GROUP, HEAD_DIM), 1, 0)
    scale = 1.0 / math.sqrt(HEAD_DIM)

    def block(qblk):
        s = jnp.einsum('bqhgd,bkhd->bhgqk', qblk, k, preferred_element_type=jnp.float32) * scale
        p = jax.nn.softmax(s, axis=-1).astype(v.dtype)
        return jnp.einsum('bhgqk,bkhd->bqhgd', p, v)

    o = lax.map(block, qb)
    o = jnp.moveaxis(o, 0, 1).reshape(B, S, N_HEADS * HEAD_DIM)
    return o @ w_o

def gla_chunked(q, k, v, logg):
    B, S, H, DK = q.shape
    DV = v.shape[-1]
    N = S // GLA_CHUNK
    to_c = lambda t: t.reshape(B, N, GLA_CHUNK, H, t.shape[-1]).transpose(0, 3, 1, 2, 4)
    q, k, v, logg = to_c(q), to_c(k), to_c(v), to_c(logg)
    b = jnp.cumsum(logg, axis=3)
    qe = q * jnp.exp(b)
    ke = k * jnp.exp(-b)
    mask = jnp.tril(jnp.ones((GLA_CHUNK, GLA_CHUNK), dtype=bool))
    a = jnp.einsum('bhncd,bhnjd->bhncj', qe, ke)
    a = jnp.where(mask, a, 0.0)
    o_intra = jnp.einsum('bhncj,bhnjv->bhncv', a, v)
    b_last = b[..., -1:, :]
    kd = k * jnp.exp(b_last - b)
    chunk_kv = jnp.einsum('bhncd,bhncv->bhndv', kd, v)
    decay = jnp.exp(b_last[..., 0, :])

    def step(state, inp):
        dec, ckv = inp
        return dec[..., None] * state + ckv, state

    init = jnp.zeros((B, H, DK, DV), jnp.float32)
    _, s_before = lax.scan(step, init, (jnp.moveaxis(decay, 2, 0), jnp.moveaxis(chunk_kv, 2, 0)))
    s_before = jnp.moveaxis(s_before, 0, 2)
    o = o_intra + jnp.einsum('bhncd,bhndv->bhncv', qe, s_before)
    return o.transpose(0, 2, 3, 1, 4).reshape(B, S, H, DV)

def gla_mixer(h, w_in, w_gate_up, b_gate, out_g, w_o):
    B, S, _ = h.shape
    f32 = jnp.float32
    proj = h @ w_in
    q, k, v, r, z = jnp.split(proj, [GLA_QK, 2 * GLA_QK, 2 * GLA_QK + GLA_V, 2 * GLA_QK + 2 * GLA_V], axis=-1)
    q = q.astype(f32).reshape(B, S, GLA_HEADS, GLA_DK) * (GLA_DK ** -0.5)
    k = k.astype(f32).reshape(B, S, GLA_HEADS, GLA_DK)
    v = v.astype(f32).reshape(B, S, GLA_HEADS, GLA_DV)
    z = z.astype(f32).reshape(B, S, 2, GATE_RANK)
    logit = jnp.einsum('bsir,ire->bsie', z, w_gate_up.astype(f32)) + b_gate.astype(f32)
    logg = (jax.nn.log_sigmoid(logit) / GATE_TAU).reshape(B, S, 2, GLA_HEADS, GLA_DK)
    o_f = gla_chunked(q, k, v, logg[:, :, 0])
    flip = lambda t: jnp.flip(t, axis=1)
    o_b = flip(gla_chunked(flip(q), flip(k), flip(v), flip(logg[:, :, 1])))
    o = rmsnorm(o_f + o_b, out_g).reshape(B, S, GLA_V)
    o = o * jax.nn.silu(r.astype(f32))
    return o.astype(h.dtype) @ w_o

def sq_relu_mlp(h, w_in, w_out):
    return jnp.square(jax.nn.relu(h @ w_in)) @ w_out

def first_inputs(seed: int = 0) -> dict:
    key = jax.random.key(seed)
    ks = jax.random.split(key, 16)
    nrm = lambda k, shape, fan_in: jax.random.normal(k, shape, jnp.float32) * (fan_in ** -0.5)
    gain = lambda k, shape: 1.0 + 0.05 * jax.random.normal(k, shape, jnp.float32)
    return {
        'x': jax.random.normal(ks[0], (BATCH, SEQ, D_MODEL), jnp.float32),
        'norm_mix': gain(ks[1], (DEPTH, D_MODEL)),
        'norm_mlp': gain(ks[2], (DEPTH, D_MODEL)),
        'attn_w_qkv': nrm(ks[3], (N_ATTN, D_MODEL, ATTN_QKV), D_MODEL),
        'attn_q_norm': gain(ks[4], (N_ATTN, HEAD_DIM)),
        'attn_k_norm': gain(ks[5], (N_ATTN, HEAD_DIM)),
        'attn_w_o': nrm(ks[6], (N_ATTN, N_HEADS * HEAD_DIM, D_MODEL), N_HEADS * HEAD_DIM),
        'gla_w_in': nrm(ks[7], (N_GLA, D_MODEL, GLA_IN), D_MODEL),
        'gla_w_gate_up': nrm(ks[8], (N_GLA, 2, GATE_RANK, GLA_QK), GATE_RANK),
        'gla_b_gate': 0.1 * jax.random.normal(ks[9], (N_GLA, 2, GLA_QK), jnp.float32),
        'gla_out_norm': gain(ks[10], (N_GLA, GLA_DV)),
        'gla_w_o': nrm(ks[11], (N_GLA, GLA_V, D_MODEL), GLA_V),
        'mlp_w_in': nrm(ks[12], (DEPTH, D_MODEL, D_FF), D_MODEL),
        'mlp_w_out': nrm(ks[13], (DEPTH, D_FF, D_MODEL), D_FF),
        'final_norm': gain(ks[14], (D_MODEL,)),
    }

def first_block(x, norm_mix, norm_mlp, attn_w_qkv, attn_q_norm, attn_k_norm, attn_w_o,
              gla_w_in, gla_w_gate_up, gla_b_gate, gla_out_norm, gla_w_o,
              mlp_w_in, mlp_w_out, final_norm):
    S = x.shape[1]
    rows = S // GRID_W
    row = jnp.repeat(jnp.arange(rows, dtype=jnp.int32), GRID_W)
    col = jnp.tile(jnp.arange(GRID_W, dtype=jnp.int32), rows)
    cr, sr = rope_angles(row, HEAD_DIM // 2)
    cc, sc = rope_angles(col, HEAD_DIM // 2)
    rope = (cr, sr, cc, sc)
    h = x
    for i in range(DEPTH):
        j = i // N_MIXERS
        hn = rmsnorm(h, norm_mix[i])
        if i % N_MIXERS == 0:
            h = h + attention_mixer(hn, attn_w_qkv[j], attn_q_norm[j], attn_k_norm[j], attn_w_o[j], rope)
        else:
            h = h + gla_mixer(hn, gla_w_in[j], gla_w_gate_up[j], gla_b_gate[j], gla_out_norm[j], gla_w_o[j])
        h = h + sq_relu_mlp(rmsnorm(h, norm_mlp[i]), mlp_w_in[i], mlp_w_out[i])
    return rmsnorm(h, final_norm)


N_ATTN_HEADS = 8
ATTN_HEAD_DIM = 64
ATTN_WIDTH = N_ATTN_HEADS * ATTN_HEAD_DIM
MOBA_BLOCK = 256
MOBA_TOPK = 3
Q_CHUNK = 16
CONV_WIDTH = 512
CONV_K = 3
N_BRANCH = 2
SPLIT_SIZES = (ATTN_WIDTH, ATTN_WIDTH, ATTN_WIDTH, CONV_WIDTH, CONV_WIDTH, CONV_WIDTH, D_MODEL, D_MODEL)
IN_COLS = sum(SPLIT_SIZES)
SPLIT_POINTS = tuple(int(s) for s in np.cumsum(SPLIT_SIZES)[:-1])
PEER_HEADS = 8
PEER_NKEYS = 128
PEER_EXPERTS = PEER_NKEYS * PEER_NKEYS
PEER_DKEY = 256
PEER_HALF = PEER_DKEY // 2
PEER_TOPK = 16
PEER_TOK_CHUNK = 128

NORM_EPS = 1e-6
MASK_VALUE = -1e30


def rmsnorm_2(x, g):
    xf = x.astype(jnp.float32)
    y = xf * lax.rsqrt(jnp.mean(xf * xf, axis=-1, keepdims=True) + NORM_EPS)
    return (y * g.astype(jnp.float32)).astype(x.dtype)

def alibi_slopes(n):
    return jnp.asarray(np.array([2.0 ** (-8.0 * (h + 1) / n) for h in range(n)], dtype=np.float32))

def moba_attention(q, k, v, slopes):
    B, S, H, hd = q.shape
    nb = -(-S // MOBA_BLOCK)
    pad = nb * MOBA_BLOCK - S
    ksel = min(MOBA_TOPK, nb - 1)
    scale = hd ** -0.5
    q = q.transpose(0, 2, 1, 3)
    k = jnp.pad(k.transpose(0, 2, 1, 3), ((0, 0), (0, 0), (0, pad), (0, 0)))
    v = jnp.pad(v.transpose(0, 2, 1, 3), ((0, 0), (0, 0), (0, pad), (0, 0)))
    kb = k.reshape(B, H, nb, MOBA_BLOCK, hd)
    vb = v.reshape(B, H, nb, MOBA_BLOCK, hd)
    qblk = jnp.arange(S, dtype=jnp.int32) // MOBA_BLOCK
    nc = S // Q_CHUNK

    def chunks(a):
        return jnp.moveaxis(a.reshape(B, H, nc, Q_CHUNK, *a.shape[3:]), 2, 0)

    xs = {"q": chunks(q), "start": jnp.arange(nc, dtype=jnp.int32) * Q_CHUNK}
    if ksel > 0:
        kmean = jnp.mean(kb.astype(jnp.float32), axis=3)
        gate = jnp.einsum("bhtd,bhnd->bhtn", q.astype(jnp.float32), kmean)
        past = jnp.arange(nb, dtype=jnp.int32)[None, :] < qblk[:, None]
        gate = jnp.where(past, gate, MASK_VALUE)
        _, idx = lax.top_k(gate, ksel)
        valid = idx < qblk[:, None]
        xs["idx"] = chunks(idx)
        xs["valid"] = chunks(valid)
    bi = jnp.arange(B)[:, None, None, None]
    hi = jnp.arange(H)[None, :, None, None]
    offs = jnp.arange(MOBA_BLOCK, dtype=jnp.int32)

    def body(xc):
        qc = xc["q"]
        start = xc["start"]
        pos_q = start + jnp.arange(Q_CHUNK, dtype=jnp.int32)
        own = start // MOBA_BLOCK
        k_own = lax.dynamic_index_in_dim(kb, own, axis=2, keepdims=False)
        v_own = lax.dynamic_index_in_dim(vb, own, axis=2, keepdims=False)
        d_own = pos_q[:, None] - (own * MOBA_BLOCK + offs)[None, :]
        s_own = (jnp.einsum("bhtd,bhsd->bhts", qc, k_own).astype(jnp.float32) * scale
                 - slopes[:, None, None] * d_own.astype(jnp.float32))
        s_own = jnp.where(d_own >= 0, s_own, MASK_VALUE)
        if ksel == 0:
            p = jax.nn.softmax(s_own, axis=-1).astype(v.dtype)
            return jnp.einsum("bhts,bhsd->bhtd", p, v_own)
        idxc = xc["idx"]
        validc = xc["valid"]
        k_g = kb[bi, hi, idxc]
        v_g = vb[bi, hi, idxc]
        pos_sel = idxc[..., None] * MOBA_BLOCK + offs
        d_sel = pos_q[None, None, :, None, None] - pos_sel
        s_sel = (jnp.einsum("bhtd,bhtjsd->bhtjs", qc, k_g).astype(jnp.float32) * scale
                 - slopes[None, :, None, None, None] * d_sel.astype(jnp.float32))
        s_sel = jnp.where(validc[..., None], s_sel, MASK_VALUE)
        s_all = jnp.concatenate([s_sel.reshape(B, H, Q_CHUNK, ksel * MOBA_BLOCK), s_own], axis=-1)
        p = jax.nn.softmax(s_all, axis=-1).astype(v.dtype)
        p_sel = p[..., : ksel * MOBA_BLOCK].reshape(B, H, Q_CHUNK, ksel, MOBA_BLOCK)
        p_own = p[..., ksel * MOBA_BLOCK:]
        return (jnp.einsum("bhts,bhsd->bhtd", p_own, v_own)
                + jnp.einsum("bhtjs,bhtjsd->bhtd", p_sel, v_g))

    out = lax.map(body, xs)
    return out.transpose(1, 0, 3, 2, 4).reshape(B, S, H * hd)

def gated_short_conv(b_gate, c_gate, h, w_conv):
    z = c_gate * h
    y = lax.conv_general_dilated(z, w_conv[:, None, :], window_strides=(1,),
                                 padding=[(CONV_K - 1, 0)],
                                 dimension_numbers=("NWC", "WIO", "NWC"),
                                 feature_group_count=CONV_WIDTH)
    return b_gate * y

def peer(h, w_query, sub_keys, expert_u, expert_v):
    B, S, D = h.shape
    T = B * S
    hf = h.reshape(T, D)
    q = (hf @ w_query).reshape(T, PEER_HEADS, 2, PEER_HALF)
    scores = jnp.einsum("thpd,hpnd->thpn", q, sub_keys).astype(jnp.float32)
    top_v, top_i = lax.top_k(scores, PEER_TOPK)
    cand_v = top_v[:, :, 0, :, None] + top_v[:, :, 1, None, :]
    cand_i = top_i[:, :, 0, :, None] * PEER_NKEYS + top_i[:, :, 1, None, :]
    cand_v = cand_v.reshape(T, PEER_HEADS, PEER_TOPK * PEER_TOPK)
    cand_i = cand_i.reshape(T, PEER_HEADS, PEER_TOPK * PEER_TOPK)
    best_v, best_pos = lax.top_k(cand_v, PEER_TOPK)
    expert_idx = jnp.take_along_axis(cand_i, best_pos, axis=-1)
    gates = jax.nn.softmax(best_v, axis=-1).astype(h.dtype)
    nc = T // PEER_TOK_CHUNK
    xs = {"h": hf.reshape(nc, PEER_TOK_CHUNK, D),
          "idx": expert_idx.reshape(nc, PEER_TOK_CHUNK, PEER_HEADS, PEER_TOPK),
          "g": gates.reshape(nc, PEER_TOK_CHUNK, PEER_HEADS, PEER_TOPK)}

    def body(xc):
        u = jnp.take(expert_u, xc["idx"], axis=0)
        vv = jnp.take(expert_v, xc["idx"], axis=0)
        a = jax.nn.gelu(jnp.einsum("td,thkd->thk", xc["h"], u))
        return jnp.einsum("thk,thkd->td", xc["g"] * a, vv)

    return lax.map(body, xs).reshape(B, S, D)

def second_inputs(seed: int = 0) -> dict:
    key = jax.random.key(seed)
    ks = jax.random.split(key, 16)
    L, D = DEPTH, D_MODEL

    def nrm(k, shape, s):
        return jax.random.normal(k, shape, jnp.float32) * s

    return {
        "x": nrm(ks[0], (BATCH, SEQ, D), 1.0),
        "c": nrm(ks[1], (BATCH, D), 1.0),
        "norm1_g": 1.0 + nrm(ks[2], (L, D), 0.02),
        "norm2_g": 1.0 + nrm(ks[3], (L, D), 0.02),
        "w_ada": nrm(ks[4], (L, D, 6 * D), 0.5 * D ** -0.5),
        "b_ada": nrm(ks[5], (L, 6 * D), 0.02),
        "w_in": nrm(ks[6], (L, D, IN_COLS), D ** -0.5),
        "conv_w": nrm(ks[7], (L, CONV_K, CONV_WIDTH), CONV_K ** -0.5),
        "w_attn_proj": nrm(ks[8], (L, ATTN_WIDTH, D), ATTN_WIDTH ** -0.5),
        "w_conv_proj": nrm(ks[9], (L, CONV_WIDTH, D), CONV_WIDTH ** -0.5),
        "w_out": nrm(ks[10], (L, D, D), D ** -0.5),
        "w_query": nrm(ks[11], (L, D, PEER_HEADS * PEER_DKEY), D ** -0.5),
        "sub_keys": nrm(ks[12], (L, PEER_HEADS, 2, PEER_NKEYS, PEER_HALF), PEER_HALF ** -0.5),
        "expert_u": nrm(ks[13], (L, PEER_EXPERTS, D), D ** -0.5),
        "expert_v": nrm(ks[14], (L, PEER_EXPERTS, D), PEER_HEADS ** -0.5),
        "final_g": 1.0 + nrm(ks[15], (D,), 0.02),
    }

def second_block(x, c, norm1_g, norm2_g, w_ada, b_ada, w_in, conv_w, w_attn_proj, w_conv_proj,
              w_out, w_query, sub_keys, expert_u, expert_v, final_g):
    B, S, D = x.shape
    slopes = alibi_slopes(N_ATTN_HEADS)
    for l in range(DEPTH):
        ada = (c @ w_ada[l] + b_ada[l])[:, None, :]
        sh1, sc1, g1, sh2, sc2, g2 = jnp.split(ada, 6, axis=-1)
        h = rmsnorm_2(x, norm1_g[l]) * (1.0 + sc1) + sh1
        proj = h @ w_in[l]
        q, k, v, b_gate, c_gate, hc, gate_a, gate_c = jnp.split(proj, SPLIT_POINTS, axis=-1)
        ya = moba_attention(q.reshape(B, S, N_ATTN_HEADS, ATTN_HEAD_DIM),
                            k.reshape(B, S, N_ATTN_HEADS, ATTN_HEAD_DIM),
                            v.reshape(B, S, N_ATTN_HEADS, ATTN_HEAD_DIM), slopes)
        yc = gated_short_conv(b_gate, c_gate, hc, conv_w[l])
        merged = (jax.nn.sigmoid(gate_a) * (ya @ w_attn_proj[l])
                  + jax.nn.sigmoid(gate_c) * (yc @ w_conv_proj[l]))
        x = x + g1 * (merged @ w_out[l])
        h = rmsnorm_2(x, norm2_g[l]) * (1.0 + sc2) + sh2
        x = x + g2 * peer(h, w_query[l], sub_keys[l], expert_u[l], expert_v[l])
    return rmsnorm_2(x, final_g)


def setup_inputs(seed=0):
    out = dict(first_inputs(seed))
    for name, value in second_inputs(seed + 1).items():
        if name != "x":
            out[name + "_2"] = value
    return out


def reference(
    x, norm_mix, norm_mlp, attn_w_qkv, attn_q_norm, attn_k_norm, attn_w_o, gla_w_in,
    gla_w_gate_up, gla_b_gate, gla_out_norm, gla_w_o, mlp_w_in, mlp_w_out, final_norm, c_2,
    norm1_g_2, norm2_g_2, w_ada_2, b_ada_2, w_in_2, conv_w_2, w_attn_proj_2, w_conv_proj_2,
    w_out_2, w_query_2, sub_keys_2, expert_u_2, expert_v_2, final_g_2,
):
    x = first_block(
        x, norm_mix, norm_mlp, attn_w_qkv, attn_q_norm, attn_k_norm, attn_w_o, gla_w_in,
        gla_w_gate_up, gla_b_gate, gla_out_norm, gla_w_o, mlp_w_in, mlp_w_out, final_norm,
    )
    return second_block(
        x, c_2, norm1_g_2, norm2_g_2, w_ada_2, b_ada_2, w_in_2, conv_w_2, w_attn_proj_2,
        w_conv_proj_2, w_out_2, w_query_2, sub_keys_2, expert_u_2, expert_v_2, final_g_2,
    )


_drawn_inputs = setup_inputs


def setup_inputs(seed=0):
    import zlib

    import numpy as np

    out = dict(_drawn_inputs(seed))
    spreads = {}
    factors = {'attn_q_norm': 3.731, 'attn_k_norm': 3.43, 'norm2_g_2': 2.878, 'final_g_2': 2.91}
    for name, (base, spread) in spreads.items():
        noise = np.random.default_rng([zlib.crc32(name.encode()), seed]).standard_normal(out[name].shape)
        drawn = base * np.exp(spread * noise) if base else spread * noise
        out[name] = __import__('jax').numpy.asarray(drawn.astype(out[name].dtype))
    for name, factor in factors.items():
        out[name] = (out[name] * factor).astype(out[name].dtype)
    return out
```

```python
import math
from contextlib import ExitStack, contextmanager

import numpy as np

import concourse.bass as bass
from concourse import mybir

ALU = mybir.AluOpType
ACT = mybir.ActivationFunctionType
AX = mybir.AxisListType
F32 = mybir.dt.float32
U32 = mybir.dt.uint32

P = 128
D = 1024
S = 256
T = S // P
KC = D // P
HALF = 512
EPS = 1e-6
SLOTS = 4
PANEL = 4096

N_HEADS, N_KV, HD = 16, 4, 64
QK_HEADS = N_HEADS + N_KV
GLA_H, GLA_DK, GLA_DV, CHUNK, RANK = 4, 128, 256, 64, 16
N_CHUNKS = S // CHUNK
D_FF = 4 * D
LAYERS = 2
MH = 8
CONV_K = 3
ADA = 6 * D
PH, NKEYS, DKEY, TOPK = 8, 128, 128, 16
EXPERTS = NKEYS * NKEYS
STAGE_SEMS = 150
POOL_SEMS = 200
MASKED = -1e30
GONE = -3.0e38


class Chain:

    def __init__(self, eng, sem):
        self.eng, self.sem, self.n = eng, sem, 0

    def __call__(self, ins):
        self.n += 1
        ins.then_inc(self.sem, 1)
        self.eng.wait_ge(self.sem, self.n)
        return ins

    def clear(self):
        self.eng.sem_clear(self.sem)
        self.n = 0

    @contextmanager
    def turn(self):
        assert self.n == 0, "clear it ahead of the loop"
        yield
        self.clear()


class Stage:

    def __init__(self, nc, K, mem, name):
        K.stages += 1
        self.nc, self.K, self.mem, self.name, self.used = nc, K, mem, f"{name}{K.stages}", 0

    def sb(self, name, shape, dt=F32):
        return self.mem.enter_context(self.nc.sbuf_tensor(f"{self.name}_{name}", shape, dt))

    def ps(self, name, shape, dt=F32):
        return self.mem.enter_context(self.nc.psum_tensor(f"{self.name}_{name}", shape, dt))

    def sem(self, name):
        self.used += 1
        return self.mem.enter_context(self.nc.semaphore(f"{self.name}_{name}", num=STAGE_SEMS + self.used - 1))

    def pool_sem(self, name):
        self.K.pool_sems += 1
        return self.mem.enter_context(self.nc.semaphore(f"{self.name}_{name}",
                                                        num=POOL_SEMS + self.K.pool_sems - 1))


class Kept:
    pass


@contextmanager
def stage(nc, K, name):
    with ExitStack() as mem:
        st = Stage(nc, K, mem, name)
        yield st
        nc.all_engine_barrier(sems_to_clear=range(STAGE_SEMS, STAGE_SEMS + st.used))


def columns(w, n):
    return w[:, n * HALF:(n + 1) * HALF].rearrange("(k p) n -> p k n", p=P)


def in_ring(K, n, k=KC):
    return K.ring[:, n % SLOTS, :].rearrange("p (k n) -> p k n", k=k)


def clear_ring(nc, K):
    nc.all_engine_barrier(sems_to_clear=range(K.ring_in[0].num, K.ring_in[-1].num + 1))


def start_panels(dma, K, panels):
    for n, (src, k) in enumerate(panels):
        dma.dma_start(in_ring(K, n, k), src).then_inc(K.ring_in[n % SLOTS], 16)



def setup(nc, K, A, first_panels):
    with stage(nc, K, "setup") as st:
        wcol = st.sb("wcol", [40, P])
        gains = st.ps("gains", [P, HALF])
        loaded, zeroed, made, turned, gpsimd_own = map(
            st.sem, ("loaded", "zeroed", "made", "turned", "gpsimd_own"))
        with nc.Block(no_gpsimd_drain=True) as block:
            @block.sync
            def _(sp):
                sp.dma_start(K.x[:], A.x[0].rearrange("(t p) d -> p t d", p=P)).then_inc(loaded, 16)
                for n, g in enumerate((A.norm_mix, A.norm_mlp)):
                    sp.dma_start(wcol[16 * n:16 * n + 16, :],
                                 g.rearrange("l (k p) -> (l k) p", p=P)).then_inc(loaded, 16)
                sp.dma_start(wcol[32:40, :], A.c_2.rearrange("a (k p) -> (a k) p", p=P)).then_inc(loaded, 16)
                start_panels(sp, K, first_panels)
                sp.wait_ge(loaded, 16 * 4)

            @block.gpsimd
            def _(pool):
                own = Chain(pool, gpsimd_own)
                own(pool.memset(K.ident[:], 0.0))
                own(pool.memset(K.ones[:], 1.0))
                pool.affine_select(out=K.ident[:], in_=K.ident[:], compare_op=ALU.not_equal, fill=1.0,
                                   base=0, pattern=[[-1, P]], channel_multiplier=1).then_inc(made, 1)

            @block.tensor
            def _(pe):
                pe.wait_ge(loaded, 16 * 4)
                pe.wait_ge(made, 1)
                pe.transpose(gains[:, 0:40], wcol[:], K.ident[0:40, 0:40]).then_inc(turned, 1)

            @block.vector
            def _(dve):
                dve.memset(K.layer_base[:], 0.0).then_inc(zeroed, 1)
                dve.wait_ge(turned, 1)
                dve.tensor_copy(K.gain_cols[:], gains[:, 0:40]).then_inc(zeroed, 1)
                dve.wait_ge(zeroed, 2)



def norm(nc, K, gain_cols=None, gain=None, modulate=None, turn=True, out=None, keep=None, panels=()):
    with stage(nc, K, "norm") as st:
        xn = st.sb("xn", [P, T, D]) if keep is None else keep
        squares = st.sb("squares", [P, T, D])
        rows = st.sb("rows", [P, D]) if gain is not None else None
        ssq, ms, std, rstd = (st.sb(n, [P, T]) for n in ("ssq", "ms", "std", "rstd"))
        tp = st.ps("tp", [P, 2 * T, HALF])
        ssq_done, ms_done, std_done, xn_done, turned, moved, loaded, stored, dve_own = map(
            st.sem, ("ssq_done", "ms_done", "std_done", "xn_done", "turned", "moved", "loaded",
                     "stored", "dve_own"))
        with nc.Block(no_gpsimd_drain=True) as block:
            @block.sync
            def _(sp):
                if gain is not None:
                    sp.dma_start(rows[:], gain.partition_broadcast(P)).then_inc(loaded, 16)
                start_panels(sp, K, panels)
                if out is not None:
                    sp.wait_ge(xn_done, T)
                    sp.dma_start(out[0].rearrange("(t p) d -> p t d", p=P), xn[:]).then_inc(stored, 16)
                    sp.wait_ge(stored, 16)

            @block.scalar
            def _(act):
                for t in range(T):
                    act.activation(squares[:, t, :], K.x[:, t, :], ACT.Square,
                                   accum_out=ssq[:, t:t + 1]).then_inc(ssq_done, 1)
                act.wait_ge(ms_done, 1)
                act.activation(std[:], ms[:], ACT.Sqrt).then_inc(std_done, 1)
                if turn and gain_cols is None:
                    for n in range(2 * T):
                        t, h = n // 2, n % 2
                        act.wait_ge(turned, n + 1)
                        act.activation(K.hT[:, 4 * h:4 * h + 4, t * P:(t + 1) * P],
                                       tp[:, n, :].rearrange("p (k n) -> p k n", k=4),
                                       ACT.Copy).then_inc(moved, 1)

            @block.vector
            def _(dve):
                own = Chain(dve, dve_own)
                if gain is not None:
                    dve.wait_ge(loaded, 16)
                if modulate is not None:
                    own(dve.scalar_tensor_tensor(out=rows[:], in0=modulate[0], scalar=1.0, in1=rows[:],
                                                 op0=ALU.add, op1=ALU.mult))
                dve.wait_ge(ssq_done, T)
                dve.tensor_scalar(ms[:], ssq[:], 1.0 / D, EPS, ALU.mult, ALU.add).then_inc(ms_done, 1)
                dve.wait_ge(std_done, 1)
                own(dve.reciprocal(rstd[:], std[:]))
                for t in range(T):
                    if gain is None:
                        dve.tensor_scalar(xn[:, t, :], K.x[:, t, :], rstd[:, t:t + 1], None,
                                          ALU.mult).then_inc(xn_done, 1)
                    elif modulate is None:
                        dve.scalar_tensor_tensor(out=xn[:, t, :], in0=K.x[:, t, :],
                                                 scalar=rstd[:, t:t + 1], in1=rows[:],
                                                 op0=ALU.mult, op1=ALU.mult).then_inc(xn_done, 1)
                    else:
                        own(dve.scalar_tensor_tensor(out=xn[:, t, :], in0=K.x[:, t, :],
                                                     scalar=rstd[:, t:t + 1], in1=rows[:],
                                                     op0=ALU.mult, op1=ALU.mult))
                        dve.tensor_tensor(xn[:, t, :], xn[:, t, :], modulate[1],
                                          ALU.add).then_inc(xn_done, 1)
                if turn and gain_cols is not None:
                    for n in range(2 * T):
                        t, h = n // 2, n % 2
                        dve.wait_ge(turned, n + 1)
                        g = gain_cols[:, 4 * h:4 * h + 4].unsqueeze(2).to_broadcast([P, 4, P])
                        dve.tensor_tensor(K.hT[:, 4 * h:4 * h + 4, t * P:(t + 1) * P],
                                          tp[:, n, :].rearrange("p (k n) -> p k n", k=4), g,
                                          ALU.mult).then_inc(moved, 1)

            @block.tensor
            def _(pe):
                for n in range(2 * T if turn else 0):
                    t, h = n // 2, n % 2
                    pe.wait_ge(xn_done, t + 1)
                    for k in range(4):
                        f = (4 * h + k) * P
                        mm = pe.transpose(tp[:, n, k * P:(k + 1) * P], xn[:, t, f:f + P], K.ident[:])
                    mm.then_inc(turned, 1)



def project(nc, K, lhs, panels, evacuate, started=0):
    with stage(nc, K, "project") as st:
        ps = st.ps("ps", [P, 4, HALF])
        bank_full, bank_free = map(st.sem, ("bank_full", "bank_free"))
        with nc.Block(no_gpsimd_drain=True) as block:
            @block.sync
            def _(sp):
                for n in range(started, len(panels)):
                    if n >= SLOTS:
                        sp.wait_ge(bank_full, 2 * (n - SLOTS) + 2)
                    sp.dma_start(in_ring(K, n), panels[n][0]).then_inc(K.ring_in[n % SLOTS], 16)

            @block.tensor
            def _(pe):
                for n, (_, kind) in enumerate(panels):
                    w = in_ring(K, n)
                    pe.wait_ge(K.ring_in[n % SLOTS], 16 * (n // SLOTS + 1))
                    for b in range(2):
                        u = 2 * n + b
                        if u >= 4:
                            pe.wait_ge(bank_free, u - 3)
                        if kind == "tokens":
                            for k in range(KC):
                                mm = pe.matmul(ps[:, u % 4, :], lhs[:, k, b * P:(b + 1) * P], w[:, k, :],
                                               start=k == 0, stop=k == KC - 1)
                        else:
                            for m in range(2):
                                f = (2 * b + m) * P
                                for k in range(KC):
                                    mm = pe.matmul(ps[:, u % 4, m * S:(m + 1) * S], w[:, k, f:f + P],
                                                   lhs[:, k, :], start=k == 0, stop=k == KC - 1)
                        mm.then_inc(bank_full, 1)

            @block.scalar
            def _(act):
                for u in range(2 * len(panels)):
                    act.wait_ge(bank_full, u + 1)
                    evacuate(act, u // 2, u % 2, ps[:, u % 4, :]).then_inc(bank_free, 1)
    clear_ring(nc, K)



def rope(nc, K, qkv, qT, kT, A, panels):
    QK = QK_HEADS * HD
    with stage(nc, K, "rope") as st:
        gains = st.sb("gains", [P, 2, HD])
        table = st.sb("table", [P, T, 2, HD])
        squares = st.sb("squares", [P, T, QK])
        straight = st.sb("straight", [P, T, QK])
        crossed = st.sb("crossed", [P, T, QK])
        kk = st.sb("kk", [P, T, N_KV, 2, HD])
        ms, std, rstd = (st.sb(n, [P, T, QK_HEADS]) for n in ("ms", "std", "rstd"))
        tp = st.ps("tp", [P, 6, HALF])
        loaded, squared, ms_done, std_done, rotated, turned, moved, dve_own = map(
            st.sem, ("loaded", "squared", "ms_done", "std_done", "rotated", "turned", "moved", "dve_own"))
        with nc.Block(no_gpsimd_drain=True) as block:
            @block.sync
            def _(sp):
                sp.dma_start(gains[:, 0, :], A.attn_q_norm[0:1, :].partition_broadcast(P)).then_inc(loaded, 16)
                sp.dma_start(gains[:, 1, :], A.attn_k_norm[0:1, :].partition_broadcast(P)).then_inc(loaded, 16)
                sp.dma_start(table[:], A.rope_table.rearrange("(t p) a d -> p t a d", p=P)).then_inc(loaded, 16)
                start_panels(sp, K, panels)

            @block.scalar
            def _(act):
                for t in range(T):
                    act.activation(squares[:, t, :], qkv[:, t, 0:QK], ACT.Square).then_inc(squared, 1)
                for t in range(T):
                    act.wait_ge(ms_done, t + 1)
                    act.activation(std[:, t, :], ms[:, t, :], ACT.Sqrt).then_inc(std_done, 1)
                for n in range(6):
                    act.wait_ge(turned, n + 1)
                    t, b = n // 3, n % 3
                    to = qT[:, 4 * b:4 * b + 4, :] if b < 2 else kT[:, 0:4, :]
                    act.activation(to[:, :, t * P:(t + 1) * P],
                                   tp[:, n, :].rearrange("p (k n) -> p k n", k=4),
                                   ACT.Copy).then_inc(moved, 1)

            @block.vector
            def _(dve):
                own = Chain(dve, dve_own)
                for t in range(T):
                    dve.wait_ge(squared, t + 1)
                    own(dve.tensor_reduce(ms[:, t, :], squares[:, t, :].rearrange("p (h d) -> p h d", d=HD),
                                          AX.X, ALU.add))
                    dve.tensor_scalar(ms[:, t, :], ms[:, t, :], 1.0 / HD, EPS, ALU.mult,
                                      ALU.add).then_inc(ms_done, 1)
                dve.wait_ge(loaded, 16 * 3)
                for t in range(T):
                    dve.wait_ge(std_done, t + 1)
                    own(dve.reciprocal(rstd[:, t, :], std[:, t, :]))
                    x = qkv[:, t, 0:QK].rearrange("p (h d) -> p h d", d=HD)
                    own(dve.tensor_tensor(x, x, rstd[:, t, :].unsqueeze(2).to_broadcast([P, QK_HEADS, HD]),
                                          ALU.mult))
                    for a, heads in ((0, slice(0, N_HEADS)), (1, slice(N_HEADS, QK_HEADS))):
                        n = heads.stop - heads.start
                        own(dve.tensor_tensor(x[:, heads, :], x[:, heads, :],
                                              gains[:, a:a + 1, :].to_broadcast([P, n, HD]), ALU.mult))
                    s = straight[:, t, :].rearrange("p (h d) -> p h d", d=HD)
                    c = crossed[:, t, :].rearrange("p (h r e d) -> p h r e d", r=2, e=2, d=HD // 4)
                    x4 = qkv[:, t, 0:QK].rearrange("p (h r e d) -> p h r e d", r=2, e=2, d=HD // 4)
                    sin = table[:, t, 1, :].rearrange("p (r e d) -> p r e d", r=2, e=2)
                    own(dve.tensor_tensor(s, x, table[:, t, 0:1, :].to_broadcast([P, QK_HEADS, HD]), ALU.mult))
                    for e in range(2):
                        own(dve.tensor_tensor(
                            c[:, :, :, e, :], x4[:, :, :, 1 - e, :],
                            sin[:, :, e, :].unsqueeze(1).to_broadcast([P, QK_HEADS, 2, HD // 4]), ALU.mult))
                    q = slice(0, N_HEADS * HD)
                    k = slice(N_HEADS * HD, QK)
                    own(dve.tensor_tensor(straight[:, t, q], straight[:, t, q], crossed[:, t, q], ALU.add))
                    for copy in range(2):
                        own(dve.tensor_tensor(
                            kk[:, t, :, copy, :], straight[:, t, k].rearrange("p (h d) -> p h d", d=HD),
                            crossed[:, t, k].rearrange("p (h d) -> p h d", d=HD), ALU.add))
                    dve.sem_inc(rotated, 1)

            @block.tensor
            def _(pe):
                for n in range(6):
                    t, b = n // 3, n % 3
                    pe.wait_ge(rotated, t + 1)
                    for k in range(4):
                        if b < 2:
                            a = straight[:, t, (4 * b + k) * P:(4 * b + k + 1) * P]
                        else:
                            a = kk[:, t, k, :, :].rearrange("p c d -> p (c d)")
                        mm = pe.transpose(tp[:, n, k * P:(k + 1) * P], a, K.ident[:])
                    mm.then_inc(turned, 1)


def attend(nc, K, heads, scale, q_of, k_of, v_of, oT, far=None, side_of=None, panels=()):
    with stage(nc, K, "attend") as st:
        scores = st.ps("scores", [P, 2, T, S])
        turn = st.ps("turn", [P, 2, T, S])
        o = st.ps("o", [P, 2, HALF])
        biased = st.sb("biased", [P, 2, T, S]) if far is not None else None
        probs = st.sb("probs", [P, 2, T, S])
        probsT = st.sb("probsT", [P, 2, T, S])
        top, shift, total, inverse = (st.sb(n, [P, 2 * heads]) for n in ("top", "shift", "total", "inverse"))
        scored, bias_done, shift_done, exp_done, normed, turned, moved, pv_done, o_moved, dve_own = map(
            st.sem, ("scored", "bias_done", "shift_done", "exp_done", "normed", "turned", "moved",
                     "pv_done", "o_moved", "dve_own"))
        side = side_of(st) if side_of else None
        with nc.Block(no_gpsimd_drain=True) as block:
            @block.sync
            def _(sp):
                if side:
                    side.sync(sp)
                start_panels(sp, K, panels)

            @block.gpsimd
            def _(pool):
                if side:
                    side.gpsimd(pool)

            @block.tensor
            def _(pe):
                if side:
                    side.tensor(pe)

                def score(h):
                    if h >= 2:
                        pe.wait_ge(bias_done if far is not None else exp_done,
                                   h - 1 if far is not None else T * (h - 1))
                    for t in range(T):
                        mm = pe.matmul(scores[:, h % 2, t, :], q_of(h)[:, t * P:(t + 1) * P], k_of(h),
                                       start=True, stop=True)
                    mm.then_inc(scored, 1)

                def transposes(h):
                    pe.wait_ge(normed, h + 1)
                    if h >= 2:
                        pe.wait_ge(moved, h - 1)
                    for t in range(T):
                        for k in range(T):
                            mm = pe.transpose(turn[:, h % 2, k, t * P:(t + 1) * P],
                                              probs[:, h % 2, t, k * P:(k + 1) * P], K.ident[:])
                    mm.then_inc(turned, 1)

                def weigh(h):
                    pe.wait_ge(moved, h + 1)
                    if h >= 4 and h % 2 == 0:
                        pe.wait_ge(o_moved, h // 2 - 1)
                    r = h % 2 * HD
                    for k in range(T):
                        mm = pe.matmul(o[r:r + HD, h // 2 % 2, 0:S], v_of(h, k), probsT[:, h % 2, k, :],
                                       start=k == 0, stop=k == T - 1)
                    mm.then_inc(pv_done, 1)

                for h in range(heads + 2):
                    if h < heads:
                        score(h)
                    if 1 <= h <= heads:
                        transposes(h - 1)
                    if h >= 2:
                        weigh(h - 2)

            @block.scalar
            def _(act):
                if side:
                    side.scalar(act)
                source = scores if far is None else biased
                for h in range(heads + 1):
                    if h < heads:
                        act.wait_ge(shift_done, h + 1)
                        if h >= 2:
                            act.wait_ge(turned, h - 1)
                        for t in range(T):
                            c = T * h + t
                            act.activation(probs[:, h % 2, t, :], source[:, h % 2, t, :], ACT.Exp,
                                           bias=shift[:, c:c + 1], scale=scale,
                                           accum_out=total[:, c:c + 1]).then_inc(exp_done, 1)
                    if h >= 1:
                        act.wait_ge(turned, h)
                        if h >= 3:
                            act.wait_ge(pv_done, h - 2)
                        act.activation(probsT[:, (h - 1) % 2, :, :], turn[:, (h - 1) % 2, :, :],
                                       ACT.Copy).then_inc(moved, 1)

            @block.vector
            def _(dve):
                own = Chain(dve, dve_own)

                def maximum(h):
                    dve.wait_ge(scored, h + 1)
                    a = scores[:, h % 2, :, :]
                    if far is not None:
                        if h >= 2:
                            dve.wait_ge(exp_done, T * (h - 1))
                        slope = 2.0 ** (-8.0 * (h + 1) / heads)
                        a = biased[:, h % 2, :, :]
                        dve.scalar_tensor_tensor(out=a, in0=far[:], scalar=slope / scale,
                                                 in1=scores[:, h % 2, :, :], op0=ALU.mult,
                                                 op1=ALU.add).then_inc(bias_done, 1)
                        dve.wait_ge(bias_done, h + 1)
                    c = slice(T * h, T * h + T)
                    own(dve.tensor_reduce(top[:, c], a, AX.X, ALU.max))
                    dve.tensor_scalar(shift[:, c], top[:, c], -scale, None, ALU.mult).then_inc(shift_done, 1)

                def normalise(h):
                    dve.wait_ge(exp_done, T * (h + 1))
                    c = slice(T * h, T * h + T)
                    own(dve.reciprocal(inverse[:, c], total[:, c]))
                    a = probs[:, h % 2, :, :]
                    dve.tensor_tensor(a, a, inverse[:, c].unsqueeze(2).to_broadcast([P, T, S]),
                                      ALU.mult).then_inc(normed, 1)

                def take(pair):
                    dve.wait_ge(pv_done, 2 * pair + 2)
                    dve.tensor_copy(oT[:, pair, :], o[:, pair % 2, 0:S]).then_inc(o_moved, 1)

                for h in range(heads + 3):
                    if h < heads:
                        maximum(h)
                    if 1 <= h <= heads:
                        normalise(h - 1)
                    if h >= 4 and h % 2 == 0:
                        take(h // 2 - 2)



def mlp(nc, K, w_in, w_out, started=0, conditions=None):
    PAIRS = D_FF // HALF
    TURNS = PAIRS // 2
    CH = 8
    with stage(nc, K, "mlp") as st:
        acc = st.ps("acc", [P, T, 2, HALF])
        hid = st.ps("hid", [P, 2, HALF])
        relu = st.sb("relu", [P, 2, S])
        act2 = st.sb("act2", [P, 2, S])
        hid_full, relu_done, act_full, act_used, dve_own = map(
            st.sem, ("hid_full", "relu_done", "act_full", "act_used", "dve_own"))
        if conditions is not None:
            csum, ccols, w_ada, b_ada = conditions
            PANELS = ADA // HALF
            ada_in = [st.pool_sem(f"ada_in{n}") for n in range(2)]
            biased = st.pool_sem("biased")
            ada_used, cleared = map(st.sem, ("ada_used", "cleared"))
            ada_panel = st.sb("ada_panel", [P, 2, KC, HALF])

        def src_in(n):
            return w_in.rearrange("(k p) n -> p k n", p=P)[:, :, bass.ds(n * HALF, HALF)]

        def src_out(n):
            return w_out[bass.ds(n * HALF, HALF), :].rearrange("(k p) n -> p k n", p=P)

        with nc.Block(no_gpsimd_drain=True) as block:
            @block.sync
            def _(sp):
                for n in range(started, 2):
                    sp.dma_start(in_ring(K, n), src_in(n)).then_inc(K.ring_in[n], 16)
                    sp.dma_start(in_ring(K, 2 + n, 4), src_out(n)).then_inc(K.ring_in[2 + n], 16)
                with sp.Fori(0, TURNS - 1) as i:
                    for g in range(2):
                        sp.wait_ge(hid_full, i * CH + 4 * (g + 1))
                        sp.dma_start(in_ring(K, g), src_in(2 * i + 2 + g)).then_inc(K.ring_in[g], 16)
                        sp.wait_ge(act_used, i * CH + 4 * (g + 1))
                        sp.dma_start(in_ring(K, 2 + g, 4), src_out(2 * i + 2 + g)).then_inc(K.ring_in[2 + g], 16)

            @block.gpsimd
            def _(pool):
                if conditions is None:
                    return

                def load(layer, n, slot):
                    src = w_ada[layer].rearrange("(k p) n -> p k n", p=P)[:, :, bass.ds(n * HALF, HALF)]
                    pool.dma_start(ada_panel[:, slot, :, :], src).then_inc(ada_in[slot], 16)

                pool.wait_ge(cleared, 1)
                pool.dma_start(csum[0:1, :], b_ada.rearrange("l (a n) -> a (l n)", a=1)).then_inc(biased, 16)
                for slot in range(2):
                    load(0, slot, slot)
                for layer in range(LAYERS):
                    with pool.Fori(0 if layer else 1, PANELS // 2) as j:
                        for slot in range(2):
                            pool.wait_ge(ada_used, 2 * j + (PANELS * layer + slot - 1))
                            load(layer, 2 * j + slot, slot)

            @block.tensor
            def _(pe):
                for t in range(T):
                    for b in range(2):
                        pe.matmul(acc[:, t, b, :], K.ident[:], K.x[:, t, b * HALF:(b + 1) * HALF],
                                  start=True, stop=False, skip_group_check=True)

                with pe.Fori(0, TURNS) as i:
                    def first(c):
                        g, m = c // 4, c % 4
                        if m == 0:
                            pe.wait_ge(K.ring_in[g], 16 * i + 16)
                        if c >= 2:
                            pe.wait_ge(relu_done, i * CH + c - 1)
                        w = in_ring(K, g)
                        for k in range(KC):
                            mm = pe.matmul(hid[:, c % 2, 0:S], w[:, k, m * P:(m + 1) * P], K.hT[:, k, :],
                                           start=k == 0, stop=k == KC - 1)
                        mm.then_inc(hid_full, 1)

                    def second(c):
                        g, m = c // 4, c % 4
                        if m == 0:
                            pe.wait_ge(K.ring_in[2 + g], 16 * i + 16)
                        pe.wait_ge(act_full, i * CH + c + 1)
                        w = in_ring(K, 2 + g, 4)
                        for t in range(T):
                            for b in range(2):
                                mm = pe.matmul(acc[:, t, b, :], act2[:, c % 2, t * P:(t + 1) * P],
                                               w[:, m, b * HALF:(b + 1) * HALF], start=False, stop=False,
                                               skip_group_check=True)
                        mm.then_inc(act_used, 1)

                    for c in range(CH):
                        first(c)
                        if c >= 1:
                            second(c - 1)
                    second(CH - 1)

            @block.scalar
            def _(act):
                with act.Fori(0, TURNS) as i:
                    for c in range(CH):
                        act.wait_ge(hid_full, i * CH + c + 1)
                        act.activation(relu[:, c % 2, :], hid[:, c % 2, 0:S], ACT.Relu).then_inc(relu_done, 1)
                        act.wait_ge(relu_done, i * CH + c + 1)
                        if c >= 2:
                            act.wait_ge(act_used, i * CH + c - 1)
                        act.activation(act2[:, c % 2, :], relu[:, c % 2, :], ACT.Square).then_inc(act_full, 1)

            @block.vector
            def _(dve):
                own = Chain(dve, dve_own)
                if conditions is not None:
                    dve.memset(csum[:], 0.0).then_inc(cleared, 1)
                    dve.wait_ge(biased, 16)
                    with dve.Fori(0, LAYERS * PANELS // 2) as j:
                        with own.turn():
                            for slot in range(2):
                                to = csum[:, bass.ds((2 * j + slot) * HALF, HALF)]
                                dve.wait_ge(ada_in[slot], 16 * j + 16)
                                for k in range(KC):
                                    ins = dve.scalar_tensor_tensor(
                                        out=to, in0=ada_panel[:, slot, k, :], scalar=ccols[:, k:k + 1],
                                        in1=to, op0=ALU.mult, op1=ALU.add)
                                    if k < KC - 1:
                                        own(ins)
                                ins.then_inc(ada_used, 1)
                dve.wait_ge(act_used, CH * TURNS)
                for t in range(T):
                    own(dve.tensor_copy(K.x[:, t, :], acc[:, t, :, :].rearrange("p b n -> p (b n)")))
    clear_ring(nc, K)


def spread(nc, K, csum):
    n_banks = LAYERS * ADA // HALF
    with stage(nc, K, "spread") as st:
        ps = st.ps("ps", [P, 4, HALF])
        summed, moved = map(st.sem, ("summed", "moved"))
        with nc.Block(no_gpsimd_drain=True) as block:
            @block.tensor
            def _(pe):
                for n in range(n_banks):
                    if n >= 4:
                        pe.wait_ge(moved, n - 3)
                    pe.matmul(ps[:, n % 4, :], K.ones[:], csum[:, n * HALF:(n + 1) * HALF],
                              start=True, stop=True).then_inc(summed, 1)

            @block.scalar
            def _(act):
                for n in range(n_banks):
                    act.wait_ge(summed, n + 1)
                    act.activation(csum[:, n * HALF:(n + 1) * HALF], ps[:, n % 4, :],
                                   ACT.Copy).then_inc(moved, 1)



def gla_gates(nc, K, A, logg, panels):
    with stage(nc, K, "gla_gates") as st:
        wz = st.sb("wz", [P, KC, 2 * RANK])
        up = st.sb("up", [2 * RANK + 1, 2, HALF])
        zT = st.sb("zT", [2 * RANK + 1, S])
        size, e, ln = (st.sb(n, [P, 4, HALF]) for n in ("size", "e", "ln"))
        zps = st.ps("zps", [P, HALF])
        logit = st.ps("logit", [P, 4, HALF])
        loaded, cleared, up_loaded, z_done, z_moved, logit_done, act_own, ln_done, logg_done, dve_own = map(
            st.sem, ("loaded", "cleared", "up_loaded", "z_done", "z_moved", "logit_done", "act_own",
                     "ln_done", "logg_done", "dve_own"))
        z0 = 2 * GLA_H * GLA_DK + 2 * GLA_H * GLA_DV
        with nc.Block(no_gpsimd_drain=True) as block:
            @block.sync
            def _(sp):
                sp.dma_start(wz[:], A.gla_w_in[0][:, z0:z0 + 2 * RANK].rearrange("(k p) n -> p k n", p=P)
                             ).then_inc(loaded, 16)
                sp.wait_ge(cleared, 1)
                for r in range(2):
                    sp.dma_start(up[RANK * r:RANK * (r + 1), r, :], A.gla_w_gate_up[0][r]).then_inc(up_loaded, 16)
                sp.dma_start(up[2 * RANK:2 * RANK + 1, :, :], A.gla_b_gate).then_inc(up_loaded, 16)
                start_panels(sp, K, panels)

            @block.tensor
            def _(pe):
                pe.wait_ge(loaded, 16)
                for k in range(KC):
                    mm = pe.matmul(zps[0:2 * RANK, 0:S], wz[:, k, :], K.hT[:, k, :], start=k == 0,
                                   stop=k == KC - 1)
                mm.then_inc(z_done, 1)
                pe.wait_ge(up_loaded, 16 * 3)
                pe.wait_ge(z_moved, 2)
                for n in range(4):
                    t, r = n // 2, n % 2
                    pe.matmul(logit[:, n, :], zT[:, t * P:(t + 1) * P], up[:, r, :], start=True,
                              stop=True).then_inc(logit_done, 1)

            @block.vector
            def _(dve):
                own = Chain(dve, dve_own)
                dve.memset(up[:], 0.0).then_inc(cleared, 1)
                dve.memset(zT[2 * RANK:2 * RANK + 1, :], 1.0).then_inc(z_moved, 1)
                dve.wait_ge(z_done, 1)
                dve.tensor_copy(zT[0:2 * RANK, :], zps[0:2 * RANK, 0:S]).then_inc(z_moved, 1)
                for n in range(4):
                    dve.wait_ge(ln_done, n + 1)
                    own(dve.scalar_tensor_tensor(out=logg[:, n // 2, n % 2, :], in0=logit[:, n, :], scalar=0.0,
                                                 in1=ln[:, n, :], op0=ALU.min, op1=ALU.subtract))

            @block.scalar
            def _(act):
                own = Chain(act, act_own)
                for n in range(4):
                    act.wait_ge(logit_done, n + 1)
                    own(act.activation(size[:, n, :], logit[:, n, :], ACT.Abs))
                for n in range(4):
                    own(act.activation(e[:, n, :], size[:, n, :], ACT.Exp, scale=-1.0))
                for n in range(4):
                    act.activation(ln[:, n, :], e[:, n, :], ACT.Ln, bias=1.0).then_inc(ln_done, 1)


def gla_scan(nc, K, q, k, v, logg, o):
    with stage(nc, K, "gla_scan") as st:
        tri = st.sb("tri", [P, 4, P])
        which = st.sb("which", [P, 2])
        eb, enb = (K.ring[:, 2, a:a + 2 * HALF].rearrange("p (s n) -> p s n", s=2) for a in (0, 2 * HALF))
        ed = st.sb("ed", [P, 2, HALF])
        qe, ke = (st.sb(n, [P, 2, HALF]) for n in ("qe", "ke"))
        kd = K.ring[:, 2, 4 * HALF:8 * HALF].rearrange("p (r t n) -> p r t n", r=2, t=T)
        qeT, keT = (st.sb(n, [P, 2, GLA_H, S]) for n in ("qeT", "keT"))
        decay = st.sb("decay", [P, 2, GLA_H, N_CHUNKS])
        aT = st.sb("aT", [P, 2, 2 * T, P])
        state = K.ring[:, 3, 0:12 * GLA_DV].rearrange("p (s r i n) -> p s r i n", s=2, r=2, i=3)
        wide = st.ps("wide", [P, 8, HALF])
        sums, turn = wide[:, 0:4, :], wide[:, 4:8, :]
        made, decayed, summed, exped, gated, turned, moved, pool_own, dve_own = map(
            st.sem, ("made", "decayed", "summed", "exped", "gated", "turned", "moved", "pool_own", "dve_own"))
        inner, masked, outer, stated, o_done, o_moved, kd_done = map(
            st.sem, ("inner", "masked", "outer", "stated", "o_done", "o_moved", "kd_done"))
        steps = [(r, t) for r in range(2) for t in range(T)]
        order = ((0, 1, 2), (3, 2, 1))
        place = {(0, 0): (2, 0), (0, 2): (2, S), (1, 1): (3, 0), (0, 1): (4, 0), (1, 0): (4, S), (1, 2): (7, 0)}

        def update(r, i):
            bank, column = place[r, i]
            return wide[:, bank, column:column + S]

        with nc.Block(no_gpsimd_drain=True) as block:
            @block.gpsimd
            def _(pool):
                own = Chain(pool, pool_own)
                own(pool.memset(tri[:], 1.0 / 16.0))
                own(pool.memset(which[:], 1.0 / 16.0))

                def keep(a, where, base, mult, step, op):
                    own(pool.affine_select(out=a, in_=a, compare_op=op, fill=0.0, base=base,
                                           pattern=[[step, where]], channel_multiplier=mult))

                keep(tri[:, 0, :], P, 0, -1, 1, ALU.is_ge)
                keep(tri[:, 1, :], P, 0, 1, -1, ALU.is_gt)
                keep(tri[:, 2, :], P, 0, 1, -1, ALU.is_ge)
                keep(tri[:, 3, :], P, 0, -1, 1, ALU.is_gt)
                for m in range(4):
                    own(pool.affine_select(out=tri[:, m, CHUNK:P], in_=tri[:, m, CHUNK:P],
                                           compare_op=ALU.is_ge, fill=0.0, base=-CHUNK,
                                           pattern=[[0, CHUNK]], channel_multiplier=1))
                    own(pool.affine_select(out=tri[:, m, 0:CHUNK], in_=tri[:, m, 0:CHUNK],
                                           compare_op=ALU.is_gt, fill=0.0, base=CHUNK,
                                           pattern=[[0, CHUNK]], channel_multiplier=-1))
                own(pool.affine_select(out=which[:, 1:2], in_=which[:, 1:2], compare_op=ALU.is_ge, fill=0.0,
                                       base=-CHUNK, pattern=[[0, 1]], channel_multiplier=1))
                own(pool.affine_select(out=which[:, 0:1], in_=which[:, 0:1], compare_op=ALU.is_gt, fill=0.0,
                                       base=CHUNK, pattern=[[0, 1]], channel_multiplier=-1))
                pool.memset(aT[:], 0.0).then_inc(made, 1)

            @block.tensor
            def _(pe):
                pe.wait_ge(made, 1)
                for r in range(2):
                    for h in range(GLA_H):
                        for t in range(T):
                            c = (r * GLA_H + h) * N_CHUNKS + 2 * t
                            mm = pe.matmul(turn[:, 3, c:c + 2], logg[:, t, r, h * P:(h + 1) * P], which[:],
                                           start=True, stop=True)
                mm.then_inc(decayed, 1)

                def sum_up(n):
                    r, t = steps[n]
                    if n >= 2:
                        pe.wait_ge(exped, 3 * (n - 1))
                    for m in range(2):
                        mm = pe.matmul(sums[:, n % 2 * 2 + m, :], tri[:, 2 * r + m, :], logg[:, t, r, :],
                                       start=True, stop=True)
                    mm.then_inc(summed, 1)

                def transposes(n):
                    pe.wait_ge(gated, 2 * n + 2)
                    for m, a in enumerate((qe, ke)):
                        u = 2 * n + m
                        if u >= 3:
                            pe.wait_ge(moved, u - 2)
                        for h in range(GLA_H):
                            mm = pe.transpose(turn[:, u % 3, h * P:(h + 1) * P],
                                              a[:, n % 2, h * P:(h + 1) * P], K.ident[:])
                        mm.then_inc(turned, 1)

                sum_up(0)
                for n in range(4):
                    if n + 1 < 4:
                        sum_up(n + 1)
                    transposes(n)

                def within(h):
                    if h >= 2:
                        pe.wait_ge(masked, h - 1)
                    for n, (r, t) in enumerate(steps):
                        mm = pe.matmul(wide[:, h % 2, n * P:(n + 1) * P], keT[:, r, h, t * P:(t + 1) * P],
                                       qeT[:, r, h, t * P:(t + 1) * P], start=True, stop=True)
                    mm.then_inc(inner, 1)

                def between(h):
                    if h >= 1:
                        pe.wait_ge(stated, 6 * h)
                    for r in range(2):
                        for i, n in enumerate(order[r]):
                            a = n % 2 * CHUNK
                            mm = pe.matmul(update(r, i),
                                           kd[a:a + CHUNK, r, n // 2, h * P:(h + 1) * P],
                                           v[a:a + CHUNK, n // 2, h * S:(h + 1) * S], start=True, stop=True)
                    mm.then_inc(outer, 1)

                def output(h):
                    pe.wait_ge(masked, h + 1)
                    pe.wait_ge(stated, 6 * (h + 1))
                    if h >= 2:
                        pe.wait_ge(o_moved, h - 1)
                    for t in range(T):
                        to = wide[:, 5 + h % 2, t * S:(t + 1) * S]
                        for r in range(2):
                            pe.matmul(to, aT[:, h % 2, 2 * r + t, :], v[:, t, h * S:(h + 1) * S],
                                      start=r == 0, stop=False, skip_group_check=True)
                        for c in range(2):
                            n = 2 * t + c
                            for r in range(2):
                                if n == (0, N_CHUNKS - 1)[r]:
                                    continue
                                i = n - 1 if r == 0 else N_CHUNKS - 2 - n
                                mm = pe.matmul(wide[c * CHUNK:(c + 1) * CHUNK, 5 + h % 2, t * S:(t + 1) * S],
                                               qeT[:, r, h, n * CHUNK:(n + 1) * CHUNK],
                                               state[:, h % 2, r, i, :], start=False, stop=True,
                                               skip_group_check=True)
                    mm.then_inc(o_done, 1)

                pe.wait_ge(moved, 8)
                pe.wait_ge(exped, 13)
                pe.wait_ge(kd_done, 4)
                for h in range(GLA_H + 1):
                    if h < GLA_H:
                        within(h)
                        between(h)
                    if h >= 1:
                        output(h - 1)

            @block.scalar
            def _(act):
                act.wait_ge(decayed, 1)
                act.activation(decay[:].rearrange("p r h n -> p (r h n)"), turn[:, 3, 0:2 * GLA_H * N_CHUNKS],
                               ACT.Exp).then_inc(exped, 1)
                for n, (r, t) in enumerate(steps):
                    act.wait_ge(summed, n + 1)
                    if n >= 2:
                        act.wait_ge(gated, 2 * (n - 1))
                        act.wait_ge(kd_done, n - 1)
                    s = n % 2
                    act.activation(eb[:, s, :], sums[:, 2 * s, :], ACT.Exp).then_inc(exped, 1)
                    act.activation(enb[:, s, :], sums[:, 2 * s, :], ACT.Exp, scale=-1.0).then_inc(exped, 1)
                    act.activation(ed[:, s, :], sums[:, 2 * s + 1, :], ACT.Exp).then_inc(exped, 1)
                    for m, to in enumerate((qeT, keT)):
                        u = 2 * n + m
                        act.wait_ge(turned, u + 1)
                        act.activation(to[:, r, :, t * P:(t + 1) * P],
                                       turn[:, u % 3, :].rearrange("p (h n) -> p h n", h=GLA_H),
                                       ACT.Copy).then_inc(moved, 1)
                for h in range(GLA_H):
                    act.wait_ge(o_done, h + 1)
                    act.activation(o[:, :, h, :], wide[:, 5 + h % 2, :].rearrange("p (t n) -> p t n", t=T),
                                   ACT.Copy).then_inc(o_moved, 1)

            @block.vector
            def _(dve):
                own = Chain(dve, dve_own)
                for n, (r, t) in enumerate(steps):
                    dve.wait_ge(exped, 1 + 3 * (n + 1))
                    if n >= 2:
                        dve.wait_ge(turned, 2 * (n - 1))
                    s = n % 2
                    dve.tensor_tensor(qe[:, s, :], q[:, t, :], eb[:, s, :], ALU.mult).then_inc(gated, 1)
                    dve.tensor_tensor(ke[:, s, :], k[:, t, :], enb[:, s, :], ALU.mult).then_inc(gated, 1)
                    dve.tensor_tensor(kd[:, r, t, :], k[:, t, :], ed[:, s, :], ALU.mult).then_inc(kd_done, 1)
                dve.wait_ge(made, 1)
                for h in range(GLA_H):
                    dve.wait_ge(inner, h + 1)
                    if h >= 2:
                        dve.wait_ge(o_done, h - 1)
                    for r in range(2):
                        mask = tri[:, 2 * r:2 * r + 1, :].bitcast(U32).to_broadcast([P, T, P])
                        ins = dve.copy_predicated(
                            aT[:, h % 2, 2 * r:2 * r + 2, :], mask,
                            wide[:, h % 2, 2 * r * P:2 * (r + 1) * P].rearrange("p (t n) -> p t n", t=T))
                        if r == 0:
                            own(ins)
                    ins.then_inc(masked, 1)
                    dve.wait_ge(outer, h + 1)
                    for r in range(2):
                        for i, n in enumerate(order[r]):
                            u = 3 * r + i
                            chunk = update(r, i)
                            to = state[:, h % 2, r, i, :]
                            if i == 0:
                                dve.tensor_copy(to, chunk).then_inc(stated, 1)
                            else:
                                dve.wait_ge(stated, 6 * h + u)
                                dve.scalar_tensor_tensor(out=to, in0=state[:, h % 2, r, i - 1, :],
                                                         scalar=decay[:, r, h, n:n + 1], in1=chunk,
                                                         op0=ALU.mult, op1=ALU.add).then_inc(stated, 1)


def gla_out(nc, K, A, o, gate, oT, panels):
    with stage(nc, K, "gla_out") as st:
        gain = st.sb("gain", [P, GLA_DV])
        squares = st.sb("squares", [P, T, D])
        ms, std, rstd = (st.sb(n, [P, T * GLA_H]) for n in ("ms", "std", "rstd"))
        tp = st.ps("tp", [P, 2 * T, HALF])
        loaded, squared, ms_done, std_done, gated, turned, moved, dve_own = map(
            st.sem, ("loaded", "squared", "ms_done", "std_done", "gated", "turned", "moved", "dve_own"))
        with nc.Block(no_gpsimd_drain=True) as block:
            @block.sync
            def _(sp):
                sp.dma_start(gain[:], A.gla_out_norm[0:1, :].partition_broadcast(P)).then_inc(loaded, 16)
                start_panels(sp, K, panels)

            @block.scalar
            def _(act):
                act.activation(squares[:].rearrange("p t (h d) -> p t h d", h=GLA_H), o[:],
                               ACT.Square).then_inc(squared, 1)
                act.wait_ge(ms_done, 1)
                act.activation(std[:], ms[:], ACT.Sqrt).then_inc(std_done, 1)
                for n in range(2 * T):
                    t, h = n // 2, n % 2
                    act.wait_ge(turned, n + 1)
                    act.activation(oT[:, 4 * h:4 * h + 4, t * P:(t + 1) * P],
                                   tp[:, n, :].rearrange("p (k n) -> p k n", k=4), ACT.Copy).then_inc(moved, 1)

            @block.vector
            def _(dve):
                own = Chain(dve, dve_own)
                dve.wait_ge(squared, 1)
                own(dve.tensor_reduce(ms[:], squares[:].rearrange("p t (h d) -> p (t h) d", h=GLA_H), AX.X,
                                      ALU.add))
                dve.tensor_scalar(ms[:], ms[:], 1.0 / GLA_DV, EPS, ALU.mult, ALU.add).then_inc(ms_done, 1)
                dve.wait_ge(loaded, 16)
                g = gate.rearrange("p t (h d) -> p t h d", h=GLA_H)
                for t in range(T):
                    own(dve.tensor_tensor(g[:, t], g[:, t], gain[:].unsqueeze(1).to_broadcast([P, GLA_H, GLA_DV]),
                                          ALU.mult))
                dve.wait_ge(std_done, 1)
                own(dve.reciprocal(rstd[:], std[:]))
                for t in range(T):
                    r = rstd[:, t * GLA_H:(t + 1) * GLA_H].unsqueeze(2).to_broadcast([P, GLA_H, GLA_DV])
                    own(dve.tensor_tensor(o[:, t], o[:, t], r, ALU.mult))
                    dve.tensor_tensor(o[:, t], o[:, t], g[:, t], ALU.mult).then_inc(gated, 1)

            @block.tensor
            def _(pe):
                for n in range(2 * T):
                    t, h = n // 2, n % 2
                    pe.wait_ge(gated, t + 1)
                    for k in range(4):
                        f = 4 * h + k
                        mm = pe.transpose(tp[:, n, k * P:(k + 1) * P], o[:, t, f // 2, f % 2 * P:(f % 2 + 1) * P],
                                          K.ident[:])
                    mm.then_inc(turned, 1)


def residual(nc, K, lhs, w, started, scale=None):
    with stage(nc, K, "residual") as st:
        ps = st.ps("ps", [P, 4, HALF])
        scaled = st.sb("scaled", [P, 4, HALF]) if scale is not None else None
        bank_full, added, dve_own = map(st.sem, ("bank_full", "added", "dve_own"))
        with nc.Block(no_gpsimd_drain=True) as block:
            @block.sync
            def _(sp):
                for n in range(started, 2):
                    sp.dma_start(in_ring(K, n), columns(w, n)).then_inc(K.ring_in[n], 16)

            @block.tensor
            def _(pe):
                for n in range(2):
                    pe.wait_ge(K.ring_in[n], 16)
                    for t in range(T):
                        for k in range(KC):
                            mm = pe.matmul(ps[:, 2 * n + t, :], lhs[:, k, t * P:(t + 1) * P],
                                           in_ring(K, n)[:, k, :], start=k == 0, stop=k == KC - 1)
                        mm.then_inc(bank_full, 1)

            @block.vector
            def _(dve):
                own = Chain(dve, dve_own)
                for u in range(4):
                    n, t = u // 2, u % 2
                    x = K.x[:, t, n * HALF:(n + 1) * HALF]
                    y = ps[:, u, :]
                    dve.wait_ge(bank_full, u + 1)
                    if scale is not None:
                        own(dve.tensor_tensor(scaled[:, u, :], y, scale(n), ALU.mult))
                        y = scaled[:, u, :]
                    own(dve.tensor_tensor(x, x, y, ALU.add))
    clear_ring(nc, K)


def block_one(nc, K, A, ada):
    def win(n):
        return columns(A.attn_w_qkv[0], n), KC

    setup(nc, K, A, [win(n) for n in range(3)])
    gains = K.gain_cols
    norm(nc, K, gain_cols=gains[:, 0:KC])
    with ExitStack() as mem:
        def sb(name, shape):
            return mem.enter_context(nc.sbuf_tensor(name, shape, F32))

        qkv = sb("qkv", [P, T, (QK_HEADS + N_KV) * HD])
        qT = sb("qT", [P, N_HEADS // 2, S])
        kT = sb("kT", [P, N_KV, S])
        project(nc, K, K.hT, [(win(n)[0], "tokens") for n in range(3)],
                lambda act, n, t, ps: act.activation(qkv[:, t, n * HALF:(n + 1) * HALF], ps, ACT.Copy),
                started=3)
        rope(nc, K, qkv, qT, kT, A, [(columns(A.attn_w_o[0], n), KC) for n in range(2)])
        v0 = QK_HEADS * HD
        attend(nc, K, N_HEADS, HD ** -0.5,
               lambda h: qT[h % 2 * HD:h % 2 * HD + HD, h // 2, :],
               lambda h: kT[h % 2 * HD:h % 2 * HD + HD, h // (N_HEADS // N_KV), :],
               lambda h, k: qkv[:, k, v0 + h // (N_HEADS // N_KV) * HD:v0 + (h // (N_HEADS // N_KV) + 1) * HD],
               K.hT)
        residual(nc, K, K.hT, A.attn_w_o[0], started=2)
    norm(nc, K, gain_cols=gains[:, 16:16 + KC])
    mlp(nc, K, A.mlp_w_in[0], A.mlp_w_out[0], conditions=(ada, gains[:, 32:40], A.w_ada_2, A.b_ada_2))
    spread(nc, K, ada)
    norm(nc, K, gain_cols=gains[:, 8:16])
    with ExitStack() as mem:
        def sb(name, shape):
            return mem.enter_context(nc.sbuf_tensor(name, shape, F32))

        q, k = (sb(n, [P, T, HALF]) for n in ("q", "k"))
        v, gate = (sb(n, [P, T, D]) for n in ("v", "gate"))

        def evacuate(act, n, t, ps):
            if n == 0:
                return act.activation(q[:, t, :], ps, ACT.Copy, scale=GLA_DK ** -0.5)
            if n == 1:
                return act.activation(k[:, t, :], ps, ACT.Copy)
            to, c = (v, n - 2) if n < 4 else (gate, n - 4)
            return act.activation(to[:, t, c * HALF:(c + 1) * HALF], ps, ACT.Copy if n < 4 else ACT.Silu)

        project(nc, K, K.hT, [(columns(A.gla_w_in[0], n), "tokens") for n in range(6)], evacuate)
        with ExitStack() as inner:
            logg = inner.enter_context(nc.sbuf_tensor("logg", [P, T, 2, HALF], F32))
            gla_gates(nc, K, A, logg, [])
            o = K.hT[:].rearrange("p k n -> p (k n)").rearrange("p (t h d) -> p t h d", t=T, h=GLA_H)
            gla_scan(nc, K, q, k, v, logg, o)
        oT = v[:].rearrange("p t d -> p (t d)").rearrange("p (k n) -> p k n", k=KC)
        gla_out(nc, K, A, o, gate[:], oT, [(columns(A.gla_w_o[0], n), KC) for n in range(2)])
        residual(nc, K, oT, A.gla_w_o[0], started=2)
    norm(nc, K, gain_cols=gains[:, 24:32])
    mlp(nc, K, A.mlp_w_in[1], A.mlp_w_out[1])
    norm(nc, K, gain=A.final_norm.rearrange("(a n) -> a n", a=1), turn=False, keep=K.x)




def tables(nc, K):
    with stage(nc, K, "tables") as st:
        whole = st.sb("whole", [P, T, S], mybir.dt.int32)
        few = st.sb("few", [P, TOPK], mybir.dt.int32)
        (own_sem,) = map(st.sem, ("own_sem",))
        with nc.Block(no_gpsimd_drain=True) as block:
            @block.gpsimd
            def _(pool):
                own = Chain(pool, own_sem)
                own(pool.iota(whole[:], pattern=[[-P, T], [1, S]], base=0, channel_multiplier=-1))
                own(pool.tensor_copy(K.far[:], whole[:]))
                own(pool.affine_select(out=K.far[:], in_=K.far[:], compare_op=ALU.is_ge, fill=MASKED, base=0,
                                       pattern=[[P, T], [-1, S]], channel_multiplier=1))
                own(pool.iota(few[:], pattern=[[1, TOPK]], base=0, channel_multiplier=0))
                own(pool.tensor_copy(K.places[:], few[:]))
                own(pool.memset(K.zeros[:], 0.0))


class Convolution:

    def __init__(self, st, K, conv_w, b, c, h):
        self.K, self.conv_w, self.b, self.c, self.h = K, conv_w, b, c, h
        self.rows = st.sb("conv_rows", [CONV_K * 4, P])
        self.w = st.sb("conv_cols", [P, CONV_K, 4])
        self.turned = st.ps("conv_turn", [P, HALF])
        self.z, self.part = (st.sb(n, [P, 4, S]) for n in ("conv_z", "conv_part"))
        self.loaded, self.cols_done, self.cols_moved, self.own_sem = map(
            st.sem, ("conv_loaded", "conv_cols_done", "conv_cols_moved", "conv_own"))

    def sync(self, sp):
        sp.dma_start(self.rows[:], self.conv_w).then_inc(self.loaded, 16)

    def tensor(self, pe):
        pe.wait_ge(self.loaded, 16)
        pe.transpose(self.turned[:, 0:12], self.rows[:], self.K.ident[0:12, 0:12]).then_inc(self.cols_done, 1)

    def scalar(self, act):
        act.wait_ge(self.cols_done, 1)
        act.activation(self.w[:].rearrange("p k c -> p (k c)"), self.turned[:, 0:12],
                       ACT.Copy).then_inc(self.cols_moved, 1)

    def gpsimd(self, pool):
        own = Chain(pool, self.own_sem)
        own(pool.tensor_tensor(self.z[:], self.c[:], self.h[:], ALU.mult))
        pool.wait_ge(self.cols_moved, 1)

        def weight(k, n):
            return self.w[:, k, :].unsqueeze(2).to_broadcast([P, 4, n])

        y = self.c
        own(pool.tensor_tensor(y[:], self.z[:], weight(2, S), ALU.mult))
        for back in (1, 2):
            n = S - back
            own(pool.tensor_tensor(self.part[:, :, 0:n], self.z[:, :, 0:n], weight(2 - back, n), ALU.mult))
            own(pool.tensor_tensor(y[:, :, back:S], y[:, :, back:S], self.part[:, :, 0:n], ALU.add))
        own(pool.tensor_tensor(y[:], y[:], self.b[:], ALU.mult))


def merge(nc, K, yaT, ycT, gates, w_attn, w_conv, mT):
    with stage(nc, K, "merge") as st:
        wide = st.ps("wide", [P, 8, HALF])
        summed, gated, turned, moved, dve_own = map(
            st.sem, ("summed", "gated", "turned", "moved", "dve_own"))
        with nc.Block(no_gpsimd_drain=True) as block:
            @block.tensor
            def _(pe):
                for t in range(T):
                    for a, y in enumerate((yaT, ycT)):
                        w = in_ring(K, a, 4)
                        pe.wait_ge(K.ring_in[a], 16)
                        for b in range(2):
                            for k in range(4):
                                mm = pe.matmul(wide[:, 4 * t + 2 * a + b, :], y[:, k, t * P:(t + 1) * P],
                                               w[:, k, b * HALF:(b + 1) * HALF], start=k == 0, stop=k == 3)
                            mm.then_inc(summed, 1)
                for t in range(T):
                    pe.wait_ge(gated, t + 1)
                    for h in range(2):
                        for k in range(4):
                            f = (4 * h + k) * P
                            mm = pe.transpose(wide[:, 4 * t + h, k * P:(k + 1) * P],
                                              gates[:, 0, t, f:f + P], K.ident[:])
                        mm.then_inc(turned, 1)

            @block.vector
            def _(dve):
                own = Chain(dve, dve_own)
                for t in range(T):
                    for a in range(2):
                        dve.wait_ge(summed, 4 * t + 2 * a + 2)
                        own(dve.tensor_tensor(gates[:, a, t, :], gates[:, a, t, :],
                                              wide[:, 4 * t + 2 * a:4 * t + 2 * a + 2, :].rearrange(
                                                  "p b n -> p (b n)"), ALU.mult))
                    dve.tensor_tensor(gates[:, 0, t, :], gates[:, 0, t, :], gates[:, 1, t, :],
                                      ALU.add).then_inc(gated, 1)

            @block.scalar
            def _(act):
                for n in range(2 * T):
                    t, h = n // 2, n % 2
                    act.wait_ge(turned, n + 1)
                    act.activation(mT[:, 4 * h:4 * h + 4, t * P:(t + 1) * P],
                                   wide[:, 4 * t + h, :].rearrange("p (k n) -> p k n", k=4),
                                   ACT.Copy).then_inc(moved, 1)
    clear_ring(nc, K)


def peer_scores(nc, K, sub_keys, qT, scores):
    M = 2 * PH
    with stage(nc, K, "peer_scores") as st:
        keys = st.sb("keys", [P, M, DKEY])
        keysT = st.sb("keysT", [P, M, NKEYS])
        tp = st.ps("tp", [P, 4, HALF])
        ps = st.ps("ps", [P, 4, HALF])
        loaded, turned, keys_moved, scored, moved = map(
            st.sem, ("loaded", "turned", "keys_moved", "scored", "moved"))
        with nc.Block(no_gpsimd_drain=True) as block:
            @block.sync
            def _(sp):
                for half in range(2):
                    m = slice(half * PH, (half + 1) * PH)
                    sp.dma_start(keys[:, m, :], sub_keys[half * 4:half * 4 + 4].rearrange(
                        "h a n d -> n (h a) d")).then_inc(loaded, 16)

            @block.tensor
            def _(pe):
                pe.wait_ge(loaded, 32)
                for n in range(4):
                    for k in range(4):
                        mm = pe.transpose(tp[:, n, k * P:(k + 1) * P], keys[:, 4 * n + k, :], K.ident[:])
                    mm.then_inc(turned, 1)
                for u in range(8):
                    g, t = u // 2, u % 2
                    pe.wait_ge(keys_moved, g + 1)
                    if u >= 4:
                        pe.wait_ge(moved, u - 3)
                    for k in range(4):
                        m = 4 * g + k
                        mm = pe.matmul(ps[:, u % 4, k * P:(k + 1) * P], qT[:, m, t * P:(t + 1) * P],
                                       keysT[:, m, :], start=True, stop=True)
                    mm.then_inc(scored, 1)

            @block.scalar
            def _(act):
                for n in range(4):
                    act.wait_ge(turned, n + 1)
                    act.activation(keysT[:, 4 * n:4 * n + 4, :],
                                   tp[:, n, :].rearrange("p (k n) -> p k n", k=4), ACT.Copy).then_inc(keys_moved, 1)

            @block.vector
            def _(dve):
                for u in range(8):
                    g, t = u // 2, u % 2
                    dve.wait_ge(scored, u + 1)
                    dve.tensor_copy(scores[:, t, 2 * g:2 * g + 2, :],
                                    ps[:, u % 4, :].rearrange("p (h n) -> p h n", h=2)).then_inc(moved, 1)


def peer(nc, K, A, l, h2, scores, g2):
    VS = 8
    U_LAYER = 16 * 2 * PH
    V_LAYER = U_LAYER * TOPK // VS
    AHEAD = 24
    rows_u = A.expert_u_2.rearrange("l e d -> (l e) d")
    rows_v = A.expert_v_2.rearrange("l e d -> (l e) d")
    u_slot = K.ring[:].rearrange("p s (j d) -> p (s j) d", d=D)
    with stage(nc, K, "peer") as st:
        v_slot = st.sb("v_slot", [P, VS, D])
        now, rest = (st.sb(n, [P, 2 * NKEYS]) for n in ("now", "rest"))
        value = st.sb("value", [P, 2, TOPK])
        place = st.sb("place", [P, 2, TOPK], U32)
        place_f = st.sb("place_f", [P, 2, TOPK])
        sums, left = (st.sb(n, [P, TOPK * TOPK]) for n in ("sums", "left"))
        best = st.sb("best", [P, T, TOPK])
        best_at = st.sb("best_at", [P, TOPK], U32)
        half = st.sb("half", [P, 2, TOPK], U32)
        half_f = st.sb("half_f", [P, 2, TOPK])
        hot = st.sb("hot", [P, TOPK, TOPK])
        key = st.sb("key", [P, 2, TOPK])
        expert_f = st.sb("expert_f", [P, TOPK])
        at_u, at_v = (st.sb(n, [P, T, TOPK], U32) for n in ("at_u", "at_v"))
        shift, total, inverse = (st.sb(n, [P, T]) for n in ("shift", "total", "inverse"))
        e, gate, dots, gelu, weight = (st.sb(n, [P, T, TOPK]) for n in ("e", "gate", "dots", "gelu", "weight"))
        diagonal = [K.hT[:].rearrange("p k n -> p (k n)").rearrange("p (j n) -> p j n", j=TOPK),
                    st.sb("diagonal", [P, TOPK, P])]
        scaled = h2
        query = st.ps("query", [P, T, D])
        y = st.ps("y", [P, T, 2, HALF])
        u_in = [st.pool_sem(f"u_in{j}") for j in range(TOPK)]
        v_in = [st.pool_sem(f"v_in{j}") for j in range(VS)]
        (query_ready, at_u_ready, at_v_ready, dots_done, shift_done, e_done, gelu_done, weight_done,
         diagonal_ready, v_used, paced, dve_own) = map(
            st.sem, ("query_ready", "at_u_ready", "at_v_ready", "dots_done", "shift_done", "e_done",
                     "gelu_done", "weight_done", "diagonal_ready", "v_used", "paced", "dve_own"))
        with nc.Block() as block:
            @block.gpsimd
            def _(pool):
                def gather_u(n, t, j):
                    pool.indirect_dma_start(
                        u_slot[:, j, :], None, rows_u,
                        bass.IndirectOffsetOnAxis(ap=at_u[:, t, j:j + 1], axis=0)).then_inc(u_in[j], 16)

                def unit(n, t, last):
                    pool.wait_ge(at_v_ready, n + 1)
                    if not last:
                        pool.wait_ge(at_u_ready, n + 2)
                    for j in range(TOPK):
                        pool.wait_ge(v_used, 16 * n + (j + 1 - VS + AHEAD))
                        pool.sem_inc(paced, 1)
                        pool.indirect_dma_start(
                            v_slot[:, j % VS, :], None, rows_v,
                            bass.IndirectOffsetOnAxis(ap=at_v[:, t, j:j + 1], axis=0)).then_inc(v_in[j % VS], 16)
                        if not last:
                            pool.wait_ge(dots_done, 16 * n + (j + 1))
                            pool.sem_inc(paced, 1)
                            gather_u(n + 1, 1 - t, j)

                pool.wait_ge(at_u_ready, 1)
                for j in range(TOPK):
                    gather_u(0, 0, j)
                with pool.Fori(0, PH - 1) as h:
                    for t in range(T):
                        unit(2 * h + t, t, False)
                unit(2 * PH - 2, 0, False)
                unit(2 * PH - 1, 1, True)

            @block.vector
            def _(dve):
                own = Chain(dve, dve_own)

                def sixteen(values, places, source, spare):
                    own(dve.max(values[:, 0:8], source))
                    own(dve.max_index(places[:, 0:8], values[:, 0:8], source))
                    own(dve.match_replace(spare, values[:, 0:8], source, GONE))
                    own(dve.max(values[:, 8:16], spare))
                    own(dve.max_index(places[:, 8:16], values[:, 8:16], spare))

                def choose(head, t):
                    own(dve.tensor_copy(now[:], scores[:, t, bass.ds(head, 1), :].rearrange("p a n -> p (a n)")))
                    for a in range(2):
                        sixteen(value[:, a, :], place[:, a, :], now[:, a * NKEYS:(a + 1) * NKEYS],
                                rest[:, a * NKEYS:(a + 1) * NKEYS])
                    own(dve.tensor_copy(place_f[:], place[:]))
                    own(dve.tensor_tensor(sums[:].rearrange("p (a b) -> p a b", b=TOPK),
                                          value[:, 0, :].unsqueeze(2).to_broadcast([P, TOPK, TOPK]),
                                          value[:, 1, :].unsqueeze(1).to_broadcast([P, TOPK, TOPK]), ALU.add))
                    sixteen(best[:, t, :], best_at[:], sums[:], left[:])
                    dve.tensor_scalar(shift[:, t:t + 1], best[:, t, 0:1], -1.0, None,
                                      ALU.mult).then_inc(shift_done, 1)
                    own(dve.tensor_scalar(half[:, 0, :], best_at[:], 4, None, ALU.logical_shift_right))
                    own(dve.tensor_scalar(half[:, 1, :], best_at[:], 15, None, ALU.bitwise_and))
                    own(dve.tensor_copy(half_f[:], half[:]))
                    for a in range(2):
                        own(dve.tensor_tensor(hot[:], half_f[:, a, :].unsqueeze(2).to_broadcast([P, TOPK, TOPK]),
                                              K.places[:].unsqueeze(1).to_broadcast([P, TOPK, TOPK]),
                                              ALU.is_equal))
                        own(dve.tensor_tensor(hot[:], hot[:],
                                              place_f[:, a, :].unsqueeze(1).to_broadcast([P, TOPK, TOPK]),
                                              ALU.mult))
                        own(dve.tensor_reduce(key[:, a, :], hot[:], AX.X, ALU.add))
                    own(dve.scalar_tensor_tensor(out=expert_f[:], in0=key[:, 0, :], scalar=float(NKEYS),
                                                 in1=key[:, 1, :], op0=ALU.mult, op1=ALU.add))
                    dve.tensor_scalar(at_u[:, t, :], expert_f[:], K.layer_base[:, 0:1], None,
                                      ALU.add).then_inc(at_u_ready, 1)

                def keep_for_v(n, t):
                    dve.wait_ge(v_used, 16 * n + AHEAD)
                    dve.wait_ge(at_u_ready, n + 2)
                    dve.tensor_copy(at_v[:, t, :], at_u[:, t, :]).then_inc(at_v_ready, 1)

                def unit(h, n, t, last):
                    if not last:
                        choose(h + t, 1 - t)
                    for j in range(TOPK):
                        dve.wait_ge(u_in[j], l * U_LAYER + 16 * n + 16)
                        dve.tensor_tensor_reduce(u_slot[:, j, :], u_slot[:, j, :], query[:, t, :], 1.0, 0.0,
                                                 ALU.mult, ALU.add, dots[:, t, j:j + 1]).then_inc(dots_done, 1)
                    dve.wait_ge(e_done, n + 1)
                    own(dve.reciprocal(inverse[:, t:t + 1], total[:, t:t + 1]))
                    own(dve.tensor_scalar(gate[:, t, :], e[:, t, :], inverse[:, t:t + 1], None, ALU.mult))
                    dve.wait_ge(gelu_done, n + 1)
                    dve.tensor_tensor(weight[:, t, :], gelu[:, t, :], gate[:, t, :],
                                      ALU.mult).then_inc(weight_done, 1)
                    if not last:
                        keep_for_v(n, 1 - t)

                choose(0, 0)
                dve.wait_ge(at_u_ready, 1)
                dve.tensor_copy(at_v[:, 0, :], at_u[:, 0, :]).then_inc(at_v_ready, 1)
                dve.wait_ge(query_ready, T)
                own.clear()
                with dve.Fori(0, PH - 1) as h:
                    with own.turn():
                        for t in range(T):
                            unit(h, 2 * h + t, t, False)
                unit(PH - 1, 2 * PH - 2, 0, False)
                unit(PH - 1, 2 * PH - 1, 1, True)
                own(dve.tensor_scalar(K.layer_base[:], K.layer_base[:], float(EXPERTS), None, ALU.add))
                dve.wait_ge(v_used, 2 * PH * TOPK + AHEAD)
                for t in range(T):
                    own(dve.tensor_tensor(scaled[:, t, :], y[:, t, :, :].rearrange("p b n -> p (b n)"), g2,
                                          ALU.mult))
                    own(dve.tensor_tensor(K.x[:, t, :], K.x[:, t, :], scaled[:, t, :], ALU.add))

            @block.scalar
            def _(act):
                for t in range(T):
                    for b in range(2):
                        ins = act.activation(query[:, t, b * HALF:(b + 1) * HALF],
                                             h2[:, t, b * HALF:(b + 1) * HALF], ACT.Copy)
                    ins.then_inc(query_ready, 1)

                def gates(n, t):
                    act.wait_ge(shift_done, n + 1)
                    act.activation(e[:, t, :], best[:, t, :], ACT.Exp, bias=shift[:, t:t + 1],
                                   accum_out=total[:, t:t + 1]).then_inc(e_done, 1)

                def unit(n, t, last):
                    if not last:
                        gates(n + 1, 1 - t)
                    act.wait_ge(dots_done, 16 * n + 16)
                    act.activation(gelu[:, t, :], dots[:, t, :], ACT.Gelu_apprx_tanh).then_inc(gelu_done, 1)
                    act.wait_ge(weight_done, n + 1)
                    act.wait_ge(v_used, 16 * n + (AHEAD - 16))
                    for j in range(TOPK):
                        act.activation(diagonal[t][:, j, :], K.ident[:], ACT.Copy,
                                       scale=weight[:, t, j:j + 1]).then_inc(diagonal_ready, 1)

                gates(0, 0)
                with act.Fori(0, PH - 1) as h:
                    for t in range(T):
                        unit(2 * h + t, t, False)
                unit(2 * PH - 2, 0, False)
                unit(2 * PH - 1, 1, True)

            @block.tensor
            def _(pe):
                for t in range(T):
                    for b in range(2):
                        mm = pe.matmul(y[:, t, b, :], K.zeros[:, 0:P], K.zeros[:], start=True, stop=False,
                                       skip_group_check=True)
                pe.sem_inc(v_used, AHEAD)

                def unit(n, t):
                    for j in range(TOPK):
                        pe.wait_ge(diagonal_ready, 16 * n + (j + 1))
                        pe.wait_ge(v_in[j % VS], l * V_LAYER + 32 * n + 16 * (j // VS + 1))
                        for b in range(2):
                            mm = pe.matmul(y[:, t, b, :], diagonal[t][:, j, :],
                                           v_slot[:, j % VS, b * HALF:(b + 1) * HALF], start=False, stop=False,
                                           skip_group_check=True)
                        mm.then_inc(v_used, 1)

                with pe.Fori(0, PH) as h:
                    for t in range(T):
                        unit(2 * h + t, t)


def block_two(nc, K, A, ada):
    tables(nc, K)
    with nc.Fori(0, LAYERS) as l:
        def layer(w):
            return w[bass.ds(l, 1)]

        def matrix(w):
            return layer(w).rearrange("a k n -> (a k) n")

        def condition(n, columns=slice(0, D)):
            return ada[:, bass.ds(l * ADA + (n * D + columns.start), columns.stop - columns.start)]

        w_in = matrix(A.w_in_2)
        norm(nc, K, gain=layer(A.norm1_g_2), modulate=(condition(1), condition(0)),
             panels=[(columns(w_in, n), KC) for n in range(SLOTS)])
        with ExitStack() as mem:
            def sb(name, shape):
                return mem.enter_context(nc.sbuf_tensor(name, shape, F32))

            turned = {n: sb(f"mix_{n}", [P, 4, S]) for n in ("q", "k", "b", "c", "h")}
            v = sb("mix_v", [P, T, HALF])
            gates = sb("mix_gates", [P, 2, T, D])
            kinds = ["q", "k", "v", "b", "c", "h", 0, 1, 2, 3]

            def evacuate(act, n, bank, ps):
                kind = kinds[n]
                if kind == "v":
                    return act.activation(v[:, bank, :], ps, ACT.Copy)
                if kind in turned:
                    return act.activation(turned[kind][:, 2 * bank:2 * bank + 2, :],
                                          ps.rearrange("p (m n) -> p m n", m=2), ACT.Copy)
                return act.activation(gates[:, kind // 2, bank, kind % 2 * HALF:(kind % 2 + 1) * HALF], ps,
                                      ACT.Sigmoid)

            project(nc, K, K.hT, [(columns(w_in, n), "features" if k in turned else "tokens")
                                  for n, k in enumerate(kinds)], evacuate, started=SLOTS)
            yaT = K.hT[:, 0:4, :]

            def head(a):
                return lambda h: turned[a][h % 2 * HD:h % 2 * HD + HD, h // 2, :]

            conv_w = layer(A.conv_w_2).rearrange("a k (c p) -> (a k c) p", p=P)
            proj = [matrix(w).rearrange("(k p) n -> p k n", p=P) for w in (A.w_attn_proj_2, A.w_conv_proj_2)]
            attend(nc, K, MH, HD ** -0.5, head("q"), head("k"),
                   lambda h, k: v[:, k, h * HD:(h + 1) * HD], yaT, far=K.far,
                   side_of=lambda st: Convolution(st, K, conv_w, turned["b"], turned["c"], turned["h"]),
                   panels=[(w, 4) for w in proj])
            merge(nc, K, yaT, turned["c"], gates, A.w_attn_proj_2, A.w_conv_proj_2, K.hT)
        residual(nc, K, K.hT, matrix(A.w_out_2), started=0,
                 scale=lambda n: condition(2, slice(n * HALF, (n + 1) * HALF)))
        with ExitStack() as mem:
            h2 = mem.enter_context(nc.sbuf_tensor("h2", [P, T, D], F32))
            scores = mem.enter_context(nc.sbuf_tensor("scores", [P, T, PH, 2 * NKEYS], F32))
            w_query = matrix(A.w_query_2)
            norm(nc, K, gain=layer(A.norm2_g_2), modulate=(condition(4), condition(3)), keep=h2,
                 panels=[(columns(w_query, n), KC) for n in range(SLOTS)])
            with ExitStack() as inner:
                qT = inner.enter_context(nc.sbuf_tensor("peer_q", [P, 2 * PH, S], F32))
                project(nc, K, K.hT, [(columns(w_query, n), "features") for n in range(4)],
                        lambda act, n, bank, ps: act.activation(
                            qT[:, 4 * n + 2 * bank:4 * n + 2 * bank + 2, :],
                            ps.rearrange("p (m n) -> p m n", m=2), ACT.Copy), started=SLOTS)
                peer_scores(nc, K, layer(A.sub_keys_2).rearrange("l h a n d -> (l h) a n d"), qT, scores)
            peer(nc, K, A, l, h2, scores, condition(5))



def program(nc, A, out):
    K = Kept()
    K.stages = K.pool_sems = 0
    with ExitStack() as kept:
        def sb(name, shape, dt=F32):
            return kept.enter_context(nc.sbuf_tensor(name, shape, dt))

        K.ring = sb("ring", [P, SLOTS, PANEL])
        K.x = sb("x", [P, T, D])
        K.hT = sb("hT", [P, KC, S])
        K.ident = sb("ident", [P, P])
        K.ones = sb("ones", [P, P])
        K.gain_cols = sb("gain_cols", [P, 5 * KC])
        K.layer_base = sb("layer_base", [P, 1])
        K.far = sb("far", [P, T, S])
        K.places = sb("places", [P, TOPK])
        K.zeros = sb("zeros", [P, HALF])
        K.ring_in = [kept.enter_context(nc.semaphore(f"ring_in{n}")) for n in range(SLOTS)]
        ada = sb("ada", [P, LAYERS * ADA])

        block_one(nc, K, A, ada)
        block_two(nc, K, A, ada)
        norm(nc, K, gain=A.final_g_2.rearrange("(a n) -> a n", a=1), turn=False, out=out)


_INS = ["x", "norm_mix", "norm_mlp", "attn_w_qkv", "attn_q_norm", "attn_k_norm", "attn_w_o", "gla_w_in",
        "gla_w_gate_up", "gla_b_gate", "gla_out_norm", "gla_w_o", "mlp_w_in", "mlp_w_out", "final_norm",
        "c_2", "norm1_g_2", "norm2_g_2", "w_ada_2", "b_ada_2", "w_in_2", "conv_w_2", "w_attn_proj_2",
        "w_conv_proj_2", "w_out_2", "w_query_2", "sub_keys_2", "expert_u_2", "expert_v_2", "final_g_2"]


def rope_table():
    half = HD // 2
    inv = np.float32(10000.0) ** (-np.arange(0, half, 2, dtype=np.float32) / np.float32(half))
    pos = np.stack([np.arange(S) // 64, np.arange(S) % 64], 1).astype(np.float32)
    ang = pos[:, :, None] * inv[None, None, :]
    cos = np.repeat(np.cos(ang)[:, :, None, :], 2, axis=2).reshape(S, HD)
    sin = (np.sin(ang)[:, :, None, :] * np.array([-1, 1], np.float32)[None, None, :, None]).reshape(S, HD)
    return np.ascontiguousarray(np.stack([cos, sin], 1).astype(np.float32))


def kernel(**inputs):
    import numpy as _np
    import concourse.bacc as _bacc
    from concourse import mybir as _mybir
    from concourse.bass_utils import run_bass_kernel_spmd as _run

    nc = _bacc.Bacc("TRN2", target_bir_lowering=False, num_devices=1)
    A = Kept()
    arrays = {}

    def declare(name, a):
        arrays[f"in_{name}_dram"] = a
        return nc.dram_tensor(f"in_{name}_dram", a.shape, _mybir.dt.from_np(a.dtype), kind="ExternalInput").ap()

    ins = {name: declare(name, _np.ascontiguousarray(inputs[name])) for name in _INS}
    ins["rope_table"] = declare("rope_table", rope_table())
    A.__dict__.update(ins)
    out = nc.dram_tensor("out_0_dram", (1, S, D), _mybir.dt.float32, kind="ExternalOutput").ap()
    program(nc, A, out)
    r = _run(nc, [arrays], core_ids=[0])
    return r.results[0]["out_0_dram"]
```

```python
import math
from contextlib import ExitStack, contextmanager

import numpy as np

import concourse.bass as bass
from concourse import mybir

ALU = mybir.AluOpType
ACT = mybir.ActivationFunctionType
AX = mybir.AxisListType
F32 = mybir.dt.float32
F32R = mybir.dt.float32r
U32 = mybir.dt.uint32

P = 128
D = 1024
S = 256
T = S // P
KC = D // P
HALF = 512
EPS = 1e-6
SLOTS = 4
PANEL = 4096
PIECE = PANEL // 4
PIECES = 3

N_HEADS, N_KV, HD = 16, 4, 64
QK_HEADS = N_HEADS + N_KV
GLA_H, GLA_DK, GLA_DV, CHUNK, RANK = 4, 128, 256, 64, 16
N_CHUNKS = S // CHUNK
D_FF = 4 * D
LAYERS = 2
MH = 8
CONV_K = 3
ADA = 6 * D
PH, NKEYS, DKEY, TOPK = 8, 128, 128, 16
EXPERTS = NKEYS * NKEYS
STAGE_SEMS = 150
POOL_SEMS = 200
MASKED = -1e30
GONE = -3.0e38


class Chain:

    def __init__(self, eng, sem):
        self.eng, self.sem, self.n = eng, sem, 0

    def __call__(self, ins):
        self.n += 1
        ins.then_inc(self.sem, 1)
        self.eng.wait_ge(self.sem, self.n)
        return ins

    def clear(self):
        self.eng.sem_clear(self.sem)
        self.n = 0

    @contextmanager
    def turn(self):
        assert self.n == 0, "clear it ahead of the loop"
        yield
        self.clear()


class Stage:

    def __init__(self, nc, K, mem, name):
        K.stages += 1
        self.nc, self.K, self.mem, self.name, self.used = nc, K, mem, f"{name}{K.stages}", 0

    def sb(self, name, shape, dt=F32):
        return self.mem.enter_context(self.nc.sbuf_tensor(f"{self.name}_{name}", shape, dt))

    def ps(self, name, shape, dt=F32):
        return self.mem.enter_context(self.nc.psum_tensor(f"{self.name}_{name}", shape, dt))

    def sem(self, name):
        self.used += 1
        return self.mem.enter_context(self.nc.semaphore(f"{self.name}_{name}", num=STAGE_SEMS + self.used - 1))

    def pool_sem(self, name):
        self.K.pool_sems += 1
        return self.mem.enter_context(self.nc.semaphore(f"{self.name}_{name}",
                                                        num=POOL_SEMS + self.K.pool_sems - 1))


class Kept:
    pass


@contextmanager
def stage(nc, K, name):
    with ExitStack() as mem:
        st = Stage(nc, K, mem, name)
        yield st
        nc.all_engine_barrier(sems_to_clear=range(STAGE_SEMS, STAGE_SEMS + st.used))


def columns(w, n):
    return w[:, n * HALF:(n + 1) * HALF].rearrange("(k p) n -> p k n", p=P)


def ring_view(K, slot, k=KC):
    return K.ring[:, slot, :].rearrange("p (k n) -> p k n", k=k)


def begin_ring(nc, K):
    K.loaded = K.used = 0
    nc.all_engine_barrier(sems_to_clear=range(K.ring_in[0].num, K.ring_in[-1].num + 1))


def start_panels(dma, K, panels, split_done=None, first=None):
    for src, k in panels:
        before = K.loaded - SLOTS
        if split_done is None:
            assert before < K.used
        elif before >= first:
            dma.wait_ge(split_done, 4 * (before - first) + 4)
        dma.dma_start(ring_view(K, K.loaded % SLOTS, k), src).then_inc(K.ring_in[K.loaded % SLOTS], 16)
        K.loaded += 1


def take_panels(K, n):
    first = K.used
    K.used += n
    return range(first, first + n)


def arrived(i):
    return 16 * (i // SLOTS + 1)


class Parts:

    def __init__(self, mem, nc, name, shape):
        self.hi, self.lo = (mem.enter_context(nc.sbuf_tensor(f"{name}_{n}", shape, F32R)) for n in ("hi", "lo"))


def rest_of(dve, out_lo, a, hi):
    return dve.tensor_tensor(out_lo, a, hi.bitcast(F32), ALU.subtract)


def three_passes(pe, out, lhs, rhs, at, to, start, stop, **more):
    pe.matmul(out, at(lhs.hi), to(rhs.hi), start=start, stop=False, **more)
    pe.matmul(out, at(lhs.hi), to(rhs.lo), start=False, stop=False, **more)
    return pe.matmul(out, at(lhs.lo), to(rhs.hi), start=False, stop=stop, **more)



def setup(nc, K, A, first_panels):
    with stage(nc, K, "setup") as st:
        rows = st.sb("rows", [KC, P])
        cols = st.ps("cols", [P, HALF])
        loaded, zeroed, made, turned, gpsimd_own = map(
            st.sem, ("loaded", "zeroed", "made", "turned", "gpsimd_own"))
        with nc.Block(no_gpsimd_drain=True) as block:
            @block.sync
            def _(sp):
                sp.dma_start(K.x[:], A.x[0].rearrange("(t p) d -> p t d", p=P)).then_inc(loaded, 16)
                sp.dma_start(rows[:], A.c_2.rearrange("a (k p) -> (a k) p", p=P)).then_inc(loaded, 16)
                start_panels(sp, K, first_panels)
                sp.wait_ge(loaded, 16 * 2)

            @block.gpsimd
            def _(pool):
                own = Chain(pool, gpsimd_own)
                own(pool.memset(K.ident[:], 0.0))
                own(pool.memset(K.ones[:], 1.0))
                pool.affine_select(out=K.ident[:], in_=K.ident[:], compare_op=ALU.not_equal, fill=1.0,
                                   base=0, pattern=[[-1, P]], channel_multiplier=1).then_inc(made, 1)

            @block.tensor
            def _(pe):
                pe.wait_ge(loaded, 16 * 2)
                pe.wait_ge(made, 1)
                pe.transpose(cols[:, 0:KC], rows[:], K.ident[0:KC, 0:KC]).then_inc(turned, 1)

            @block.vector
            def _(dve):
                dve.memset(K.layer_base[:], 0.0).then_inc(zeroed, 1)
                dve.wait_ge(turned, 1)
                dve.tensor_copy(K.c_cols[:], cols[:, 0:KC]).then_inc(zeroed, 1)
                dve.wait_ge(zeroed, 2)



def norm(nc, K, gain, modulate=None, hT=None, out=None, keep=None, panels=()):
    with stage(nc, K, "norm") as st:
        xn = st.sb("xn", [P, T, D]) if keep is None else keep
        squares = st.ps("squares", [P, T, 2, HALF])
        rows = st.sb("rows", [P, D])
        ssq, ms, std, rstd = (st.sb(n, [P, T]) for n in ("ssq", "ms", "std", "rstd"))
        tp = st.ps("tp", [P, 2 * T, HALF])
        ssq_done, ms_done, std_done, xn_done, turned, hi_done, loaded, stored, dve_own = map(
            st.sem, ("ssq_done", "ms_done", "std_done", "xn_done", "turned", "hi_done", "loaded",
                     "stored", "dve_own"))

        def halves(a, n):
            t, h = n // 2, n % 2
            return a[:, 4 * h:4 * h + 4, t * P:(t + 1) * P]

        def bank(n):
            return tp[:, n, :].rearrange("p (k n) -> p k n", k=4)

        with nc.Block(no_gpsimd_drain=True) as block:
            @block.sync
            def _(sp):
                sp.dma_start(rows[:], gain.partition_broadcast(P)).then_inc(loaded, 16)
                start_panels(sp, K, panels)
                if out is not None:
                    sp.wait_ge(xn_done, T)
                    sp.dma_start(out[0].rearrange("(t p) d -> p t d", p=P), xn[:]).then_inc(stored, 16)
                    sp.wait_ge(stored, 16)

            @block.scalar
            def _(act):
                for t in range(T):
                    act.activation(squares[:, t, :, :].rearrange("p b n -> p (b n)"), K.x[:, t, :], ACT.Square,
                                   accum_out=ssq[:, t:t + 1]).then_inc(ssq_done, 1)
                act.wait_ge(ms_done, 1)
                act.activation(std[:], ms[:], ACT.Sqrt).then_inc(std_done, 1)
                for n in range(2 * T if hT else 0):
                    act.wait_ge(turned, n + 1)
                    act.activation(halves(hT.hi, n), bank(n), ACT.Copy).then_inc(hi_done, 1)

            @block.vector
            def _(dve):
                own = Chain(dve, dve_own)
                dve.wait_ge(loaded, 16)
                if modulate is not None:
                    own(dve.scalar_tensor_tensor(out=rows[:], in0=modulate[0], scalar=1.0, in1=rows[:],
                                                 op0=ALU.add, op1=ALU.mult))
                dve.wait_ge(ssq_done, T)
                dve.tensor_scalar(ms[:], ssq[:], 1.0 / D, EPS, ALU.mult, ALU.add).then_inc(ms_done, 1)
                dve.wait_ge(std_done, 1)
                own(dve.reciprocal(rstd[:], std[:]))
                for t in range(T):
                    ins = dve.scalar_tensor_tensor(out=xn[:, t, :], in0=K.x[:, t, :], scalar=rstd[:, t:t + 1],
                                                   in1=rows[:], op0=ALU.mult, op1=ALU.mult)
                    if modulate is None:
                        ins.then_inc(xn_done, 1)
                    else:
                        own(ins)
                        dve.tensor_tensor(xn[:, t, :], xn[:, t, :], modulate[1], ALU.add).then_inc(xn_done, 1)
                for n in range(2 * T if hT else 0):
                    dve.wait_ge(hi_done, n + 1)
                    rest_of(dve, halves(hT.lo, n), bank(n), halves(hT.hi, n))

            @block.tensor
            def _(pe):
                for n in range(2 * T if hT else 0):
                    t, h = n // 2, n % 2
                    pe.wait_ge(xn_done, t + 1)
                    for k in range(4):
                        f = (4 * h + k) * P
                        mm = pe.transpose(tp[:, n, k * P:(k + 1) * P], xn[:, t, f:f + P], K.ident[:])
                    mm.then_inc(turned, 1)



def split_piece(act, K, w, i, c, piece, piece_free, hi_done):
    if c == 0:
        act.wait_ge(K.ring_in[i % SLOTS], arrived(i))
    if piece >= PIECES:
        act.wait_ge(piece_free, piece - PIECES + 1)
    act.activation(w.hi[:, piece % PIECES, :], K.ring[:, i % SLOTS, c * PIECE:(c + 1) * PIECE],
                   ACT.Copy).then_inc(hi_done, 1)


def rest_of_piece(dve, K, w, i, c, piece, hi_done, split_done):
    dve.wait_ge(hi_done, piece + 1)
    rest_of(dve, w.lo[:, piece % PIECES, :], K.ring[:, i % SLOTS, c * PIECE:(c + 1) * PIECE],
            w.hi[:, piece % PIECES, :]).then_inc(split_done, 1)


def project(nc, K, lhs, kinds, evacuate, own_panels=(), following=()):
    panels = take_panels(K, len(kinds))
    with stage(nc, K, "project") as st:
        w = Parts(st.mem, nc, st.name, [P, PIECES, PIECE])
        ps = st.ps("ps", [P, 2, 4, HALF])
        hi_done, split_done, piece_used, bank_free = map(
            st.sem, ("hi_done", "split_done", "piece_used", "bank_free"))
        with nc.Block(no_gpsimd_drain=True) as block:
            @block.sync
            def _(sp):
                start_panels(sp, K, own_panels, split_done, panels[0])
                start_panels(sp, K, following, split_done, panels[0])

            @block.tensor
            def _(pe):
                for n, kind in enumerate(kinds):
                    if n >= 2:
                        pe.wait_ge(bank_free, 2 * (n - 2) + 2)
                    for c in range(4):
                        piece = 4 * n + c
                        pe.wait_ge(split_done, piece + 1)
                        for kk in range(2):
                            k = 2 * c + kk
                            a = piece % PIECES
                            if kind == "tokens":
                                for t in range(T):
                                    mm = three_passes(pe, ps[:, n % 2, t, :], lhs, w,
                                                      lambda x: x[:, k, t * P:(t + 1) * P],
                                                      lambda x: x[:, a, kk * HALF:(kk + 1) * HALF],
                                                      start=k == 0, stop=k == KC - 1)
                            else:
                                for m in range(4):
                                    f = kk * HALF + m * P
                                    mm = three_passes(pe, ps[:, n % 2, m, 0:S], w, lhs,
                                                      lambda x: x[:, a, f:f + P], lambda x: x[:, k, :],
                                                      start=k == 0, stop=k == KC - 1)
                        mm.then_inc(piece_used, 1)

            @block.scalar
            def _(act):
                def take_out(n):
                    for b in range(2):
                        act.wait_ge(piece_used, 4 * n + 4)
                        a = ps[:, n % 2, b, :] if kinds[n] == "tokens" else ps[:, n % 2, 2 * b:2 * b + 2, 0:S]
                        evacuate(act, n, b, a).then_inc(bank_free, 1)

                for n, i in enumerate(panels):
                    for c in range(4):
                        split_piece(act, K, w, i, c, 4 * n + c, piece_used, hi_done)
                        if c == 2 and n >= 1:
                            take_out(n - 1)
                take_out(len(kinds) - 1)

            @block.vector
            def _(dve):
                for n, i in enumerate(panels):
                    for c in range(4):
                        rest_of_piece(dve, K, w, i, c, 4 * n + c, hi_done, split_done)



def rope(nc, K, qkv, qT, kT, A):
    QK = QK_HEADS * HD
    with stage(nc, K, "rope") as st:
        gains = st.sb("gains", [P, 2, HD])
        table = st.sb("table", [P, T, 2, HD])
        squares = st.sb("squares", [P, T, QK])
        straight = st.sb("straight", [P, T, QK])
        crossed = st.sb("crossed", [P, T, QK])
        kk = st.sb("kk", [P, T, N_KV, 2, HD])
        ms, std, rstd = (st.sb(n, [P, T, QK_HEADS]) for n in ("ms", "std", "rstd"))
        tp = st.ps("tp", [P, 6, HALF])
        loaded, squared, ms_done, std_done, rotated, turned, moved, dve_own = map(
            st.sem, ("loaded", "squared", "ms_done", "std_done", "rotated", "turned", "moved", "dve_own"))
        with nc.Block(no_gpsimd_drain=True) as block:
            @block.sync
            def _(sp):
                sp.dma_start(gains[:, 0, :], A.attn_q_norm[0:1, :].partition_broadcast(P)).then_inc(loaded, 16)
                sp.dma_start(gains[:, 1, :], A.attn_k_norm[0:1, :].partition_broadcast(P)).then_inc(loaded, 16)
                sp.dma_start(table[:], A.rope_table.rearrange("(t p) a d -> p t a d", p=P)).then_inc(loaded, 16)

            @block.scalar
            def _(act):
                for t in range(T):
                    act.activation(squares[:, t, :], qkv[:, t, 0:QK], ACT.Square).then_inc(squared, 1)
                for t in range(T):
                    act.wait_ge(ms_done, t + 1)
                    act.activation(std[:, t, :], ms[:, t, :], ACT.Sqrt).then_inc(std_done, 1)
                for n in range(6):
                    act.wait_ge(turned, n + 1)
                    t, b = n // 3, n % 3
                    to = qT[:, 4 * b:4 * b + 4, :] if b < 2 else kT[:, 0:4, :]
                    act.activation(to[:, :, t * P:(t + 1) * P],
                                   tp[:, n, :].rearrange("p (k n) -> p k n", k=4),
                                   ACT.Copy).then_inc(moved, 1)

            @block.vector
            def _(dve):
                own = Chain(dve, dve_own)
                for t in range(T):
                    dve.wait_ge(squared, t + 1)
                    own(dve.tensor_reduce(ms[:, t, :], squares[:, t, :].rearrange("p (h d) -> p h d", d=HD),
                                          AX.X, ALU.add))
                    dve.tensor_scalar(ms[:, t, :], ms[:, t, :], 1.0 / HD, EPS, ALU.mult,
                                      ALU.add).then_inc(ms_done, 1)
                dve.wait_ge(loaded, 16 * 3)
                for t in range(T):
                    dve.wait_ge(std_done, t + 1)
                    own(dve.reciprocal(rstd[:, t, :], std[:, t, :]))
                    x = qkv[:, t, 0:QK].rearrange("p (h d) -> p h d", d=HD)
                    own(dve.tensor_tensor(x, x, rstd[:, t, :].unsqueeze(2).to_broadcast([P, QK_HEADS, HD]),
                                          ALU.mult))
                    for a, heads in ((0, slice(0, N_HEADS)), (1, slice(N_HEADS, QK_HEADS))):
                        n = heads.stop - heads.start
                        own(dve.tensor_tensor(x[:, heads, :], x[:, heads, :],
                                              gains[:, a:a + 1, :].to_broadcast([P, n, HD]), ALU.mult))
                    s = straight[:, t, :].rearrange("p (h d) -> p h d", d=HD)
                    c = crossed[:, t, :].rearrange("p (h r e d) -> p h r e d", r=2, e=2, d=HD // 4)
                    x4 = qkv[:, t, 0:QK].rearrange("p (h r e d) -> p h r e d", r=2, e=2, d=HD // 4)
                    sin = table[:, t, 1, :].rearrange("p (r e d) -> p r e d", r=2, e=2)
                    own(dve.tensor_tensor(s, x, table[:, t, 0:1, :].to_broadcast([P, QK_HEADS, HD]), ALU.mult))
                    for e in range(2):
                        own(dve.tensor_tensor(
                            c[:, :, :, e, :], x4[:, :, :, 1 - e, :],
                            sin[:, :, e, :].unsqueeze(1).to_broadcast([P, QK_HEADS, 2, HD // 4]), ALU.mult))
                    q = slice(0, N_HEADS * HD)
                    k = slice(N_HEADS * HD, QK)
                    own(dve.tensor_tensor(straight[:, t, q], straight[:, t, q], crossed[:, t, q], ALU.add))
                    for copy in range(2):
                        own(dve.tensor_tensor(
                            kk[:, t, :, copy, :], straight[:, t, k].rearrange("p (h d) -> p h d", d=HD),
                            crossed[:, t, k].rearrange("p (h d) -> p h d", d=HD), ALU.add))
                    dve.sem_inc(rotated, 1)

            @block.tensor
            def _(pe):
                for n in range(6):
                    t, b = n // 3, n % 3
                    pe.wait_ge(rotated, t + 1)
                    for k in range(4):
                        if b < 2:
                            a = straight[:, t, (4 * b + k) * P:(4 * b + k + 1) * P]
                        else:
                            a = kk[:, t, k, :, :].rearrange("p c d -> p (c d)")
                        mm = pe.transpose(tp[:, n, k * P:(k + 1) * P], a, K.ident[:])
                    mm.then_inc(turned, 1)


def attend(nc, K, heads, scale, q_of, k_of, v_of, oT, far=None, side_of=None, panels=()):
    with stage(nc, K, "attend") as st:
        scores = st.ps("scores", [P, 2, T, S])
        turn = st.ps("turn", [P, 2, T, S])
        o = st.ps("o", [P, 2, HALF])
        biased = st.sb("biased", [P, 2, T, S]) if far is not None else None
        probs = st.sb("probs", [P, 2, T, S])
        probsT = st.sb("probsT", [P, 2, T, S])
        top, shift, total, inverse = (st.sb(n, [P, 2 * heads]) for n in ("top", "shift", "total", "inverse"))
        scored, bias_done, shift_done, exp_done, normed, turned, moved, pv_done, o_hi, o_moved, dve_own = map(
            st.sem, ("scored", "bias_done", "shift_done", "exp_done", "normed", "turned", "moved",
                     "pv_done", "o_hi", "o_moved", "dve_own"))
        side = side_of(st) if side_of else None
        with nc.Block(no_gpsimd_drain=True) as block:
            @block.sync
            def _(sp):
                if side:
                    side.sync(sp)
                start_panels(sp, K, panels)

            @block.gpsimd
            def _(pool):
                if side:
                    side.gpsimd(pool)

            @block.tensor
            def _(pe):
                if side:
                    side.tensor(pe)

                def score(h):
                    if h >= 2:
                        pe.wait_ge(bias_done if far is not None else exp_done,
                                   h - 1 if far is not None else T * (h - 1))
                    for t in range(T):
                        mm = pe.matmul(scores[:, h % 2, t, :], q_of(h)[:, t * P:(t + 1) * P], k_of(h),
                                       start=True, stop=True)
                    mm.then_inc(scored, 1)

                def transposes(h):
                    pe.wait_ge(normed, h + 1)
                    if h >= 2:
                        pe.wait_ge(moved, h - 1)
                    for t in range(T):
                        for k in range(T):
                            mm = pe.transpose(turn[:, h % 2, k, t * P:(t + 1) * P],
                                              probs[:, h % 2, t, k * P:(k + 1) * P], K.ident[:])
                    mm.then_inc(turned, 1)

                def weigh(h):
                    pe.wait_ge(moved, h + 1)
                    if h >= 4 and h % 2 == 0:
                        pe.wait_ge(o_moved, h // 2 - 1)
                    r = h % 2 * HD
                    for k in range(T):
                        mm = pe.matmul(o[r:r + HD, h // 2 % 2, 0:S], v_of(h, k), probsT[:, h % 2, k, :],
                                       start=k == 0, stop=k == T - 1)
                    mm.then_inc(pv_done, 1)

                for h in range(heads + 2):
                    if h < heads:
                        score(h)
                    if 1 <= h <= heads:
                        transposes(h - 1)
                    if h >= 2:
                        weigh(h - 2)

            @block.scalar
            def _(act):
                if side:
                    side.scalar(act)
                source = scores if far is None else biased

                def hi_of(pair):
                    act.wait_ge(pv_done, 2 * pair + 2)
                    act.activation(oT.hi[:, pair, :], o[:, pair % 2, 0:S], ACT.Copy).then_inc(o_hi, 1)

                for h in range(heads + 1):
                    if h < heads:
                        act.wait_ge(shift_done, h + 1)
                        if h >= 2:
                            act.wait_ge(turned, h - 1)
                        for t in range(T):
                            c = T * h + t
                            act.activation(probs[:, h % 2, t, :], source[:, h % 2, t, :], ACT.Exp,
                                           bias=shift[:, c:c + 1], scale=scale,
                                           accum_out=total[:, c:c + 1]).then_inc(exp_done, 1)
                    if h >= 1:
                        act.wait_ge(turned, h)
                        if h >= 3:
                            act.wait_ge(pv_done, h - 2)
                        act.activation(probsT[:, (h - 1) % 2, :, :], turn[:, (h - 1) % 2, :, :],
                                       ACT.Copy).then_inc(moved, 1)
                    if h >= 3 and h % 2 == 1:
                        hi_of(h // 2 - 1)
                hi_of(heads // 2 - 1)
                if side:
                    side.scalar_end(act)

            @block.vector
            def _(dve):
                own = Chain(dve, dve_own)

                def maximum(h):
                    dve.wait_ge(scored, h + 1)
                    a = scores[:, h % 2, :, :]
                    if far is not None:
                        if h >= 2:
                            dve.wait_ge(exp_done, T * (h - 1))
                        slope = 2.0 ** (-8.0 * (h + 1) / heads)
                        a = biased[:, h % 2, :, :]
                        dve.scalar_tensor_tensor(out=a, in0=far[:], scalar=slope / scale,
                                                 in1=scores[:, h % 2, :, :], op0=ALU.mult,
                                                 op1=ALU.add).then_inc(bias_done, 1)
                        dve.wait_ge(bias_done, h + 1)
                    c = slice(T * h, T * h + T)
                    own(dve.tensor_reduce(top[:, c], a, AX.X, ALU.max))
                    dve.tensor_scalar(shift[:, c], top[:, c], -scale, None, ALU.mult).then_inc(shift_done, 1)

                def normalise(h):
                    dve.wait_ge(exp_done, T * (h + 1))
                    c = slice(T * h, T * h + T)
                    own(dve.reciprocal(inverse[:, c], total[:, c]))
                    a = probs[:, h % 2, :, :]
                    dve.tensor_tensor(a, a, inverse[:, c].unsqueeze(2).to_broadcast([P, T, S]),
                                      ALU.mult).then_inc(normed, 1)

                def take(pair):
                    dve.wait_ge(o_hi, pair + 1)
                    rest_of(dve, oT.lo[:, pair, :], o[:, pair % 2, 0:S], oT.hi[:, pair, :]).then_inc(o_moved, 1)

                for h in range(heads + 3):
                    if h < heads:
                        maximum(h)
                    if 1 <= h <= heads:
                        normalise(h - 1)
                    if h >= 4 and h % 2 == 0:
                        take(h // 2 - 2)
                if side:
                    side.vector(dve)



def mlp(nc, K, hT, w_in, w_out, conditions, following=()):
    PAIRS = D_FF // HALF
    TURNS = PAIRS // 2
    CH = 8
    LAG = 2
    panels = take_panels(K, 2 * PAIRS)
    slot_in, slot_out = ([(panels[0] + 2 * g + o) % SLOTS for g in range(2)] for o in range(2))
    at_in, at_out = ([arrived(panels[0] + 2 * g + o) for g in range(2)] for o in range(2))
    assert K.loaded == panels[0] + SLOTS
    K.loaded = panels[0] + 2 * PAIRS
    csum, ccols, w_ada, b_ada = conditions
    HALVES = 2 * ADA // HALF
    STEPS = KC // 2
    with stage(nc, K, "mlp") as st:
        acc = st.ps("acc", [P, T, 2, HALF])
        hid = st.ps("hid", [P, 2, HALF])
        first_w, second_w = (Parts(st.mem, nc, f"{st.name}_{n}", [P, 2, PIECE]) for n in ("in", "out"))
        relu, act2 = (st.sb(n, [P, 2, S]) for n in ("relu", "act2"))
        hidden = Parts(st.mem, nc, f"{st.name}_hidden", [P, 4, S])
        ada_half = st.sb("ada_half", [P, 2, KC // 2, HALF])
        ada_in = [st.pool_sem(f"ada_in{n}") for n in range(2)]
        biased = st.pool_sem("biased")
        (hid_full, relu_done, act2_done, in_hi, in_split, out_hi, out_split, hidden_hi, hidden_split, act_used,
         summed, cleared, dve_own) = map(
            st.sem, ("hid_full", "relu_done", "act2_done", "in_hi", "in_split", "out_hi", "out_split", "hidden_hi",
                     "hidden_split", "act_used", "summed", "cleared", "dve_own"))

        def src_in(n):
            return w_in.rearrange("(k p) n -> p k n", p=P)[:, :, bass.ds(n * HALF, HALF)]

        def src_out(n):
            return w_out[bass.ds(n * HALF, HALF), :].rearrange("(k p) n -> p k n", p=P)

        def raw_in(g, m):
            return ring_view(K, slot_in[g])[:, :, m * P:(m + 1) * P]

        def raw_out(g, m):
            return ring_view(K, slot_out[g], 4)[:, m, :]

        def by_row(a):
            return a.rearrange("p (k n) -> p k n", k=KC)

        with nc.Block(no_gpsimd_drain=True) as block:
            @block.sync
            def _(sp):
                with sp.Fori(0, TURNS - 1) as i:
                    for g in range(2):
                        sp.wait_ge(in_split, i * CH + 4 * (g + 1))
                        sp.dma_start(ring_view(K, slot_in[g]), src_in(2 * i + 2 + g)
                                     ).then_inc(K.ring_in[slot_in[g]], 16)
                        sp.wait_ge(out_split, i * CH + 4 * (g + 1))
                        sp.dma_start(ring_view(K, slot_out[g], 4), src_out(2 * i + 2 + g)
                                     ).then_inc(K.ring_in[slot_out[g]], 16)
                for n, panel in enumerate(following):
                    sp.wait_ge((in_split, out_split)[n % 2], (TURNS - 1) * CH + 4 * (n // 2 + 1))
                    start_panels(sp, K, [panel], in_split, K.loaded)

            @block.gpsimd
            def _(pool):
                def load(n, slot):
                    src = w_ada.rearrange("(a k p) n -> p a k n", a=2, p=P)[:, slot, :, bass.ds(n * HALF, HALF)]
                    pool.dma_start(ada_half[:, slot, :, :], src).then_inc(ada_in[slot], 16)

                pool.wait_ge(cleared, 1)
                pool.dma_start(csum[0:1, :], b_ada).then_inc(biased, 16)
                for slot in range(2):
                    load(0, slot)
                with pool.Fori(1, HALVES // 2) as j:
                    for slot in range(2):
                        pool.wait_ge(summed, STEPS * (2 * j + (slot - 1)))
                        load(j, slot)

            @block.tensor
            def _(pe):
                for t in range(T):
                    for b in range(2):
                        pe.matmul(acc[:, t, b, :], K.ident[:], K.x[:, t, b * HALF:(b + 1) * HALF],
                                  start=True, stop=False, skip_group_check=True)
                pe.sem_inc(act_used, LAG)

                with pe.Fori(0, TURNS) as i:
                    def first(c):
                        if c >= 2:
                            pe.wait_ge(relu_done, i * CH + c - 1)
                        pe.wait_ge(in_split, i * CH + c + 1)
                        for k in range(KC):
                            mm = three_passes(pe, hid[:, c % 2, 0:S], first_w, hT,
                                              lambda x: x[:, c % 2, k * P:(k + 1) * P], lambda x: x[:, k, :],
                                              start=k == 0, stop=k == KC - 1)
                        mm.then_inc(hid_full, 1)

                    def second(c):
                        pe.wait_ge(hidden_split, i * CH + c + 1)
                        pe.wait_ge(out_split, i * CH + c + 1)
                        for t in range(T):
                            for b in range(2):
                                mm = three_passes(pe, acc[:, t, b, :], hidden, second_w,
                                                  lambda x: x[:, c % 4, t * P:(t + 1) * P],
                                                  lambda x: x[:, c % 2, b * HALF:(b + 1) * HALF],
                                                  start=False, stop=False, skip_group_check=True)
                        mm.then_inc(act_used, 1)

                    for c in range(CH + LAG):
                        if c < CH:
                            first(c)
                        if c >= LAG:
                            second(c - LAG)

            @block.scalar
            def _(act):
                with act.Fori(0, TURNS) as i:
                    def first(c):
                        g, m = c // 4, c % 4
                        if m == 0:
                            act.wait_ge(K.ring_in[slot_in[g]], 16 * i + at_in[g])
                        if c >= 2:
                            act.wait_ge(hid_full, i * CH + c - 1)
                        act.activation(by_row(first_w.hi[:, c % 2, :]), raw_in(g, m),
                                       ACT.Copy).then_inc(in_hi, 1)

                    def rectify(c):
                        act.wait_ge(hid_full, i * CH + c + 1)
                        act.activation(relu[:, c % 2, :], hid[:, c % 2, 0:S], ACT.Relu).then_inc(relu_done, 1)

                    def second(c):
                        g, m = c // 4, c % 4
                        if m == 0:
                            act.wait_ge(K.ring_in[slot_out[g]], 16 * i + at_out[g])
                        act.wait_ge(act_used, i * CH + (c + 1 - 2 + LAG))
                        act.activation(second_w.hi[:, c % 2, :], raw_out(g, m), ACT.Copy).then_inc(out_hi, 1)
                        act.wait_ge(act2_done, i * CH + c + 1)
                        act.activation(hidden.hi[:, c % 4, :], act2[:, c % 2, :],
                                       ACT.Copy).then_inc(hidden_hi, 1)

                    for c in range(CH + LAG):
                        if c >= LAG:
                            rectify(c - LAG)
                        if c < CH:
                            first(c)
                        if c >= LAG:
                            second(c - LAG)

            @block.vector
            def _(dve):
                own = Chain(dve, dve_own)
                dve.memset(csum[:], 0.0).then_inc(cleared, 1)
                dve.wait_ge(biased, 16)
                with dve.Fori(0, TURNS) as i:
                    def first(c):
                        dve.wait_ge(in_hi, i * CH + c + 1)
                        rest_of(dve, by_row(first_w.lo[:, c % 2, :]), raw_in(c // 4, c % 4),
                                by_row(first_w.hi[:, c % 2, :])).then_inc(in_split, 1)

                    def square(c):
                        dve.wait_ge(relu_done, i * CH + c + 1)
                        a = relu[:, c % 2, :]
                        dve.tensor_tensor(act2[:, c % 2, :], a, a, ALU.mult).then_inc(act2_done, 1)

                    def second(c):
                        dve.wait_ge(out_hi, i * CH + c + 1)
                        rest_of(dve, second_w.lo[:, c % 2, :], raw_out(c // 4, c % 4),
                                second_w.hi[:, c % 2, :]).then_inc(out_split, 1)
                        dve.wait_ge(hidden_hi, i * CH + c + 1)
                        rest_of(dve, hidden.lo[:, c % 4, :], act2[:, c % 2, :],
                                hidden.hi[:, c % 4, :]).then_inc(hidden_split, 1)

                    def condition(step):
                        half, k = step // STEPS, step % STEPS
                        slot = half % 2
                        if k == 0:
                            dve.wait_ge(ada_in[slot], 48 * i + 16 * (half // 2 + 1))
                        if step:
                            dve.wait_ge(summed, 24 * i + step)
                        to = csum[:, bass.ds(3 * HALF * i + half // 2 * HALF, HALF)]
                        row = slot * STEPS + k
                        dve.scalar_tensor_tensor(out=to, in0=ada_half[:, slot, k, :],
                                                 scalar=ccols[:, row:row + 1], in1=to,
                                                 op0=ALU.mult, op1=ALU.add).then_inc(summed, 1)

                    for c in range(CH + LAG):
                        if c >= LAG:
                            square(c - LAG)
                        if c < CH:
                            condition(3 * c)
                            first(c)
                            condition(3 * c + 1)
                        if c >= LAG:
                            second(c - LAG)
                        if c < CH:
                            condition(3 * c + 2)
                    dve.wait_ge(summed, 24 * i + 24)
                dve.wait_ge(act_used, CH * TURNS + LAG)
                for t in range(T):
                    own(dve.tensor_copy(K.x[:, t, :], acc[:, t, :, :].rearrange("p b n -> p (b n)")))


def spread(nc, K, csum):
    n_banks = LAYERS * ADA // HALF
    with stage(nc, K, "spread") as st:
        ps = st.ps("ps", [P, 4, HALF])
        summed, moved = map(st.sem, ("summed", "moved"))
        with nc.Block(no_gpsimd_drain=True) as block:
            @block.tensor
            def _(pe):
                for n in range(n_banks):
                    if n >= 4:
                        pe.wait_ge(moved, n - 3)
                    pe.matmul(ps[:, n % 4, :], K.ones[:], csum[:, n * HALF:(n + 1) * HALF],
                              start=True, stop=True).then_inc(summed, 1)

            @block.scalar
            def _(act):
                for n in range(n_banks):
                    act.wait_ge(summed, n + 1)
                    act.activation(csum[:, n * HALF:(n + 1) * HALF], ps[:, n % 4, :],
                                   ACT.Copy).then_inc(moved, 1)



def gla_gates(nc, K, A, hT, logg):
    with stage(nc, K, "gla_gates") as st:
        wz = st.sb("wz", [P, KC, 2 * RANK])
        up = st.sb("up", [2 * RANK + 1, 2, HALF])
        zT = st.sb("zT", [2 * RANK + 1, S])
        size, e, ln = (st.sb(n, [P, 4, HALF]) for n in ("size", "e", "ln"))
        zps = st.ps("zps", [P, HALF])
        logit = st.ps("logit", [P, 4, HALF])
        loaded, cleared, up_loaded, z_done, z_moved, logit_done, act_own, ln_done, logg_done, dve_own = map(
            st.sem, ("loaded", "cleared", "up_loaded", "z_done", "z_moved", "logit_done", "act_own",
                     "ln_done", "logg_done", "dve_own"))
        z0 = 2 * GLA_H * GLA_DK + 2 * GLA_H * GLA_DV
        with nc.Block(no_gpsimd_drain=True) as block:
            @block.sync
            def _(sp):
                sp.dma_start(wz[:], A.gla_w_in[0][:, z0:z0 + 2 * RANK].rearrange("(k p) n -> p k n", p=P)
                             ).then_inc(loaded, 16)
                sp.wait_ge(cleared, 1)
                for r in range(2):
                    sp.dma_start(up[RANK * r:RANK * (r + 1), r, :], A.gla_w_gate_up[0][r]).then_inc(up_loaded, 16)
                sp.dma_start(up[2 * RANK:2 * RANK + 1, :, :], A.gla_b_gate).then_inc(up_loaded, 16)

            @block.tensor
            def _(pe):
                pe.wait_ge(loaded, 16)
                for k in range(KC):
                    for part in (hT.hi, hT.lo):
                        mm = pe.matmul(zps[0:2 * RANK, 0:S], wz[:, k, :], part[:, k, :].bitcast(F32),
                                       start=k == 0 and part is hT.hi, stop=k == KC - 1 and part is hT.lo)
                mm.then_inc(z_done, 1)
                pe.wait_ge(up_loaded, 16 * 3)
                pe.wait_ge(z_moved, 2)
                for n in range(4):
                    t, r = n // 2, n % 2
                    pe.matmul(logit[:, n, :], zT[:, t * P:(t + 1) * P], up[:, r, :], start=True,
                              stop=True).then_inc(logit_done, 1)

            @block.vector
            def _(dve):
                own = Chain(dve, dve_own)
                dve.memset(up[:], 0.0).then_inc(cleared, 1)
                dve.memset(zT[2 * RANK:2 * RANK + 1, :], 1.0).then_inc(z_moved, 1)
                dve.wait_ge(z_done, 1)
                dve.tensor_copy(zT[0:2 * RANK, :], zps[0:2 * RANK, 0:S]).then_inc(z_moved, 1)
                for n in range(4):
                    dve.wait_ge(ln_done, n + 1)
                    own(dve.scalar_tensor_tensor(out=logg[:, n // 2, n % 2, :], in0=logit[:, n, :], scalar=0.0,
                                                 in1=ln[:, n, :], op0=ALU.min, op1=ALU.subtract))

            @block.scalar
            def _(act):
                own = Chain(act, act_own)
                for n in range(4):
                    act.wait_ge(logit_done, n + 1)
                    own(act.activation(size[:, n, :], logit[:, n, :], ACT.Abs))
                for n in range(4):
                    own(act.activation(e[:, n, :], size[:, n, :], ACT.Exp, scale=-1.0))
                for n in range(4):
                    act.activation(ln[:, n, :], e[:, n, :], ACT.Ln, bias=1.0).then_inc(ln_done, 1)


def gla_scan(nc, K, q, k, v, logg, o):
    empty = [(K.loaded + n) % SLOTS for n in range(2)]
    assert K.loaded - K.used <= SLOTS - 2
    with stage(nc, K, "gla_scan") as st:
        tri = st.sb("tri", [P, 4, P])
        which = st.sb("which", [P, 2])
        eb, enb = (K.ring[:, empty[0], a:a + 2 * HALF].rearrange("p (s n) -> p s n", s=2) for a in (0, 2 * HALF))
        ed = st.sb("ed", [P, 2, HALF])
        qe, ke = (st.sb(n, [P, 2, HALF]) for n in ("qe", "ke"))
        kd = K.ring[:, empty[0], 4 * HALF:8 * HALF].rearrange("p (r t n) -> p r t n", r=2, t=T)
        qeT, keT = (st.sb(n, [P, 2, GLA_H, S]) for n in ("qeT", "keT"))
        decay = st.sb("decay", [P, 2, GLA_H, N_CHUNKS])
        aT = st.sb("aT", [P, 2, 2 * T, P])
        state = K.ring[:, empty[1], 0:12 * GLA_DV].rearrange("p (s r i n) -> p s r i n", s=2, r=2, i=3)
        wide = st.ps("wide", [P, 8, HALF])
        sums, turn = wide[:, 0:4, :], wide[:, 4:8, :]
        made, decayed, summed, exped, gated, turned, moved, pool_own, dve_own = map(
            st.sem, ("made", "decayed", "summed", "exped", "gated", "turned", "moved", "pool_own", "dve_own"))
        inner, masked, outer, stated, o_done, o_moved, kd_done = map(
            st.sem, ("inner", "masked", "outer", "stated", "o_done", "o_moved", "kd_done"))
        steps = [(r, t) for r in range(2) for t in range(T)]
        order = ((0, 1, 2), (3, 2, 1))
        place = {(0, 0): (2, 0), (0, 2): (2, S), (1, 1): (3, 0), (0, 1): (4, 0), (1, 0): (4, S), (1, 2): (7, 0)}

        def update(r, i):
            bank, column = place[r, i]
            return wide[:, bank, column:column + S]

        with nc.Block(no_gpsimd_drain=True) as block:
            @block.gpsimd
            def _(pool):
                own = Chain(pool, pool_own)
                own(pool.memset(tri[:], 1.0 / 16.0))
                own(pool.memset(which[:], 1.0 / 16.0))

                def keep(a, where, base, mult, step, op):
                    own(pool.affine_select(out=a, in_=a, compare_op=op, fill=0.0, base=base,
                                           pattern=[[step, where]], channel_multiplier=mult))

                keep(tri[:, 0, :], P, 0, -1, 1, ALU.is_ge)
                keep(tri[:, 1, :], P, 0, 1, -1, ALU.is_gt)
                keep(tri[:, 2, :], P, 0, 1, -1, ALU.is_ge)
                keep(tri[:, 3, :], P, 0, -1, 1, ALU.is_gt)
                for m in range(4):
                    own(pool.affine_select(out=tri[:, m, CHUNK:P], in_=tri[:, m, CHUNK:P],
                                           compare_op=ALU.is_ge, fill=0.0, base=-CHUNK,
                                           pattern=[[0, CHUNK]], channel_multiplier=1))
                    own(pool.affine_select(out=tri[:, m, 0:CHUNK], in_=tri[:, m, 0:CHUNK],
                                           compare_op=ALU.is_gt, fill=0.0, base=CHUNK,
                                           pattern=[[0, CHUNK]], channel_multiplier=-1))
                own(pool.affine_select(out=which[:, 1:2], in_=which[:, 1:2], compare_op=ALU.is_ge, fill=0.0,
                                       base=-CHUNK, pattern=[[0, 1]], channel_multiplier=1))
                own(pool.affine_select(out=which[:, 0:1], in_=which[:, 0:1], compare_op=ALU.is_gt, fill=0.0,
                                       base=CHUNK, pattern=[[0, 1]], channel_multiplier=-1))
                pool.memset(aT[:], 0.0).then_inc(made, 1)

            @block.tensor
            def _(pe):
                pe.wait_ge(made, 1)
                for r in range(2):
                    for h in range(GLA_H):
                        for t in range(T):
                            c = (r * GLA_H + h) * N_CHUNKS + 2 * t
                            mm = pe.matmul(turn[:, 3, c:c + 2], logg[:, t, r, h * P:(h + 1) * P], which[:],
                                           start=True, stop=True)
                mm.then_inc(decayed, 1)

                def sum_up(n):
                    r, t = steps[n]
                    if n >= 2:
                        pe.wait_ge(exped, 3 * (n - 1))
                    for m in range(2):
                        mm = pe.matmul(sums[:, n % 2 * 2 + m, :], tri[:, 2 * r + m, :], logg[:, t, r, :],
                                       start=True, stop=True)
                    mm.then_inc(summed, 1)

                def transposes(n):
                    pe.wait_ge(gated, 2 * n + 2)
                    for m, a in enumerate((qe, ke)):
                        u = 2 * n + m
                        if u >= 3:
                            pe.wait_ge(moved, u - 2)
                        for h in range(GLA_H):
                            mm = pe.transpose(turn[:, u % 3, h * P:(h + 1) * P],
                                              a[:, n % 2, h * P:(h + 1) * P], K.ident[:])
                        mm.then_inc(turned, 1)

                sum_up(0)
                for n in range(4):
                    if n + 1 < 4:
                        sum_up(n + 1)
                    transposes(n)

                def within(h):
                    if h >= 2:
                        pe.wait_ge(masked, h - 1)
                    for n, (r, t) in enumerate(steps):
                        mm = pe.matmul(wide[:, h % 2, n * P:(n + 1) * P], keT[:, r, h, t * P:(t + 1) * P],
                                       qeT[:, r, h, t * P:(t + 1) * P], start=True, stop=True)
                    mm.then_inc(inner, 1)

                def between(h):
                    if h >= 1:
                        pe.wait_ge(stated, 6 * h)
                    for r in range(2):
                        for i, n in enumerate(order[r]):
                            a = n % 2 * CHUNK
                            mm = pe.matmul(update(r, i),
                                           kd[a:a + CHUNK, r, n // 2, h * P:(h + 1) * P],
                                           v[a:a + CHUNK, n // 2, h * S:(h + 1) * S], start=True, stop=True)
                    mm.then_inc(outer, 1)

                def output(h):
                    pe.wait_ge(masked, h + 1)
                    pe.wait_ge(stated, 6 * (h + 1))
                    if h >= 2:
                        pe.wait_ge(o_moved, h - 1)
                    for t in range(T):
                        to = wide[:, 5 + h % 2, t * S:(t + 1) * S]
                        for r in range(2):
                            pe.matmul(to, aT[:, h % 2, 2 * r + t, :], v[:, t, h * S:(h + 1) * S],
                                      start=r == 0, stop=False, skip_group_check=True)
                        for c in range(2):
                            n = 2 * t + c
                            for r in range(2):
                                if n == (0, N_CHUNKS - 1)[r]:
                                    continue
                                i = n - 1 if r == 0 else N_CHUNKS - 2 - n
                                mm = pe.matmul(wide[c * CHUNK:(c + 1) * CHUNK, 5 + h % 2, t * S:(t + 1) * S],
                                               qeT[:, r, h, n * CHUNK:(n + 1) * CHUNK],
                                               state[:, h % 2, r, i, :], start=False, stop=True,
                                               skip_group_check=True)
                    mm.then_inc(o_done, 1)

                pe.wait_ge(moved, 8)
                pe.wait_ge(exped, 13)
                pe.wait_ge(kd_done, 4)
                for h in range(GLA_H + 1):
                    if h < GLA_H:
                        within(h)
                        between(h)
                    if h >= 1:
                        output(h - 1)

            @block.scalar
            def _(act):
                act.wait_ge(decayed, 1)
                act.activation(decay[:].rearrange("p r h n -> p (r h n)"), turn[:, 3, 0:2 * GLA_H * N_CHUNKS],
                               ACT.Exp).then_inc(exped, 1)
                for n, (r, t) in enumerate(steps):
                    act.wait_ge(summed, n + 1)
                    if n >= 2:
                        act.wait_ge(gated, 2 * (n - 1))
                        act.wait_ge(kd_done, n - 1)
                    s = n % 2
                    act.activation(eb[:, s, :], sums[:, 2 * s, :], ACT.Exp).then_inc(exped, 1)
                    act.activation(enb[:, s, :], sums[:, 2 * s, :], ACT.Exp, scale=-1.0).then_inc(exped, 1)
                    act.activation(ed[:, s, :], sums[:, 2 * s + 1, :], ACT.Exp).then_inc(exped, 1)
                    for m, to in enumerate((qeT, keT)):
                        u = 2 * n + m
                        act.wait_ge(turned, u + 1)
                        act.activation(to[:, r, :, t * P:(t + 1) * P],
                                       turn[:, u % 3, :].rearrange("p (h n) -> p h n", h=GLA_H),
                                       ACT.Copy).then_inc(moved, 1)
                for h in range(GLA_H):
                    act.wait_ge(o_done, h + 1)
                    act.activation(o[:, :, h, :], wide[:, 5 + h % 2, :].rearrange("p (t n) -> p t n", t=T),
                                   ACT.Copy).then_inc(o_moved, 1)

            @block.vector
            def _(dve):
                own = Chain(dve, dve_own)
                for n, (r, t) in enumerate(steps):
                    dve.wait_ge(exped, 1 + 3 * (n + 1))
                    if n >= 2:
                        dve.wait_ge(turned, 2 * (n - 1))
                    s = n % 2
                    dve.tensor_tensor(qe[:, s, :], q[:, t, :], eb[:, s, :], ALU.mult).then_inc(gated, 1)
                    dve.tensor_tensor(ke[:, s, :], k[:, t, :], enb[:, s, :], ALU.mult).then_inc(gated, 1)
                    dve.tensor_tensor(kd[:, r, t, :], k[:, t, :], ed[:, s, :], ALU.mult).then_inc(kd_done, 1)
                dve.wait_ge(made, 1)
                for h in range(GLA_H):
                    dve.wait_ge(inner, h + 1)
                    if h >= 2:
                        dve.wait_ge(o_done, h - 1)
                    for r in range(2):
                        mask = tri[:, 2 * r:2 * r + 1, :].bitcast(U32).to_broadcast([P, T, P])
                        ins = dve.copy_predicated(
                            aT[:, h % 2, 2 * r:2 * r + 2, :], mask,
                            wide[:, h % 2, 2 * r * P:2 * (r + 1) * P].rearrange("p (t n) -> p t n", t=T))
                        if r == 0:
                            own(ins)
                    ins.then_inc(masked, 1)
                    dve.wait_ge(outer, h + 1)
                    for r in range(2):
                        for i, n in enumerate(order[r]):
                            u = 3 * r + i
                            chunk = update(r, i)
                            to = state[:, h % 2, r, i, :]
                            if i == 0:
                                dve.tensor_copy(to, chunk).then_inc(stated, 1)
                            else:
                                dve.wait_ge(stated, 6 * h + u)
                                dve.scalar_tensor_tensor(out=to, in0=state[:, h % 2, r, i - 1, :],
                                                         scalar=decay[:, r, h, n:n + 1], in1=chunk,
                                                         op0=ALU.mult, op1=ALU.add).then_inc(stated, 1)


def gla_out(nc, K, A, o, gate, oT, panels):
    with stage(nc, K, "gla_out") as st:
        gain = st.sb("gain", [P, GLA_DV])
        squares = st.sb("squares", [P, T, D])
        ms, std, rstd = (st.sb(n, [P, T * GLA_H]) for n in ("ms", "std", "rstd"))
        tp = st.ps("tp", [P, 2 * T, HALF])
        loaded, squared, ms_done, std_done, gated, turned, hi_done, dve_own = map(
            st.sem, ("loaded", "squared", "ms_done", "std_done", "gated", "turned", "hi_done", "dve_own"))

        def halves(a, n):
            t, h = n // 2, n % 2
            return a[:, 4 * h:4 * h + 4, t * P:(t + 1) * P]

        def bank(n):
            return tp[:, n, :].rearrange("p (k n) -> p k n", k=4)

        with nc.Block(no_gpsimd_drain=True) as block:
            @block.sync
            def _(sp):
                sp.dma_start(gain[:], A.gla_out_norm[0:1, :].partition_broadcast(P)).then_inc(loaded, 16)
                start_panels(sp, K, panels)

            @block.scalar
            def _(act):
                act.activation(squares[:].rearrange("p t (h d) -> p t h d", h=GLA_H), o[:],
                               ACT.Square).then_inc(squared, 1)
                act.wait_ge(ms_done, 1)
                act.activation(std[:], ms[:], ACT.Sqrt).then_inc(std_done, 1)
                for n in range(2 * T):
                    act.wait_ge(turned, n + 1)
                    act.activation(halves(oT.hi, n), bank(n), ACT.Copy).then_inc(hi_done, 1)

            @block.vector
            def _(dve):
                own = Chain(dve, dve_own)
                dve.wait_ge(squared, 1)
                own(dve.tensor_reduce(ms[:], squares[:].rearrange("p t (h d) -> p (t h) d", h=GLA_H), AX.X,
                                      ALU.add))
                dve.tensor_scalar(ms[:], ms[:], 1.0 / GLA_DV, EPS, ALU.mult, ALU.add).then_inc(ms_done, 1)
                dve.wait_ge(loaded, 16)
                g = gate.rearrange("p t (h d) -> p t h d", h=GLA_H)
                for t in range(T):
                    own(dve.tensor_tensor(g[:, t], g[:, t], gain[:].unsqueeze(1).to_broadcast([P, GLA_H, GLA_DV]),
                                          ALU.mult))
                dve.wait_ge(std_done, 1)
                own(dve.reciprocal(rstd[:], std[:]))
                for t in range(T):
                    r = rstd[:, t * GLA_H:(t + 1) * GLA_H].unsqueeze(2).to_broadcast([P, GLA_H, GLA_DV])
                    own(dve.tensor_tensor(o[:, t], o[:, t], r, ALU.mult))
                    dve.tensor_tensor(o[:, t], o[:, t], g[:, t], ALU.mult).then_inc(gated, 1)
                for n in range(2 * T):
                    dve.wait_ge(hi_done, n + 1)
                    rest_of(dve, halves(oT.lo, n), bank(n), halves(oT.hi, n))

            @block.tensor
            def _(pe):
                for n in range(2 * T):
                    t, h = n // 2, n % 2
                    pe.wait_ge(gated, t + 1)
                    for k in range(4):
                        f = 4 * h + k
                        mm = pe.transpose(tp[:, n, k * P:(k + 1) * P], o[:, t, f // 2, f % 2 * P:(f % 2 + 1) * P],
                                          K.ident[:])
                    mm.then_inc(turned, 1)


def residual(nc, K, lhs, scale=None, following=()):
    panels = take_panels(K, 2)
    with stage(nc, K, "residual") as st:
        w = Parts(st.mem, nc, st.name, [P, PIECES, PIECE])
        ps = st.ps("ps", [P, 4, HALF])
        scaled = st.sb("scaled", [P, 2, HALF]) if scale is not None else None
        hi_done, split_done, piece_used, dve_own = map(
            st.sem, ("hi_done", "split_done", "piece_used", "dve_own"))
        with nc.Block(no_gpsimd_drain=True) as block:
            @block.sync
            def _(sp):
                start_panels(sp, K, following, split_done, panels[0])

            @block.tensor
            def _(pe):
                for n in range(2):
                    for c in range(4):
                        piece = 4 * n + c
                        a = piece % PIECES
                        pe.wait_ge(split_done, piece + 1)
                        for kk in range(2):
                            k = 2 * c + kk
                            for t in range(T):
                                mm = three_passes(pe, ps[:, 2 * n + t, :], lhs, w,
                                                  lambda x: x[:, k, t * P:(t + 1) * P],
                                                  lambda x: x[:, a, kk * HALF:(kk + 1) * HALF],
                                                  start=k == 0, stop=k == KC - 1)
                        mm.then_inc(piece_used, 1)

            @block.scalar
            def _(act):
                for n, i in enumerate(panels):
                    for c in range(4):
                        split_piece(act, K, w, i, c, 4 * n + c, piece_used, hi_done)

            @block.vector
            def _(dve):
                own = Chain(dve, dve_own)

                def add(n):
                    dve.wait_ge(piece_used, 4 * n + 4)
                    for t in range(T):
                        x = K.x[:, t, n * HALF:(n + 1) * HALF]
                        y = ps[:, 2 * n + t, :]
                        if scale is not None:
                            own(dve.tensor_tensor(scaled[:, t, :], y, scale(n), ALU.mult))
                            y = scaled[:, t, :]
                        own(dve.tensor_tensor(x, x, y, ALU.add))

                for n, i in enumerate(panels):
                    for c in range(4):
                        rest_of_piece(dve, K, w, i, c, 4 * n + c, hi_done, split_done)
                        if n == 1 and c == 2:
                            add(0)
                add(1)


def block_one(nc, K, A, ada):
    gains = A.norm_mix, A.norm_mlp

    def gain(kind, layer):
        return gains[kind][layer:layer + 1, :]

    def wide(w, panels):
        return [(columns(w, n), KC) for n in panels]

    def pairs(layer, numbers):
        w_in, w_out = A.mlp_w_in[layer], A.mlp_w_out[layer]
        return [panel for n in numbers
                for panel in ((columns(w_in, n), KC),
                              (w_out[n * HALF:(n + 1) * HALF, :].rearrange("(k p) n -> p k n", p=P), 4))]

    def conditions(layer):
        return (ada[:, layer * ADA:(layer + 1) * ADA], K.c_cols, A.w_ada_2[layer], A.b_ada_2[layer:layer + 1, :])

    w_qkv, w_o, w_gla = A.attn_w_qkv[0], A.attn_w_o[0], A.gla_w_in[0]
    begin_ring(nc, K)
    setup(nc, K, A, [])
    with ExitStack() as mem:
        def sb(name, shape):
            return mem.enter_context(nc.sbuf_tensor(name, shape, F32))

        hT = Parts(mem, nc, "attn_hT", [P, KC, S])
        norm(nc, K, gain(0, 0), hT=hT, panels=wide(w_qkv, range(3)) + wide(w_o, range(1)))
        qkv = sb("qkv", [P, T, (QK_HEADS + N_KV) * HD])
        qT = sb("qT", [P, N_HEADS // 2, S])
        kT = sb("kT", [P, N_KV, S])
        project(nc, K, hT, ["tokens"] * 3,
                lambda act, n, t, ps: act.activation(qkv[:, t, n * HALF:(n + 1) * HALF], ps, ACT.Copy),
                following=wide(w_o, range(1, 2)) + pairs(0, range(1)))
        rope(nc, K, qkv, qT, kT, A)
        v0 = QK_HEADS * HD
        attend(nc, K, N_HEADS, HD ** -0.5,
               lambda h: qT[h % 2 * HD:h % 2 * HD + HD, h // 2, :],
               lambda h: kT[h % 2 * HD:h % 2 * HD + HD, h // (N_HEADS // N_KV), :],
               lambda h, k: qkv[:, k, v0 + h // (N_HEADS // N_KV) * HD:v0 + (h // (N_HEADS // N_KV) + 1) * HD],
               hT)
        residual(nc, K, hT, following=pairs(0, range(1, 2)))
    with ExitStack() as mem:
        hT = Parts(mem, nc, "mlp0_hT", [P, KC, S])
        norm(nc, K, gain(1, 0), hT=hT)
        mlp(nc, K, hT, A.mlp_w_in[0], A.mlp_w_out[0], conditions(0), following=wide(w_gla, range(SLOTS)))
    with ExitStack() as mem:
        def sb(name, shape):
            return mem.enter_context(nc.sbuf_tensor(name, shape, F32))

        q, k = (sb(n, [P, T, HALF]) for n in ("q", "k"))
        v, gate = (sb(n, [P, T, D]) for n in ("v", "gate"))
        logg = sb("logg", [P, T, 2, HALF])

        def evacuate(act, n, t, ps):
            if n == 0:
                return act.activation(q[:, t, :], ps, ACT.Copy, scale=GLA_DK ** -0.5)
            if n == 1:
                return act.activation(k[:, t, :], ps, ACT.Copy)
            to, c = (v, n - 2) if n < 4 else (gate, n - 4)
            return act.activation(to[:, t, c * HALF:(c + 1) * HALF], ps, ACT.Copy if n < 4 else ACT.Silu)

        with ExitStack() as inner:
            hT = Parts(inner, nc, "gla_hT", [P, KC, S])
            norm(nc, K, gain(0, 1), hT=hT)
            project(nc, K, hT, ["tokens"] * 6, evacuate, own_panels=wide(w_gla, range(SLOTS, 6)),
                    following=wide(A.gla_w_o[0], range(2)))
            gla_gates(nc, K, A, hT, logg)
        o = logg[:].rearrange("p t r n -> p (t r n)").rearrange("p (t h d) -> p t h d", t=T, h=GLA_H)
        gla_scan(nc, K, q, k, v, logg, o)
        oT = Parts(mem, nc, "oT", [P, KC, S])
        gla_out(nc, K, A, o, gate[:], oT, pairs(1, range(1)))
        residual(nc, K, oT, following=pairs(1, range(1, 2)))
    with ExitStack() as mem:
        hT = Parts(mem, nc, "mlp1_hT", [P, KC, S])
        norm(nc, K, gain(1, 1), hT=hT)
        mlp(nc, K, hT, A.mlp_w_in[1], A.mlp_w_out[1], conditions(1))
    spread(nc, K, ada)
    norm(nc, K, A.final_norm.rearrange("(a n) -> a n", a=1), keep=K.x)




def tables(nc, K):
    with stage(nc, K, "tables") as st:
        whole = st.sb("whole", [P, T, S], mybir.dt.int32)
        few = st.sb("few", [P, TOPK], mybir.dt.int32)
        (own_sem,) = map(st.sem, ("own_sem",))
        with nc.Block(no_gpsimd_drain=True) as block:
            @block.gpsimd
            def _(pool):
                own = Chain(pool, own_sem)
                own(pool.iota(whole[:], pattern=[[-P, T], [1, S]], base=0, channel_multiplier=-1))
                own(pool.tensor_copy(K.far[:], whole[:]))
                own(pool.affine_select(out=K.far[:], in_=K.far[:], compare_op=ALU.is_ge, fill=MASKED, base=0,
                                       pattern=[[P, T], [-1, S]], channel_multiplier=1))
                own(pool.iota(few[:], pattern=[[1, TOPK]], base=0, channel_multiplier=0))
                own(pool.tensor_copy(K.places[:], few[:]))
                own(pool.memset(K.zeros[:], 0.0))


class Convolution:

    def __init__(self, st, K, conv_w, b, c, h, hi, lo):
        self.K, self.conv_w, self.b, self.c, self.h, self.hi, self.lo = K, conv_w, b, c, h, hi, lo
        self.rows = st.sb("conv_rows", [CONV_K * 4, P])
        self.w = st.sb("conv_cols", [P, CONV_K, 4])
        self.turned = st.ps("conv_turn", [P, HALF])
        self.z, self.part = (st.sb(n, [P, 4, S]) for n in ("conv_z", "conv_part"))
        self.loaded, self.cols_done, self.cols_moved, self.done, self.hi_done, self.own_sem = map(
            st.sem, ("conv_loaded", "conv_cols_done", "conv_cols_moved", "conv_done", "conv_hi_done",
                     "conv_own"))

    def sync(self, sp):
        sp.dma_start(self.rows[:], self.conv_w).then_inc(self.loaded, 16)

    def tensor(self, pe):
        pe.wait_ge(self.loaded, 16)
        pe.transpose(self.turned[:, 0:12], self.rows[:], self.K.ident[0:12, 0:12]).then_inc(self.cols_done, 1)

    def scalar(self, act):
        act.wait_ge(self.cols_done, 1)
        act.activation(self.w[:].rearrange("p k c -> p (k c)"), self.turned[:, 0:12],
                       ACT.Copy).then_inc(self.cols_moved, 1)

    def gpsimd(self, pool):
        own = Chain(pool, self.own_sem)
        own(pool.tensor_tensor(self.z[:], self.c[:], self.h[:], ALU.mult))
        pool.wait_ge(self.cols_moved, 1)

        def weight(k, n):
            return self.w[:, k, :].unsqueeze(2).to_broadcast([P, 4, n])

        y = self.c
        own(pool.tensor_tensor(y[:], self.z[:], weight(2, S), ALU.mult))
        for back in (1, 2):
            n = S - back
            own(pool.tensor_tensor(self.part[:, :, 0:n], self.z[:, :, 0:n], weight(2 - back, n), ALU.mult))
            own(pool.tensor_tensor(y[:, :, back:S], y[:, :, back:S], self.part[:, :, 0:n], ALU.add))
        pool.tensor_tensor(y[:], y[:], self.b[:], ALU.mult).then_inc(self.done, 1)

    def scalar_end(self, act):
        act.wait_ge(self.done, 1)
        act.activation(self.hi, self.c[:], ACT.Copy).then_inc(self.hi_done, 1)

    def vector(self, dve):
        dve.wait_ge(self.hi_done, 1)
        rest_of(dve, self.lo, self.c[:], self.hi)


def merge(nc, K, y, gates, following):
    panels = take_panels(K, 2)
    with stage(nc, K, "merge") as st:
        w = Parts(st.mem, nc, st.name, [P, PIECES, PIECE])
        wide = st.ps("wide", [P, 2, 4, HALF])
        hi_done, split_done, piece_used, gated, turned, turned_hi, dve_own = map(
            st.sem, ("hi_done", "split_done", "piece_used", "gated", "turned", "turned_hi", "dve_own"))

        def halves(a, n):
            t, h = n // 2, n % 2
            return a[:, 4 * h:4 * h + 4, t * P:(t + 1) * P]

        def bank(n):
            return wide[:, 0, n, :].rearrange("p (k n) -> p k n", k=4)

        with nc.Block(no_gpsimd_drain=True) as block:
            @block.sync
            def _(sp):
                start_panels(sp, K, following, split_done, panels[0])

            @block.tensor
            def _(pe):
                for a in range(2):
                    for k in range(4):
                        piece = 4 * a + k
                        pe.wait_ge(split_done, piece + 1)
                        for t in range(T):
                            for b in range(2):
                                mm = three_passes(pe, wide[:, a, 2 * t + b, :], y, w,
                                                  lambda x: x[:, piece, t * P:(t + 1) * P],
                                                  lambda x: x[:, piece % PIECES, b * HALF:(b + 1) * HALF],
                                                  start=k == 0, stop=k == 3)
                        mm.then_inc(piece_used, 1)
                for n in range(2 * T):
                    t, h = n // 2, n % 2
                    pe.wait_ge(gated, t + 1)
                    for k in range(4):
                        f = (4 * h + k) * P
                        mm = pe.transpose(wide[:, 0, n, k * P:(k + 1) * P], gates[:, 0, t, f:f + P], K.ident[:])
                    mm.then_inc(turned, 1)

            @block.vector
            def _(dve):
                own = Chain(dve, dve_own)

                def gate(a, t):
                    dve.wait_ge(piece_used, 4 * a + 4)
                    own(dve.tensor_tensor(gates[:, a, t, :], gates[:, a, t, :],
                                          wide[:, a, 2 * t:2 * t + 2, :].rearrange("p b n -> p (b n)"),
                                          ALU.mult))

                for a, i in enumerate(panels):
                    for c in range(4):
                        rest_of_piece(dve, K, w, i, c, 4 * a + c, hi_done, split_done)
                        if a == 1 and c >= 2:
                            gate(0, c - 2)
                for t in range(T):
                    gate(1, t)
                    dve.tensor_tensor(gates[:, 0, t, :], gates[:, 0, t, :], gates[:, 1, t, :],
                                      ALU.add).then_inc(gated, 1)
                for n in range(2 * T):
                    dve.wait_ge(turned_hi, n + 1)
                    rest_of(dve, halves(y.lo, n), bank(n), halves(y.hi, n))

            @block.scalar
            def _(act):
                for a, i in enumerate(panels):
                    for c in range(4):
                        split_piece(act, K, w, i, c, 4 * a + c, piece_used, hi_done)
                for n in range(2 * T):
                    act.wait_ge(turned, n + 1)
                    act.activation(halves(y.hi, n), bank(n), ACT.Copy).then_inc(turned_hi, 1)


def peer_scores(nc, K, sub_keys, qT, scores):
    M = 2 * PH
    with stage(nc, K, "peer_scores") as st:
        keys = st.sb("keys", [P, M, DKEY])
        keysT = st.sb("keysT", [P, M, NKEYS])
        tp = st.ps("tp", [P, 4, HALF])
        ps = st.ps("ps", [P, 4, HALF])
        loaded, turned, keys_moved, scored, moved = map(
            st.sem, ("loaded", "turned", "keys_moved", "scored", "moved"))
        with nc.Block(no_gpsimd_drain=True) as block:
            @block.sync
            def _(sp):
                for half in range(2):
                    m = slice(half * PH, (half + 1) * PH)
                    sp.dma_start(keys[:, m, :], sub_keys[half * 4:half * 4 + 4].rearrange(
                        "h a n d -> n (h a) d")).then_inc(loaded, 16)

            @block.tensor
            def _(pe):
                pe.wait_ge(loaded, 32)
                for n in range(4):
                    for k in range(4):
                        mm = pe.transpose(tp[:, n, k * P:(k + 1) * P], keys[:, 4 * n + k, :], K.ident[:])
                    mm.then_inc(turned, 1)
                for u in range(8):
                    g, t = u // 2, u % 2
                    pe.wait_ge(keys_moved, g + 1)
                    if u >= 4:
                        pe.wait_ge(moved, u - 3)
                    for k in range(4):
                        m = 4 * g + k
                        mm = pe.matmul(ps[:, u % 4, k * P:(k + 1) * P], qT[:, m, t * P:(t + 1) * P],
                                       keysT[:, m, :], start=True, stop=True)
                    mm.then_inc(scored, 1)

            @block.scalar
            def _(act):
                for n in range(4):
                    act.wait_ge(turned, n + 1)
                    act.activation(keysT[:, 4 * n:4 * n + 4, :],
                                   tp[:, n, :].rearrange("p (k n) -> p k n", k=4), ACT.Copy).then_inc(keys_moved, 1)

            @block.vector
            def _(dve):
                for u in range(8):
                    g, t = u // 2, u % 2
                    dve.wait_ge(scored, u + 1)
                    dve.tensor_copy(scores[:, t, 2 * g:2 * g + 2, :],
                                    ps[:, u % 4, :].rearrange("p (h n) -> p h n", h=2)).then_inc(moved, 1)


def peer(nc, K, A, l, h2, scores, g2):
    VS = 8
    U_LAYER = 16 * 2 * PH
    V_LAYER = U_LAYER * TOPK // VS
    AHEAD = 24
    rows_u = A.expert_u_2.rearrange("l e d -> (l e) d")
    rows_v = A.expert_v_2.rearrange("l e d -> (l e) d")
    u_slot = K.ring[:].rearrange("p s (j d) -> p (s j) d", d=D)
    with stage(nc, K, "peer") as st:
        v_slot = st.sb("v_slot", [P, VS, D])
        now, rest = (st.sb(n, [P, 2 * NKEYS]) for n in ("now", "rest"))
        value = st.sb("value", [P, 2, TOPK])
        place = st.sb("place", [P, 2, TOPK], U32)
        place_f = st.sb("place_f", [P, 2, TOPK])
        sums, left = (st.sb(n, [P, TOPK * TOPK]) for n in ("sums", "left"))
        best = st.sb("best", [P, T, TOPK])
        best_at = st.sb("best_at", [P, TOPK], U32)
        half = st.sb("half", [P, 2, TOPK], U32)
        half_f = st.sb("half_f", [P, 2, TOPK])
        hot = st.sb("hot", [P, TOPK, TOPK])
        key = st.sb("key", [P, 2, TOPK])
        expert_f = st.sb("expert_f", [P, TOPK])
        at_u, at_v = (st.sb(n, [P, T, TOPK], U32) for n in ("at_u", "at_v"))
        shift, total, inverse = (st.sb(n, [P, T]) for n in ("shift", "total", "inverse"))
        e, gate, dots, gelu, weight = (st.sb(n, [P, T, TOPK]) for n in ("e", "gate", "dots", "gelu", "weight"))
        diagonal = [st.sb(f"diagonal{t}", [P, TOPK, P]) for t in range(T)]
        scaled = h2
        query = st.ps("query", [P, T, D])
        y = st.ps("y", [P, T, 2, HALF])
        u_in = [st.pool_sem(f"u_in{j}") for j in range(TOPK)]
        v_in = [st.pool_sem(f"v_in{j}") for j in range(VS)]
        (query_ready, at_u_ready, at_v_ready, dots_done, shift_done, e_done, gelu_done, weight_done,
         diagonal_ready, v_used, paced, dve_own) = map(
            st.sem, ("query_ready", "at_u_ready", "at_v_ready", "dots_done", "shift_done", "e_done",
                     "gelu_done", "weight_done", "diagonal_ready", "v_used", "paced", "dve_own"))
        with nc.Block() as block:
            @block.gpsimd
            def _(pool):
                def gather_u(n, t, j):
                    pool.indirect_dma_start(
                        u_slot[:, j, :], None, rows_u,
                        bass.IndirectOffsetOnAxis(ap=at_u[:, t, j:j + 1], axis=0)).then_inc(u_in[j], 16)

                def unit(n, t, last):
                    pool.wait_ge(at_v_ready, n + 1)
                    if not last:
                        pool.wait_ge(at_u_ready, n + 2)
                    for j in range(TOPK):
                        pool.wait_ge(v_used, 16 * n + (j + 1 - VS + AHEAD))
                        pool.sem_inc(paced, 1)
                        pool.indirect_dma_start(
                            v_slot[:, j % VS, :], None, rows_v,
                            bass.IndirectOffsetOnAxis(ap=at_v[:, t, j:j + 1], axis=0)).then_inc(v_in[j % VS], 16)
                        if not last:
                            pool.wait_ge(dots_done, 16 * n + (j + 1))
                            pool.sem_inc(paced, 1)
                            gather_u(n + 1, 1 - t, j)

                pool.wait_ge(at_u_ready, 1)
                for j in range(TOPK):
                    gather_u(0, 0, j)
                with pool.Fori(0, PH - 1) as h:
                    for t in range(T):
                        unit(2 * h + t, t, False)
                unit(2 * PH - 2, 0, False)
                unit(2 * PH - 1, 1, True)

            @block.vector
            def _(dve):
                own = Chain(dve, dve_own)

                def sixteen(values, places, source, spare):
                    own(dve.max(values[:, 0:8], source))
                    own(dve.max_index(places[:, 0:8], values[:, 0:8], source))
                    own(dve.match_replace(spare, values[:, 0:8], source, GONE))
                    own(dve.max(values[:, 8:16], spare))
                    own(dve.max_index(places[:, 8:16], values[:, 8:16], spare))

                def choose(head, t):
                    own(dve.tensor_copy(now[:], scores[:, t, bass.ds(head, 1), :].rearrange("p a n -> p (a n)")))
                    for a in range(2):
                        sixteen(value[:, a, :], place[:, a, :], now[:, a * NKEYS:(a + 1) * NKEYS],
                                rest[:, a * NKEYS:(a + 1) * NKEYS])
                    own(dve.tensor_copy(place_f[:], place[:]))
                    own(dve.tensor_tensor(sums[:].rearrange("p (a b) -> p a b", b=TOPK),
                                          value[:, 0, :].unsqueeze(2).to_broadcast([P, TOPK, TOPK]),
                                          value[:, 1, :].unsqueeze(1).to_broadcast([P, TOPK, TOPK]), ALU.add))
                    sixteen(best[:, t, :], best_at[:], sums[:], left[:])
                    dve.tensor_scalar(shift[:, t:t + 1], best[:, t, 0:1], -1.0, None,
                                      ALU.mult).then_inc(shift_done, 1)
                    own(dve.tensor_scalar(half[:, 0, :], best_at[:], 4, None, ALU.logical_shift_right))
                    own(dve.tensor_scalar(half[:, 1, :], best_at[:], 15, None, ALU.bitwise_and))
                    own(dve.tensor_copy(half_f[:], half[:]))
                    for a in range(2):
                        own(dve.tensor_tensor(hot[:], half_f[:, a, :].unsqueeze(2).to_broadcast([P, TOPK, TOPK]),
                                              K.places[:].unsqueeze(1).to_broadcast([P, TOPK, TOPK]),
                                              ALU.is_equal))
                        own(dve.tensor_tensor(hot[:], hot[:],
                                              place_f[:, a, :].unsqueeze(1).to_broadcast([P, TOPK, TOPK]),
                                              ALU.mult))
                        own(dve.tensor_reduce(key[:, a, :], hot[:], AX.X, ALU.add))
                    own(dve.scalar_tensor_tensor(out=expert_f[:], in0=key[:, 0, :], scalar=float(NKEYS),
                                                 in1=key[:, 1, :], op0=ALU.mult, op1=ALU.add))
                    dve.tensor_scalar(at_u[:, t, :], expert_f[:], K.layer_base[:, 0:1], None,
                                      ALU.add).then_inc(at_u_ready, 1)

                def keep_for_v(n, t):
                    dve.wait_ge(v_used, 16 * n + AHEAD)
                    dve.wait_ge(at_u_ready, n + 2)
                    dve.tensor_copy(at_v[:, t, :], at_u[:, t, :]).then_inc(at_v_ready, 1)

                def unit(h, n, t, last):
                    if not last:
                        choose(h + t, 1 - t)
                    for j in range(TOPK):
                        dve.wait_ge(u_in[j], l * U_LAYER + 16 * n + 16)
                        dve.tensor_tensor_reduce(u_slot[:, j, :], u_slot[:, j, :], query[:, t, :], 1.0, 0.0,
                                                 ALU.mult, ALU.add, dots[:, t, j:j + 1]).then_inc(dots_done, 1)
                    dve.wait_ge(e_done, n + 1)
                    own(dve.reciprocal(inverse[:, t:t + 1], total[:, t:t + 1]))
                    own(dve.tensor_scalar(gate[:, t, :], e[:, t, :], inverse[:, t:t + 1], None, ALU.mult))
                    dve.wait_ge(gelu_done, n + 1)
                    dve.tensor_tensor(weight[:, t, :], gelu[:, t, :], gate[:, t, :],
                                      ALU.mult).then_inc(weight_done, 1)
                    if not last:
                        keep_for_v(n, 1 - t)

                choose(0, 0)
                dve.wait_ge(at_u_ready, 1)
                dve.tensor_copy(at_v[:, 0, :], at_u[:, 0, :]).then_inc(at_v_ready, 1)
                dve.wait_ge(query_ready, T)
                own.clear()
                with dve.Fori(0, PH - 1) as h:
                    with own.turn():
                        for t in range(T):
                            unit(h, 2 * h + t, t, False)
                unit(PH - 1, 2 * PH - 2, 0, False)
                unit(PH - 1, 2 * PH - 1, 1, True)
                own(dve.tensor_scalar(K.layer_base[:], K.layer_base[:], float(EXPERTS), None, ALU.add))
                dve.wait_ge(v_used, 2 * PH * TOPK + AHEAD)
                for t in range(T):
                    own(dve.tensor_tensor(scaled[:, t, :], y[:, t, :, :].rearrange("p b n -> p (b n)"), g2,
                                          ALU.mult))
                    own(dve.tensor_tensor(K.x[:, t, :], K.x[:, t, :], scaled[:, t, :], ALU.add))

            @block.scalar
            def _(act):
                for t in range(T):
                    for b in range(2):
                        ins = act.activation(query[:, t, b * HALF:(b + 1) * HALF],
                                             h2[:, t, b * HALF:(b + 1) * HALF], ACT.Copy)
                    ins.then_inc(query_ready, 1)

                def gates(n, t):
                    act.wait_ge(shift_done, n + 1)
                    act.activation(e[:, t, :], best[:, t, :], ACT.Exp, bias=shift[:, t:t + 1],
                                   accum_out=total[:, t:t + 1]).then_inc(e_done, 1)

                def unit(n, t, last):
                    if not last:
                        gates(n + 1, 1 - t)
                    act.wait_ge(dots_done, 16 * n + 16)
                    act.activation(gelu[:, t, :], dots[:, t, :], ACT.Gelu_apprx_tanh).then_inc(gelu_done, 1)
                    act.wait_ge(weight_done, n + 1)
                    act.wait_ge(v_used, 16 * n + (AHEAD - 16))
                    for j in range(TOPK):
                        act.activation(diagonal[t][:, j, :], K.ident[:], ACT.Copy,
                                       scale=weight[:, t, j:j + 1]).then_inc(diagonal_ready, 1)

                gates(0, 0)
                with act.Fori(0, PH - 1) as h:
                    for t in range(T):
                        unit(2 * h + t, t, False)
                unit(2 * PH - 2, 0, False)
                unit(2 * PH - 1, 1, True)

            @block.tensor
            def _(pe):
                for t in range(T):
                    for b in range(2):
                        mm = pe.matmul(y[:, t, b, :], K.zeros[:, 0:P], K.zeros[:], start=True, stop=False,
                                       skip_group_check=True)
                pe.sem_inc(v_used, AHEAD)

                def unit(n, t):
                    for j in range(TOPK):
                        pe.wait_ge(diagonal_ready, 16 * n + (j + 1))
                        pe.wait_ge(v_in[j % VS], l * V_LAYER + 32 * n + 16 * (j // VS + 1))
                        for b in range(2):
                            mm = pe.matmul(y[:, t, b, :], diagonal[t][:, j, :],
                                           v_slot[:, j % VS, b * HALF:(b + 1) * HALF], start=False, stop=False,
                                           skip_group_check=True)
                        mm.then_inc(v_used, 1)

                with pe.Fori(0, PH) as h:
                    for t in range(T):
                        unit(2 * h + t, t)


def block_two(nc, K, A, ada):
    tables(nc, K)
    with nc.Fori(0, LAYERS) as l:
        begin_ring(nc, K)

        def layer(w):
            return w[bass.ds(l, 1)]

        def matrix(w):
            return layer(w).rearrange("a k n -> (a k) n")

        def condition(n, columns=slice(0, D)):
            return ada[:, bass.ds(l * ADA + (n * D + columns.start), columns.stop - columns.start)]

        def wide(w, panels):
            return [(columns(w, n), KC) for n in panels]

        w_in, w_out, w_query = (matrix(w) for w in (A.w_in_2, A.w_out_2, A.w_query_2))
        proj = [matrix(w).rearrange("(k p) n -> p k n", p=P) for w in (A.w_attn_proj_2, A.w_conv_proj_2)]
        with ExitStack() as mem:
            hT = Parts(mem, nc, "mix_hT", [P, KC, S])
            norm(nc, K, layer(A.norm1_g_2), modulate=(condition(1), condition(0)), hT=hT,
                 panels=wide(w_in, range(SLOTS)))
            with ExitStack() as inner:
                def sb(name, shape):
                    return inner.enter_context(nc.sbuf_tensor(name, shape, F32))

                turned = {n: sb(f"mix_{n}", [P, 4, S]) for n in ("q", "k", "b", "c", "h")}
                v = sb("mix_v", [P, T, HALF])
                gates = sb("mix_gates", [P, 2, T, D])
                kinds = ["q", "k", "v", "b", "c", "h", 0, 1, 2, 3]

                def evacuate(act, n, half, ps):
                    kind = kinds[n]
                    if kind == "v":
                        return act.activation(v[:, half, :], ps, ACT.Copy)
                    if kind in turned:
                        return act.activation(turned[kind][:, 2 * half:2 * half + 2, :], ps, ACT.Copy)
                    return act.activation(gates[:, kind // 2, half, kind % 2 * HALF:(kind % 2 + 1) * HALF], ps,
                                          ACT.Sigmoid)

                project(nc, K, hT, ["features" if k in turned else "tokens" for k in kinds], evacuate,
                        own_panels=wide(w_in, range(SLOTS, len(kinds))),
                        following=[(w, 4) for w in proj] + wide(w_out, range(2)))

                def head(a):
                    return lambda h: turned[a][h % 2 * HD:h % 2 * HD + HD, h // 2, :]

                conv_w = layer(A.conv_w_2).rearrange("a k (c p) -> (a k c) p", p=P)
                attend(nc, K, MH, HD ** -0.5, head("q"), head("k"),
                       lambda h, k: v[:, k, h * HD:(h + 1) * HD], hT, far=K.far,
                       side_of=lambda st: Convolution(st, K, conv_w, turned["b"], turned["c"], turned["h"],
                                                      hT.hi[:, 4:8, :], hT.lo[:, 4:8, :]))
                merge(nc, K, hT, gates, following=wide(w_query, range(2)))
            residual(nc, K, hT, scale=lambda n: condition(2, slice(n * HALF, (n + 1) * HALF)),
                     following=wide(w_query, range(2, 4)))
        with ExitStack() as mem:
            h2 = mem.enter_context(nc.sbuf_tensor("h2", [P, T, D], F32))
            scores = mem.enter_context(nc.sbuf_tensor("scores", [P, T, PH, 2 * NKEYS], F32))
            with ExitStack() as inner:
                h2T = Parts(inner, nc, "h2T", [P, KC, S])
                norm(nc, K, layer(A.norm2_g_2), modulate=(condition(4), condition(3)), hT=h2T, keep=h2)
                qT = inner.enter_context(nc.sbuf_tensor("peer_q", [P, 2 * PH, S], F32))
                project(nc, K, h2T, ["features"] * 4,
                        lambda act, n, half, ps: act.activation(
                            qT[:, 4 * n + 2 * half:4 * n + 2 * half + 2, :], ps, ACT.Copy))
                peer_scores(nc, K, layer(A.sub_keys_2).rearrange("l h a n d -> (l h) a n d"), qT, scores)
            peer(nc, K, A, l, h2, scores, condition(5))



def program(nc, A, out):
    K = Kept()
    K.stages = K.pool_sems = 0
    with ExitStack() as kept:
        def sb(name, shape, dt=F32):
            return kept.enter_context(nc.sbuf_tensor(name, shape, dt))

        K.ring = sb("ring", [P, SLOTS, PANEL])
        K.x = sb("x", [P, T, D])
        K.ident = sb("ident", [P, P])
        K.ones = sb("ones", [P, P])
        K.c_cols = sb("c_cols", [P, KC])
        K.layer_base = sb("layer_base", [P, 1])
        K.far = sb("far", [P, T, S])
        K.places = sb("places", [P, TOPK])
        K.zeros = sb("zeros", [P, HALF])
        K.ring_in = [kept.enter_context(nc.semaphore(f"ring_in{n}")) for n in range(SLOTS)]
        ada = sb("ada", [P, LAYERS * ADA])

        block_one(nc, K, A, ada)
        block_two(nc, K, A, ada)
        begin_ring(nc, K)
        norm(nc, K, A.final_g_2.rearrange("(a n) -> a n", a=1), out=out)


_INS = ["x", "norm_mix", "norm_mlp", "attn_w_qkv", "attn_q_norm", "attn_k_norm", "attn_w_o", "gla_w_in",
        "gla_w_gate_up", "gla_b_gate", "gla_out_norm", "gla_w_o", "mlp_w_in", "mlp_w_out", "final_norm",
        "c_2", "norm1_g_2", "norm2_g_2", "w_ada_2", "b_ada_2", "w_in_2", "conv_w_2", "w_attn_proj_2",
        "w_conv_proj_2", "w_out_2", "w_query_2", "sub_keys_2", "expert_u_2", "expert_v_2", "final_g_2"]


def rope_table():
    half = HD // 2
    inv = np.float32(10000.0) ** (-np.arange(0, half, 2, dtype=np.float32) / np.float32(half))
    pos = np.stack([np.arange(S) // 64, np.arange(S) % 64], 1).astype(np.float32)
    ang = pos[:, :, None] * inv[None, None, :]
    cos = np.repeat(np.cos(ang)[:, :, None, :], 2, axis=2).reshape(S, HD)
    sin = (np.sin(ang)[:, :, None, :] * np.array([-1, 1], np.float32)[None, None, :, None]).reshape(S, HD)
    return np.ascontiguousarray(np.stack([cos, sin], 1).astype(np.float32))


def kernel(**inputs):
    import numpy as _np
    import concourse.bacc as _bacc
    from concourse import mybir as _mybir
    from concourse.bass_utils import run_bass_kernel_spmd as _run

    nc = _bacc.Bacc("TRN2", target_bir_lowering=False, num_devices=1)
    A = Kept()
    arrays = {}

    def declare(name, a):
        arrays[f"in_{name}_dram"] = a
        return nc.dram_tensor(f"in_{name}_dram", a.shape, _mybir.dt.from_np(a.dtype), kind="ExternalInput").ap()

    ins = {name: declare(name, _np.ascontiguousarray(inputs[name])) for name in _INS}
    ins["rope_table"] = declare("rope_table", rope_table())
    A.__dict__.update(ins)
    out = nc.dram_tensor("out_0_dram", (1, S, D), _mybir.dt.float32, kind="ExternalOutput").ap()
    program(nc, A, out)
    r = _run(nc, [arrays], core_ids=[0])
    return r.results[0]["out_0_dram"]
```

```python
import math
from contextlib import ExitStack, contextmanager

import numpy as np

import concourse.bass as bass
from concourse import mybir

ALU = mybir.AluOpType
ACT = mybir.ActivationFunctionType
AX = mybir.AxisListType
F32 = mybir.dt.float32
F32R = mybir.dt.float32r
U32 = mybir.dt.uint32

P = 128
D = 1024
S = 256
T = S // P
KC = D // P
HALF = 512
EPS = 1e-6
SLOTS = 4
PANEL = 4096
PIECE = PANEL // 4
PIECES = 3

N_HEADS, N_KV, HD = 16, 4, 64
QK_HEADS = N_HEADS + N_KV
GLA_H, GLA_DK, GLA_DV, CHUNK, RANK = 4, 128, 256, 64, 16
N_CHUNKS = S // CHUNK
D_FF = 4 * D
LAYERS = 2
MH = 8
CONV_K = 3
ADA = 6 * D
PH, NKEYS, DKEY, TOPK = 8, 128, 128, 16
EXPERTS = NKEYS * NKEYS
STAGE_SEMS = 150
POOL_SEMS = 200
MASKED = -1e30
GONE = -3.0e38


class Chain:

    def __init__(self, eng, sem):
        self.eng, self.sem, self.n = eng, sem, 0

    def __call__(self, ins):
        self.n += 1
        ins.then_inc(self.sem, 1)
        self.eng.wait_ge(self.sem, self.n)
        return ins

    def several(self, *many):
        for ins in many:
            self.n += 1
            ins.then_inc(self.sem, 1)
        self.eng.wait_ge(self.sem, self.n)

    def clear(self):
        self.eng.sem_clear(self.sem)
        self.n = 0

    @contextmanager
    def turn(self):
        assert self.n == 0, "clear it ahead of the loop"
        yield
        self.clear()


class Stage:

    def __init__(self, nc, K, mem, name):
        K.stages += 1
        self.nc, self.K, self.mem, self.name, self.used = nc, K, mem, f"{name}{K.stages}", 0

    def sb(self, name, shape, dt=F32):
        return self.mem.enter_context(self.nc.sbuf_tensor(f"{self.name}_{name}", shape, dt))

    def ps(self, name, shape, dt=F32):
        return self.mem.enter_context(self.nc.psum_tensor(f"{self.name}_{name}", shape, dt))

    def sem(self, name):
        self.used += 1
        return self.mem.enter_context(self.nc.semaphore(f"{self.name}_{name}", num=STAGE_SEMS + self.used - 1))

    def pool_sem(self, name):
        self.K.pool_sems += 1
        return self.mem.enter_context(self.nc.semaphore(f"{self.name}_{name}",
                                                        num=POOL_SEMS + self.K.pool_sems - 1))


class Kept:
    pass


@contextmanager
def stage(nc, K, name):
    with ExitStack() as mem:
        st = Stage(nc, K, mem, name)
        yield st
        nc.all_engine_barrier(sems_to_clear=range(STAGE_SEMS, STAGE_SEMS + st.used))


def columns(w, n):
    return w[:, n * HALF:(n + 1) * HALF].rearrange("(k p) n -> p k n", p=P)


def ring_view(K, slot, k=KC):
    return K.ring[:, slot, :].rearrange("p (k n) -> p k n", k=k)


def begin_ring(nc, K):
    K.loaded = K.used = 0
    nc.all_engine_barrier(sems_to_clear=range(K.ring_in[0].num, K.ring_in[-1].num + 1))


def start_panels(dma, K, panels, split_done=None, first=None):
    for src, k in panels:
        before = K.loaded - SLOTS
        if split_done is None:
            assert before < K.used
        elif before >= first:
            dma.wait_ge(split_done, 4 * (before - first) + 4)
        dma.dma_start(ring_view(K, K.loaded % SLOTS, k), src).then_inc(K.ring_in[K.loaded % SLOTS], 16)
        K.loaded += 1


def take_panels(K, n):
    first = K.used
    K.used += n
    return range(first, first + n)


def arrived(i):
    return 16 * (i // SLOTS + 1)


class Parts:

    def __init__(self, mem, nc, name, shape):
        self.hi, self.lo = (mem.enter_context(nc.sbuf_tensor(f"{name}_{n}", shape, F32R)) for n in ("hi", "lo"))


def rest_of(dve, out_lo, a, hi):
    return dve.tensor_tensor(out_lo, a, hi.bitcast(F32), ALU.subtract)


def three_passes(pe, out, lhs, rhs, at, to, start, stop, **more):
    pe.matmul(out, at(lhs.hi), to(rhs.hi), start=start, stop=False, **more)
    pe.matmul(out, at(lhs.hi), to(rhs.lo), start=False, stop=False, **more)
    return pe.matmul(out, at(lhs.lo), to(rhs.hi), start=False, stop=stop, **more)



def setup(nc, K, A, first_panels):
    with stage(nc, K, "setup") as st:
        rows = st.sb("rows", [KC, P])
        cols = st.ps("cols", [P, HALF])
        loaded, zeroed, made, turned, gpsimd_own = map(
            st.sem, ("loaded", "zeroed", "made", "turned", "gpsimd_own"))
        with nc.Block(no_gpsimd_drain=True) as block:
            @block.sync
            def _(sp):
                sp.dma_start(K.x[:], A.x[0].rearrange("(t p) d -> p t d", p=P)).then_inc(loaded, 16)
                sp.dma_start(rows[:], A.c_2.rearrange("a (k p) -> (a k) p", p=P)).then_inc(loaded, 16)
                start_panels(sp, K, first_panels)
                sp.wait_ge(loaded, 16 * 2)

            @block.gpsimd
            def _(pool):
                own = Chain(pool, gpsimd_own)
                own(pool.memset(K.ident[:], 0.0))
                own(pool.memset(K.pick[:], 0.0))
                for r in range(6):
                    own(pool.memset(K.pick[:, r, r:r + 1], 1.0))
                own(pool.memset(K.select[:], 0.0))
                own(pool.affine_select(out=K.select[:], in_=K.select[:], compare_op=ALU.not_equal, fill=1.0,
                                       base=0, pattern=[[-1, 6], [0, P]], channel_multiplier=1))
                pool.affine_select(out=K.ident[:], in_=K.ident[:], compare_op=ALU.not_equal, fill=1.0,
                                   base=0, pattern=[[-1, P]], channel_multiplier=1).then_inc(made, 1)

            @block.tensor
            def _(pe):
                pe.wait_ge(loaded, 16 * 2)
                pe.wait_ge(made, 1)
                pe.transpose(cols[:, 0:KC], rows[:], K.ident[0:KC, 0:KC]).then_inc(turned, 1)

            @block.vector
            def _(dve):
                dve.memset(K.layer_base[:], 0.0).then_inc(zeroed, 1)
                dve.wait_ge(turned, 1)
                dve.tensor_copy(K.c_cols[:], cols[:, 0:KC]).then_inc(zeroed, 1)
                dve.wait_ge(zeroed, 2)


def give(pe, K, to, layer, n):
    for b in range(2):
        mm = pe.matmul(to[:, b * HALF:(b + 1) * HALF], K.select[:, n, :],
                       K.ada[:, bass.ds(layer * D + b * HALF, HALF)], start=True, stop=True)
    return mm


class Conditions:

    def __init__(self, st, K, csum, bias, layer):
        self.K, self.csum, self.source, self.layer = K, csum, bias, layer
        self.ps = st.ps("cond", [P, 2, HALF])
        self.bias = st.sb("cond_bias", [6, D])
        self.loaded, self.done = st.sem("cond_loaded"), st.sem("cond_done")

    def sync(self, sp):
        sp.dma_start(self.bias[:], self.source.rearrange("(r n) -> r n", r=6)).then_inc(self.loaded, 16)

    def tensor(self, pe):
        for b in range(2):
            for r in range(6):
                c = r * D + b * HALF
                mm = pe.matmul(self.ps[0:6, b, :], self.K.pick[:, r, :], self.csum[:, c:c + HALF],
                               start=r == 0, stop=r == 5)
        mm.then_inc(self.done, 1)

    def vector(self, dve):
        dve.wait_ge(self.loaded, 16)
        dve.wait_ge(self.done, 1)
        dve.tensor_tensor(self.K.ada[:, self.layer * D:(self.layer + 1) * D],
                          self.ps[0:6, :, :].rearrange("p b n -> p (b n)"), self.bias[:], ALU.add)



def norm(nc, K, gain, modulate=None, hT=None, out=None, keep=None, panels=(), side_of=None):
    with stage(nc, K, "norm") as st:
        xn = st.sb("xn", [P, T, D]) if keep is None else keep
        side = side_of(st) if side_of else None
        rows = st.sb("rows", [P, D])
        ssq, ms, std, rstd = (st.sb(n, [P, T]) for n in ("ssq", "ms", "std", "rstd"))
        tp = st.ps("tp", [P, 2 * T, HALF])
        squares = tp[:].rearrange("p (t b) n -> p t (b n)", t=T)
        if modulate is not None:
            given = st.ps("given", [P, 2, D])
        ms_done, std_done, xn_done, turned, hi_done, loaded, stored, given_done, dve_own = map(
            st.sem, ("ms_done", "std_done", "xn_done", "turned", "hi_done", "loaded",
                     "stored", "given_done", "dve_own"))

        def halves(a, n):
            t, h = n // 2, n % 2
            return a[:, 4 * h:4 * h + 4, t * P:(t + 1) * P]

        def bank(n):
            return tp[:, n, :].rearrange("p (k n) -> p k n", k=4)

        with nc.Block(no_gpsimd_drain=True) as block:
            @block.sync
            def _(sp):
                sp.dma_start(rows[:], gain.partition_broadcast(P)).then_inc(loaded, 16)
                start_panels(sp, K, panels)
                if side:
                    side.sync(sp)
                if out is not None:
                    for t in range(T):
                        sp.wait_ge(xn_done, 2 * t + 2)
                        sp.dma_start(out[0][t * P:(t + 1) * P, :], xn[:, t, :]).then_inc(stored, 16)
                    sp.wait_ge(stored, 16 * T)

            @block.scalar
            def _(act):
                act.wait_ge(ms_done, 1)
                act.activation(std[:], ms[:], ACT.Sqrt).then_inc(std_done, 1)
                for n in range(2 * T if hT else 0):
                    act.wait_ge(turned, n + 1)
                    act.activation(halves(hT.hi, n), bank(n), ACT.Copy).then_inc(hi_done, 1)

            @block.vector
            def _(dve):
                own = Chain(dve, dve_own)
                own.several(*(dve.tensor_tensor_reduce(squares[:, t, :], K.x[:, t, :], K.x[:, t, :], 1.0, 0.0,
                                                       ALU.mult, ALU.add, ssq[:, t:t + 1]) for t in range(T)))
                dve.tensor_scalar(ms[:], ssq[:], 1.0 / D, EPS, ALU.mult, ALU.add).then_inc(ms_done, 1)
                if modulate is not None:
                    dve.wait_ge(loaded, 16)
                    dve.wait_ge(given_done, 1)
                    own(dve.scalar_tensor_tensor(out=rows[:], in0=given[:, 0, :], scalar=1.0, in1=rows[:],
                                                 op0=ALU.add, op1=ALU.mult))
                dve.wait_ge(std_done, 1)
                own(dve.reciprocal(rstd[:], std[:]))
                if modulate is None:
                    dve.wait_ge(loaded, 16)
                else:
                    dve.wait_ge(given_done, 2)
                for t in range(T):
                    if modulate is None:
                        for f in (0, HALF):
                            dve.scalar_tensor_tensor(
                                out=xn[:, t, f:f + HALF], in0=K.x[:, t, f:f + HALF], scalar=rstd[:, t:t + 1],
                                in1=rows[:, f:f + HALF], op0=ALU.mult, op1=ALU.mult).then_inc(xn_done, 1)
                    else:
                        own(dve.scalar_tensor_tensor(out=xn[:, t, :], in0=K.x[:, t, :], scalar=rstd[:, t:t + 1],
                                                     in1=rows[:], op0=ALU.mult, op1=ALU.mult))
                        for f in (0, HALF):
                            dve.tensor_tensor(xn[:, t, f:f + HALF], xn[:, t, f:f + HALF],
                                              given[:, 1, f:f + HALF], ALU.add).then_inc(xn_done, 1)
                for n in range(2 * T if hT else 0):
                    dve.wait_ge(hi_done, n + 1)
                    rest_of(dve, halves(hT.lo, n), bank(n), halves(hT.hi, n))
                if side:
                    side.vector(dve)

            @block.tensor
            def _(pe):
                if modulate is not None:
                    for n in range(2):
                        give(pe, K, given[:, n, :], modulate[0], modulate[1 + n]).then_inc(given_done, 1)
                if side:
                    side.tensor(pe)
                for n in range(2 * T if hT else 0):
                    t, h = n // 2, n % 2
                    pe.wait_ge(xn_done, n + 1)
                    for k in range(4):
                        f = (4 * h + k) * P
                        mm = pe.transpose(tp[:, n, k * P:(k + 1) * P], xn[:, t, f:f + P], K.ident[:])
                    mm.then_inc(turned, 1)



def split_piece(act, K, w, i, c, piece, piece_free, hi_done):
    if c == 0:
        act.wait_ge(K.ring_in[i % SLOTS], arrived(i))
    if piece >= PIECES:
        act.wait_ge(piece_free, piece - PIECES + 1)
    act.activation(w.hi[:, piece % PIECES, :], K.ring[:, i % SLOTS, c * PIECE:(c + 1) * PIECE],
                   ACT.Copy).then_inc(hi_done, 1)


def chunk_of(K, i, m):
    return ring_view(K, i % SLOTS)[:, :, m * P:(m + 1) * P]


def rest_of_piece(dve, K, w, i, c, piece, hi_done, split_done):
    dve.wait_ge(hi_done, piece + 1)
    rest_of(dve, w.lo[:, piece % PIECES, :], K.ring[:, i % SLOTS, c * PIECE:(c + 1) * PIECE],
            w.hi[:, piece % PIECES, :]).then_inc(split_done, 1)


def project(nc, K, lhs, kinds, evacuate, own_panels=(), following=()):
    panels = take_panels(K, len(kinds))
    with stage(nc, K, "project") as st:
        w = Parts(st.mem, nc, st.name, [P, PIECES, PIECE])
        ps = st.ps("ps", [P, 2, 4, HALF])
        hi_done, split_done, piece_used, bank_free = map(
            st.sem, ("hi_done", "split_done", "piece_used", "bank_free"))
        with nc.Block(no_gpsimd_drain=True) as block:
            @block.sync
            def _(sp):
                start_panels(sp, K, own_panels, split_done, panels[0])
                start_panels(sp, K, following, split_done, panels[0])

            @block.tensor
            def _(pe):
                for n, kind in enumerate(kinds):
                    if n >= 2:
                        pe.wait_ge(bank_free, 2 * (n - 2) + 2)
                    for c in range(4):
                        piece = 4 * n + c
                        pe.wait_ge(split_done, piece + 1)
                        for kk in range(2):
                            k = 2 * c + kk
                            a = piece % PIECES
                            if kind == "tokens":
                                for t in range(T):
                                    mm = three_passes(pe, ps[:, n % 2, t, :], lhs, w,
                                                      lambda x: x[:, k, t * P:(t + 1) * P],
                                                      lambda x: x[:, a, kk * HALF:(kk + 1) * HALF],
                                                      start=k == 0, stop=k == KC - 1)
                            else:
                                for m in range(4):
                                    f = kk * HALF + m * P
                                    mm = three_passes(pe, ps[:, n % 2, m, 0:S], w, lhs,
                                                      lambda x: x[:, a, f:f + P], lambda x: x[:, k, :],
                                                      start=k == 0, stop=k == KC - 1)
                        mm.then_inc(piece_used, 1)

            @block.scalar
            def _(act):
                def take_out(n):
                    for b in range(2):
                        act.wait_ge(piece_used, 4 * n + 4)
                        a = ps[:, n % 2, b, :] if kinds[n] == "tokens" else ps[:, n % 2, 2 * b:2 * b + 2, 0:S]
                        evacuate(act, n, b, a).then_inc(bank_free, 1)

                for n, i in enumerate(panels):
                    for c in range(4):
                        split_piece(act, K, w, i, c, 4 * n + c, piece_used, hi_done)
                        if c == 2 and n >= 1:
                            take_out(n - 1)
                take_out(len(kinds) - 1)

            @block.vector
            def _(dve):
                for n, i in enumerate(panels):
                    for c in range(4):
                        rest_of_piece(dve, K, w, i, c, 4 * n + c, hi_done, split_done)



def rope(nc, K, qkv, qT, kT, A, side_of):
    QK = QK_HEADS * HD
    with stage(nc, K, "rope") as st:
        side = side_of(st)
        gains = st.sb("gains", [P, 2, HD])
        table = st.sb("table", [P, T, 2, HD])
        squares = st.sb("squares", [P, T, QK])
        straight = st.sb("straight", [P, T, QK])
        crossed = st.sb("crossed", [P, T, QK])
        kk = st.sb("kk", [P, T, N_KV, 2, HD])
        ms, std, rstd = (st.sb(n, [P, T, QK_HEADS]) for n in ("ms", "std", "rstd"))
        tp = st.ps("tp", [P, 6, HALF])
        loaded, squared, ms_done, std_done, rotated, turned, moved, dve_own = map(
            st.sem, ("loaded", "squared", "ms_done", "std_done", "rotated", "turned", "moved", "dve_own"))
        with nc.Block(no_gpsimd_drain=True) as block:
            @block.sync
            def _(sp):
                sp.dma_start(gains[:, 0, :], A.attn_q_norm[0:1, :].partition_broadcast(P)).then_inc(loaded, 16)
                sp.dma_start(gains[:, 1, :], A.attn_k_norm[0:1, :].partition_broadcast(P)).then_inc(loaded, 16)
                sp.dma_start(table[:], A.rope_table.rearrange("(t p) a d -> p t a d", p=P)).then_inc(loaded, 16)

            @block.gpsimd
            def _(pool):
                side.gpsimd(pool)

            @block.scalar
            def _(act):
                for t in range(T):
                    act.activation(squares[:, t, :], qkv[:, t, 0:QK], ACT.Square).then_inc(squared, 1)
                for t in range(T):
                    act.wait_ge(ms_done, t + 1)
                    act.activation(std[:, t, :], ms[:, t, :], ACT.Sqrt).then_inc(std_done, 1)
                for n in range(6):
                    act.wait_ge(turned, n + 1)
                    t, b = n // 3, n % 3
                    to = qT[:, 4 * b:4 * b + 4, :] if b < 2 else kT[:, 0:4, :]
                    act.activation(to[:, :, t * P:(t + 1) * P],
                                   tp[:, n, :].rearrange("p (k n) -> p k n", k=4),
                                   ACT.Copy).then_inc(moved, 1)

            @block.vector
            def _(dve):
                own = Chain(dve, dve_own)
                for t in range(T):
                    dve.wait_ge(squared, t + 1)
                    own(dve.tensor_reduce(ms[:, t, :], squares[:, t, :].rearrange("p (h d) -> p h d", d=HD),
                                          AX.X, ALU.add))
                    dve.tensor_scalar(ms[:, t, :], ms[:, t, :], 1.0 / HD, EPS, ALU.mult,
                                      ALU.add).then_inc(ms_done, 1)
                dve.wait_ge(loaded, 16 * 3)
                for t in range(T):
                    dve.wait_ge(std_done, t + 1)
                    own(dve.reciprocal(rstd[:, t, :], std[:, t, :]))
                    x = qkv[:, t, 0:QK].rearrange("p (h d) -> p h d", d=HD)
                    own(dve.tensor_tensor(x, x, rstd[:, t, :].unsqueeze(2).to_broadcast([P, QK_HEADS, HD]),
                                          ALU.mult))
                    for a, heads in ((0, slice(0, N_HEADS)), (1, slice(N_HEADS, QK_HEADS))):
                        n = heads.stop - heads.start
                        own(dve.tensor_tensor(x[:, heads, :], x[:, heads, :],
                                              gains[:, a:a + 1, :].to_broadcast([P, n, HD]), ALU.mult))
                    s = straight[:, t, :].rearrange("p (h d) -> p h d", d=HD)
                    c = crossed[:, t, :].rearrange("p (h r e d) -> p h r e d", r=2, e=2, d=HD // 4)
                    x4 = qkv[:, t, 0:QK].rearrange("p (h r e d) -> p h r e d", r=2, e=2, d=HD // 4)
                    sin = table[:, t, 1, :].rearrange("p (r e d) -> p r e d", r=2, e=2)
                    own(dve.tensor_tensor(s, x, table[:, t, 0:1, :].to_broadcast([P, QK_HEADS, HD]), ALU.mult))
                    for e in range(2):
                        own(dve.tensor_tensor(
                            c[:, :, :, e, :], x4[:, :, :, 1 - e, :],
                            sin[:, :, e, :].unsqueeze(1).to_broadcast([P, QK_HEADS, 2, HD // 4]), ALU.mult))
                    q = slice(0, N_HEADS * HD)
                    k = slice(N_HEADS * HD, QK)
                    own(dve.tensor_tensor(straight[:, t, q], straight[:, t, q], crossed[:, t, q], ALU.add))
                    for copy in range(2):
                        own(dve.tensor_tensor(
                            kk[:, t, :, copy, :], straight[:, t, k].rearrange("p (h d) -> p h d", d=HD),
                            crossed[:, t, k].rearrange("p (h d) -> p h d", d=HD), ALU.add))
                    dve.sem_inc(rotated, 1)

            @block.tensor
            def _(pe):
                for n in range(6):
                    t, b = n // 3, n % 3
                    pe.wait_ge(rotated, t + 1)
                    for k in range(4):
                        if b < 2:
                            a = straight[:, t, (4 * b + k) * P:(4 * b + k + 1) * P]
                        else:
                            a = kk[:, t, k, :, :].rearrange("p c d -> p (c d)")
                        mm = pe.transpose(tp[:, n, k * P:(k + 1) * P], a, K.ident[:])
                    mm.then_inc(turned, 1)


def attend(nc, K, heads, scale, q_of, k_of, v_of, oT, far=None, side_of=None, panels=()):
    B = 3
    with stage(nc, K, "attend") as st:
        scores = st.ps("scores", [P, B, T, S])
        turn = st.ps("turn", [P, 2, T, S])
        o = st.ps("o", [P, 2, HALF])
        biased = st.sb("biased", [P, B, T, S]) if far is not None else None
        probs = st.sb("probs", [P, B, T, S])
        probsT = st.sb("probsT", [P, 2, T, S])
        top, shift, total, inverse = (st.sb(n, [P, 2 * heads]) for n in ("top", "shift", "total", "inverse"))
        scored, bias_done, shift_done, exp_done, normed, turned, moved, pv_done, o_hi, o_moved, dve_own = map(
            st.sem, ("scored", "bias_done", "shift_done", "exp_done", "normed", "turned", "moved",
                     "pv_done", "o_hi", "o_moved", "dve_own"))
        side = side_of(st) if side_of else None
        with nc.Block(no_gpsimd_drain=True) as block:
            @block.sync
            def _(sp):
                if side:
                    side.sync(sp)
                start_panels(sp, K, panels)

            @block.gpsimd
            def _(pool):
                if side:
                    side.gpsimd(pool)

            @block.tensor
            def _(pe):
                if side:
                    side.tensor(pe)

                def score(h):
                    if h >= B:
                        pe.wait_ge(bias_done if far is not None else exp_done,
                                   h - B + 1 if far is not None else T * (h - B + 1))
                    for t in range(T):
                        mm = pe.matmul(scores[:, h % B, t, :], q_of(h)[:, t * P:(t + 1) * P], k_of(h),
                                       start=True, stop=True)
                    mm.then_inc(scored, 1)

                def transposes(h):
                    pe.wait_ge(normed, h + 1)
                    if h >= 2:
                        pe.wait_ge(moved, h - 1)
                    for t in range(T):
                        for k in range(T):
                            mm = pe.transpose(turn[:, h % 2, k, t * P:(t + 1) * P],
                                              probs[:, h % B, t, k * P:(k + 1) * P], K.ident[:])
                    mm.then_inc(turned, 1)

                def weigh(h):
                    pe.wait_ge(moved, h + 1)
                    if h >= 4 and h % 2 == 0:
                        pe.wait_ge(o_moved, h // 2 - 1)
                    r = h % 2 * HD
                    for k in range(T):
                        mm = pe.matmul(o[r:r + HD, h // 2 % 2, 0:S], v_of(h, k), probsT[:, h % 2, k, :],
                                       start=k == 0, stop=k == T - 1)
                    mm.then_inc(pv_done, 1)

                for h in range(heads + B):
                    if h < heads:
                        score(h)
                    if B - 1 <= h < heads + B - 1:
                        transposes(h - B + 1)
                    if h >= B:
                        weigh(h - B)

            @block.scalar
            def _(act):
                if side:
                    side.scalar(act)
                source = scores if far is None else biased

                def hi_of(pair):
                    act.wait_ge(pv_done, 2 * pair + 2)
                    act.activation(oT.hi[:, pair, :], o[:, pair % 2, 0:S], ACT.Copy).then_inc(o_hi, 1)

                def exponentials(h):
                    act.wait_ge(shift_done, h + 1)
                    if h >= B:
                        act.wait_ge(turned, h - B + 1)
                    for t in range(T):
                        c = T * h + t
                        act.activation(probs[:, h % B, t, :], source[:, h % B, t, :], ACT.Exp,
                                       bias=shift[:, c:c + 1], scale=scale,
                                       accum_out=total[:, c:c + 1]).then_inc(exp_done, 1)

                def move(h):
                    act.wait_ge(turned, h + 1)
                    if h >= 2:
                        act.wait_ge(pv_done, h - 1)
                    act.activation(probsT[:, h % 2, :, :], turn[:, h % 2, :, :], ACT.Copy).then_inc(moved, 1)

                for h in range(heads + B - 1):
                    if h < heads:
                        exponentials(h)
                    if h >= B - 1:
                        move(h - B + 1)
                    if h >= 5 and h % 2 == 1:
                        hi_of((h - 5) // 2)
                for pair in range((heads + B - 6) // 2 + 1, heads // 2):
                    hi_of(pair)
                if side:
                    side.scalar_end(act)

            @block.vector
            def _(dve):
                own = Chain(dve, dve_own)

                def maximum(h):
                    dve.wait_ge(scored, h + 1)
                    a = scores[:, h % B, :, :]
                    if far is not None:
                        if h >= B:
                            dve.wait_ge(exp_done, T * (h - B + 1))
                        slope = 2.0 ** (-8.0 * (h + 1) / heads)
                        a = biased[:, h % B, :, :]
                        dve.scalar_tensor_tensor(out=a, in0=far[:], scalar=slope / scale,
                                                 in1=scores[:, h % B, :, :], op0=ALU.mult,
                                                 op1=ALU.add).then_inc(bias_done, 1)
                        dve.wait_ge(bias_done, h + 1)
                    c = slice(T * h, T * h + T)
                    own(dve.tensor_reduce(top[:, c], a, AX.X, ALU.max))
                    dve.tensor_scalar(shift[:, c], top[:, c], -scale, None, ALU.mult).then_inc(shift_done, 1)

                def normalise(h):
                    dve.wait_ge(exp_done, T * (h + 1))
                    c = slice(T * h, T * h + T)
                    own(dve.reciprocal(inverse[:, c], total[:, c]))
                    a = probs[:, h % B, :, :]
                    dve.tensor_tensor(a, a, inverse[:, c].unsqueeze(2).to_broadcast([P, T, S]),
                                      ALU.mult).then_inc(normed, 1)

                def take(pair):
                    dve.wait_ge(o_hi, pair + 1)
                    rest_of(dve, oT.lo[:, pair, :], o[:, pair % 2, 0:S], oT.hi[:, pair, :]).then_inc(o_moved, 1)

                for h in range(heads + 1):
                    if h < heads:
                        maximum(h)
                    if h >= 1:
                        normalise(h - 1)
                    if h >= 6 and h % 2 == 0:
                        take(h // 2 - 3)
                for pair in range(heads // 2 - 2, heads // 2):
                    take(pair)
                if side:
                    side.vector(dve)



def mlp(nc, K, hT, w_in, w_out, conditions, following=()):
    PAIRS = D_FF // HALF
    TURNS = PAIRS // 2
    CH = 8
    LAG = 2
    panels = take_panels(K, 2 * PAIRS)
    slot_in, slot_out = ([(panels[0] + 2 * g + o) % SLOTS for g in range(2)] for o in range(2))
    at_in, at_out = ([arrived(panels[0] + 2 * g + o) for g in range(2)] for o in range(2))
    assert K.loaded == panels[0] + SLOTS
    K.loaded = panels[0] + 2 * PAIRS
    csum, ccols, w_ada = conditions
    HALVES = 2 * ADA // HALF
    STEPS = KC // 2
    with stage(nc, K, "mlp") as st:
        acc = st.ps("acc", [P, T, 2, HALF])
        hid = st.ps("hid", [P, 2, HALF])
        first_w, second_w = (Parts(st.mem, nc, f"{st.name}_{n}", [P, 2, PIECE]) for n in ("in", "out"))
        relu, act2 = (st.sb(n, [P, 2, S]) for n in ("relu", "act2"))
        hidden = Parts(st.mem, nc, f"{st.name}_hidden", [P, 4, S])
        ada_half = st.sb("ada_half", [P, 2, KC // 2, HALF])
        ada_in = [st.pool_sem(f"ada_in{n}") for n in range(2)]
        (hid_full, relu_done, act2_done, in_hi, in_split, out_hi, out_split, hidden_hi, hidden_split, act_used,
         summed, dve_own) = map(
            st.sem, ("hid_full", "relu_done", "act2_done", "in_hi", "in_split", "out_hi", "out_split", "hidden_hi",
                     "hidden_split", "act_used", "summed", "dve_own"))

        def src_in(n):
            return w_in.rearrange("(k p) n -> p k n", p=P)[:, :, bass.ds(n * HALF, HALF)]

        def src_out(n):
            return w_out[bass.ds(n * HALF, HALF), :].rearrange("(k p) n -> p k n", p=P)

        def raw_in(g, m):
            return ring_view(K, slot_in[g])[:, :, m * P:(m + 1) * P]

        def raw_out(g, m):
            return ring_view(K, slot_out[g], 4)[:, m, :]

        def by_row(a):
            return a.rearrange("p (k n) -> p k n", k=KC)

        with nc.Block(no_gpsimd_drain=True) as block:
            @block.sync
            def _(sp):
                with sp.Fori(0, TURNS - 1) as i:
                    for g in range(2):
                        sp.wait_ge(in_split, i * CH + 4 * (g + 1))
                        sp.dma_start(ring_view(K, slot_in[g]), src_in(2 * i + 2 + g)
                                     ).then_inc(K.ring_in[slot_in[g]], 16)
                        sp.wait_ge(out_split, i * CH + 4 * (g + 1))
                        sp.dma_start(ring_view(K, slot_out[g], 4), src_out(2 * i + 2 + g)
                                     ).then_inc(K.ring_in[slot_out[g]], 16)
                for n, panel in enumerate(following):
                    sp.wait_ge((in_split, out_split)[n % 2], (TURNS - 1) * CH + 4 * (n // 2 + 1))
                    start_panels(sp, K, [panel], in_split, K.loaded)

            @block.gpsimd
            def _(pool):
                def load(n, slot):
                    src = w_ada.rearrange("(a k p) n -> p a k n", a=2, p=P)[:, slot, :, bass.ds(n * HALF, HALF)]
                    pool.dma_start(ada_half[:, slot, :, :], src).then_inc(ada_in[slot], 16)

                for slot in range(2):
                    load(0, slot)
                with pool.Fori(1, HALVES // 2) as j:
                    for slot in range(2):
                        pool.wait_ge(summed, STEPS * (2 * j + (slot - 1)))
                        load(j, slot)

            @block.tensor
            def _(pe):
                for t in range(T):
                    for b in range(2):
                        pe.matmul(acc[:, t, b, :], K.ident[:], K.x[:, t, b * HALF:(b + 1) * HALF],
                                  start=True, stop=False, skip_group_check=True)
                pe.sem_inc(act_used, LAG)

                with pe.Fori(0, TURNS) as i:
                    def first(c):
                        if c >= 2:
                            pe.wait_ge(relu_done, i * CH + c - 1)
                        pe.wait_ge(in_split, i * CH + c + 1)
                        for k in range(KC):
                            mm = three_passes(pe, hid[:, c % 2, 0:S], first_w, hT,
                                              lambda x: x[:, c % 2, k * P:(k + 1) * P], lambda x: x[:, k, :],
                                              start=k == 0, stop=k == KC - 1)
                        mm.then_inc(hid_full, 1)

                    def second(c):
                        pe.wait_ge(hidden_split, i * CH + c + 1)
                        pe.wait_ge(out_split, i * CH + c + 1)
                        for t in range(T):
                            for b in range(2):
                                mm = three_passes(pe, acc[:, t, b, :], hidden, second_w,
                                                  lambda x: x[:, c % 4, t * P:(t + 1) * P],
                                                  lambda x: x[:, c % 2, b * HALF:(b + 1) * HALF],
                                                  start=False, stop=False, skip_group_check=True)
                        mm.then_inc(act_used, 1)

                    for c in range(CH + LAG):
                        if c < CH:
                            first(c)
                        if c >= LAG:
                            second(c - LAG)

            @block.scalar
            def _(act):
                with act.Fori(0, TURNS) as i:
                    def first(c):
                        g, m = c // 4, c % 4
                        if m == 0:
                            act.wait_ge(K.ring_in[slot_in[g]], 16 * i + at_in[g])
                        if c >= 2:
                            act.wait_ge(hid_full, i * CH + c - 1)
                        act.activation(by_row(first_w.hi[:, c % 2, :]), raw_in(g, m),
                                       ACT.Copy).then_inc(in_hi, 1)

                    def rectify(c):
                        act.wait_ge(hid_full, i * CH + c + 1)
                        act.activation(relu[:, c % 2, :], hid[:, c % 2, 0:S], ACT.Relu).then_inc(relu_done, 1)

                    def second(c):
                        g, m = c // 4, c % 4
                        if m == 0:
                            act.wait_ge(K.ring_in[slot_out[g]], 16 * i + at_out[g])
                        act.wait_ge(act_used, i * CH + (c + 1 - 2 + LAG))
                        act.activation(second_w.hi[:, c % 2, :], raw_out(g, m), ACT.Copy).then_inc(out_hi, 1)
                        act.wait_ge(act2_done, i * CH + c + 1)
                        act.activation(hidden.hi[:, c % 4, :], act2[:, c % 2, :],
                                       ACT.Copy).then_inc(hidden_hi, 1)

                    for c in range(CH + LAG):
                        if c >= LAG:
                            rectify(c - LAG)
                        if c < CH:
                            first(c)
                        if c >= LAG:
                            second(c - LAG)

            @block.vector
            def _(dve):
                own = Chain(dve, dve_own)
                with dve.Fori(0, TURNS) as i:
                    def first(c):
                        dve.wait_ge(in_hi, i * CH + c + 1)
                        rest_of(dve, by_row(first_w.lo[:, c % 2, :]), raw_in(c // 4, c % 4),
                                by_row(first_w.hi[:, c % 2, :])).then_inc(in_split, 1)

                    def square(c):
                        dve.wait_ge(relu_done, i * CH + c + 1)
                        a = relu[:, c % 2, :]
                        dve.tensor_tensor(act2[:, c % 2, :], a, a, ALU.mult).then_inc(act2_done, 1)

                    def second(c):
                        dve.wait_ge(out_hi, i * CH + c + 1)
                        rest_of(dve, second_w.lo[:, c % 2, :], raw_out(c // 4, c % 4),
                                second_w.hi[:, c % 2, :]).then_inc(out_split, 1)
                        dve.wait_ge(hidden_hi, i * CH + c + 1)
                        rest_of(dve, hidden.lo[:, c % 4, :], act2[:, c % 2, :],
                                hidden.hi[:, c % 4, :]).then_inc(hidden_split, 1)

                    def condition(step):
                        half, k = step // STEPS, step % STEPS
                        slot = half % 2
                        if k == 0:
                            dve.wait_ge(ada_in[slot], 48 * i + 16 * (half // 2 + 1))
                        if step:
                            dve.wait_ge(summed, 24 * i + step)
                        to = csum[:, bass.ds(3 * HALF * i + half // 2 * HALF, HALF)]
                        row = slot * STEPS + k
                        if row == 0:
                            ins = dve.tensor_scalar(to, ada_half[:, slot, k, :], ccols[:, 0:1], None, ALU.mult)
                        else:
                            ins = dve.scalar_tensor_tensor(out=to, in0=ada_half[:, slot, k, :],
                                                           scalar=ccols[:, row:row + 1], in1=to,
                                                           op0=ALU.mult, op1=ALU.add)
                        ins.then_inc(summed, 1)

                    for c in range(CH + LAG):
                        if c >= LAG:
                            square(c - LAG)
                        step = 3 * (c - 1)
                        if 0 < c <= CH:
                            condition(step)
                        if c < CH:
                            first(c)
                        if 0 < c <= CH:
                            condition(step + 1)
                        if c >= LAG:
                            second(c - LAG)
                        if 0 < c <= CH:
                            condition(step + 2)
                    dve.wait_ge(summed, 24 * i + 24)
                dve.wait_ge(act_used, CH * TURNS + LAG)
                for t in range(T):
                    own(dve.tensor_copy(K.x[:, t, :], acc[:, t, :, :].rearrange("p b n -> p (b n)")))



def gla_gates(nc, K, A, hT, logg):
    with stage(nc, K, "gla_gates") as st:
        wz = st.sb("wz", [P, KC, 2 * RANK])
        up = st.sb("up", [2 * RANK + 1, 2, HALF])
        zT = st.sb("zT", [2 * RANK + 1, S])
        size, e, ln = (st.sb(n, [P, 4, HALF]) for n in ("size", "e", "ln"))
        zps = st.ps("zps", [P, HALF])
        logit = st.ps("logit", [P, 4, HALF])
        loaded, cleared, up_loaded, z_done, z_moved, logit_done, act_own, ln_done, logg_done, dve_own = map(
            st.sem, ("loaded", "cleared", "up_loaded", "z_done", "z_moved", "logit_done", "act_own",
                     "ln_done", "logg_done", "dve_own"))
        z0 = 2 * GLA_H * GLA_DK + 2 * GLA_H * GLA_DV
        with nc.Block(no_gpsimd_drain=True) as block:
            @block.sync
            def _(sp):
                sp.dma_start(wz[:], A.gla_w_in[0][:, z0:z0 + 2 * RANK].rearrange("(k p) n -> p k n", p=P)
                             ).then_inc(loaded, 16)
                sp.wait_ge(cleared, 1)
                for r in range(2):
                    sp.dma_start(up[RANK * r:RANK * (r + 1), r, :], A.gla_w_gate_up[0][r]).then_inc(up_loaded, 16)
                sp.dma_start(up[2 * RANK:2 * RANK + 1, :, :], A.gla_b_gate).then_inc(up_loaded, 16)

            @block.tensor
            def _(pe):
                pe.wait_ge(loaded, 16)
                for k in range(KC):
                    for part in (hT.hi, hT.lo):
                        mm = pe.matmul(zps[0:2 * RANK, 0:S], wz[:, k, :], part[:, k, :].bitcast(F32),
                                       start=k == 0 and part is hT.hi, stop=k == KC - 1 and part is hT.lo)
                mm.then_inc(z_done, 1)
                pe.wait_ge(up_loaded, 16 * 3)
                pe.wait_ge(z_moved, 2)
                for n in range(4):
                    t, r = n // 2, n % 2
                    pe.matmul(logit[:, n, :], zT[:, t * P:(t + 1) * P], up[:, r, :], start=True,
                              stop=True).then_inc(logit_done, 1)

            @block.vector
            def _(dve):
                own = Chain(dve, dve_own)
                dve.memset(up[:], 0.0).then_inc(cleared, 1)
                dve.memset(zT[2 * RANK:2 * RANK + 1, :], 1.0).then_inc(z_moved, 1)
                dve.wait_ge(z_done, 1)
                dve.tensor_copy(zT[0:2 * RANK, :], zps[0:2 * RANK, 0:S]).then_inc(z_moved, 1)
                for n in range(4):
                    dve.wait_ge(ln_done, n + 1)
                    own(dve.scalar_tensor_tensor(out=logg[:, n // 2, n % 2, :], in0=logit[:, n, :], scalar=0.0,
                                                 in1=ln[:, n, :], op0=ALU.min, op1=ALU.subtract))

            @block.scalar
            def _(act):
                own = Chain(act, act_own)
                for n in range(4):
                    act.wait_ge(logit_done, n + 1)
                    own(act.activation(size[:, n, :], logit[:, n, :], ACT.Abs))
                for n in range(4):
                    own(act.activation(e[:, n, :], size[:, n, :], ACT.Exp, scale=-1.0))
                for n in range(4):
                    act.activation(ln[:, n, :], e[:, n, :], ACT.Ln, bias=1.0).then_inc(ln_done, 1)


def gla_scan(nc, K, q, k, v, logg, o):
    empty = [(K.loaded + n) % SLOTS for n in range(2)]
    assert K.loaded - K.used <= SLOTS - 2
    with stage(nc, K, "gla_scan") as st:
        tri = st.sb("tri", [P, 4, P])
        which = st.sb("which", [P, 2])
        eb, enb = (K.ring[:, empty[0], a:a + 2 * HALF].rearrange("p (s n) -> p s n", s=2) for a in (0, 2 * HALF))
        ed = st.sb("ed", [P, 2, HALF])
        qe, ke = (st.sb(n, [P, 2, HALF]) for n in ("qe", "ke"))
        kd = K.ring[:, empty[0], 4 * HALF:8 * HALF].rearrange("p (r t n) -> p r t n", r=2, t=T)
        qeT, keT = (st.sb(n, [P, 2, GLA_H, S]) for n in ("qeT", "keT"))
        decay = st.sb("decay", [P, 2, GLA_H, N_CHUNKS])
        aT = st.sb("aT", [P, 2, 2 * T, P])
        state = K.ring[:, empty[1], 0:12 * GLA_DV].rearrange("p (s r i n) -> p s r i n", s=2, r=2, i=3)
        wide = st.ps("wide", [P, 8, HALF])
        sums, turn = wide[:, 0:4, :], wide[:, 4:8, :]
        made, decayed, summed, exped, gated, turned, moved, pool_own, dve_own = map(
            st.sem, ("made", "decayed", "summed", "exped", "gated", "turned", "moved", "pool_own", "dve_own"))
        inner, masked, outer, stated, o_done, o_moved, kd_done = map(
            st.sem, ("inner", "masked", "outer", "stated", "o_done", "o_moved", "kd_done"))
        steps = [(r, t) for r in range(2) for t in range(T)]
        order = ((0, 1, 2), (3, 2, 1))
        place = {(0, 0): (2, 0), (0, 2): (2, S), (1, 1): (3, 0), (0, 1): (4, 0), (1, 0): (4, S), (1, 2): (7, 0)}

        def update(r, i):
            bank, column = place[r, i]
            return wide[:, bank, column:column + S]

        with nc.Block(no_gpsimd_drain=True) as block:
            @block.gpsimd
            def _(pool):
                own = Chain(pool, pool_own)
                own(pool.memset(tri[:], 1.0 / 16.0))
                own(pool.memset(which[:], 1.0 / 16.0))

                def keep(a, where, base, mult, step, op):
                    own(pool.affine_select(out=a, in_=a, compare_op=op, fill=0.0, base=base,
                                           pattern=[[step, where]], channel_multiplier=mult))

                keep(tri[:, 0, :], P, 0, -1, 1, ALU.is_ge)
                keep(tri[:, 1, :], P, 0, 1, -1, ALU.is_gt)
                keep(tri[:, 2, :], P, 0, 1, -1, ALU.is_ge)
                keep(tri[:, 3, :], P, 0, -1, 1, ALU.is_gt)
                for m in range(4):
                    own(pool.affine_select(out=tri[:, m, CHUNK:P], in_=tri[:, m, CHUNK:P],
                                           compare_op=ALU.is_ge, fill=0.0, base=-CHUNK,
                                           pattern=[[0, CHUNK]], channel_multiplier=1))
                    own(pool.affine_select(out=tri[:, m, 0:CHUNK], in_=tri[:, m, 0:CHUNK],
                                           compare_op=ALU.is_gt, fill=0.0, base=CHUNK,
                                           pattern=[[0, CHUNK]], channel_multiplier=-1))
                own(pool.affine_select(out=which[:, 1:2], in_=which[:, 1:2], compare_op=ALU.is_ge, fill=0.0,
                                       base=-CHUNK, pattern=[[0, 1]], channel_multiplier=1))
                own(pool.affine_select(out=which[:, 0:1], in_=which[:, 0:1], compare_op=ALU.is_gt, fill=0.0,
                                       base=CHUNK, pattern=[[0, 1]], channel_multiplier=-1))
                pool.memset(aT[:], 0.0).then_inc(made, 1)

            @block.tensor
            def _(pe):
                pe.wait_ge(made, 1)
                for r in range(2):
                    for h in range(GLA_H):
                        for t in range(T):
                            c = (r * GLA_H + h) * N_CHUNKS + 2 * t
                            mm = pe.matmul(turn[:, 3, c:c + 2], logg[:, t, r, h * P:(h + 1) * P], which[:],
                                           start=True, stop=True)
                mm.then_inc(decayed, 1)

                def sum_up(n):
                    r, t = steps[n]
                    if n >= 2:
                        pe.wait_ge(exped, 3 * (n - 1))
                    for m in range(2):
                        mm = pe.matmul(sums[:, n % 2 * 2 + m, :], tri[:, 2 * r + m, :], logg[:, t, r, :],
                                       start=True, stop=True)
                    mm.then_inc(summed, 1)

                def transposes(n):
                    pe.wait_ge(gated, 2 * n + 2)
                    for m, a in enumerate((qe, ke)):
                        u = 2 * n + m
                        if u >= 3:
                            pe.wait_ge(moved, u - 2)
                        for h in range(GLA_H):
                            mm = pe.transpose(turn[:, u % 3, h * P:(h + 1) * P],
                                              a[:, n % 2, h * P:(h + 1) * P], K.ident[:])
                        mm.then_inc(turned, 1)

                sum_up(0)
                for n in range(4):
                    if n + 1 < 4:
                        sum_up(n + 1)
                    transposes(n)

                def within(h):
                    if h >= 2:
                        pe.wait_ge(masked, h - 1)
                    for n, (r, t) in enumerate(steps):
                        mm = pe.matmul(wide[:, h % 2, n * P:(n + 1) * P], keT[:, r, h, t * P:(t + 1) * P],
                                       qeT[:, r, h, t * P:(t + 1) * P], start=True, stop=True)
                    mm.then_inc(inner, 1)

                def between(h):
                    if h >= 1:
                        pe.wait_ge(stated, 6 * h)
                    for r in range(2):
                        for i, n in enumerate(order[r]):
                            a = n % 2 * CHUNK
                            mm = pe.matmul(update(r, i),
                                           kd[a:a + CHUNK, r, n // 2, h * P:(h + 1) * P],
                                           v[a:a + CHUNK, n // 2, h * S:(h + 1) * S], start=True, stop=True)
                    mm.then_inc(outer, 1)

                def output(h):
                    pe.wait_ge(masked, h + 1)
                    pe.wait_ge(stated, 6 * (h + 1))
                    if h >= 2:
                        pe.wait_ge(o_moved, h - 1)
                    for t in range(T):
                        to = wide[:, 5 + h % 2, t * S:(t + 1) * S]
                        for r in range(2):
                            pe.matmul(to, aT[:, h % 2, 2 * r + t, :], v[:, t, h * S:(h + 1) * S],
                                      start=r == 0, stop=False, skip_group_check=True)
                        for c in range(2):
                            n = 2 * t + c
                            for r in range(2):
                                if n == (0, N_CHUNKS - 1)[r]:
                                    continue
                                i = n - 1 if r == 0 else N_CHUNKS - 2 - n
                                mm = pe.matmul(wide[c * CHUNK:(c + 1) * CHUNK, 5 + h % 2, t * S:(t + 1) * S],
                                               qeT[:, r, h, n * CHUNK:(n + 1) * CHUNK],
                                               state[:, h % 2, r, i, :], start=False, stop=True,
                                               skip_group_check=True)
                    mm.then_inc(o_done, 1)

                pe.wait_ge(moved, 8)
                pe.wait_ge(exped, 13)
                pe.wait_ge(kd_done, 4)
                for h in range(GLA_H + 1):
                    if h < GLA_H:
                        within(h)
                        between(h)
                    if h >= 1:
                        output(h - 1)

            @block.scalar
            def _(act):
                act.wait_ge(decayed, 1)
                act.activation(decay[:].rearrange("p r h n -> p (r h n)"), turn[:, 3, 0:2 * GLA_H * N_CHUNKS],
                               ACT.Exp).then_inc(exped, 1)

                def exponentials(n):
                    act.wait_ge(summed, n + 1)
                    if n >= 2:
                        act.wait_ge(gated, 2 * (n - 1))
                        act.wait_ge(kd_done, n - 1)
                    s = n % 2
                    act.activation(eb[:, s, :], sums[:, 2 * s, :], ACT.Exp).then_inc(exped, 1)
                    act.activation(enb[:, s, :], sums[:, 2 * s, :], ACT.Exp, scale=-1.0).then_inc(exped, 1)
                    act.activation(ed[:, s, :], sums[:, 2 * s + 1, :], ACT.Exp).then_inc(exped, 1)

                def move(n):
                    r, t = steps[n]
                    for m, to in enumerate((qeT, keT)):
                        u = 2 * n + m
                        act.wait_ge(turned, u + 1)
                        act.activation(to[:, r, :, t * P:(t + 1) * P],
                                       turn[:, u % 3, :].rearrange("p (h n) -> p h n", h=GLA_H),
                                       ACT.Copy).then_inc(moved, 1)

                exponentials(0)
                for n in range(4):
                    if n + 1 < 4:
                        exponentials(n + 1)
                    move(n)
                for h in range(GLA_H):
                    act.wait_ge(o_done, h + 1)
                    act.activation(o[:, :, h, :], wide[:, 5 + h % 2, :].rearrange("p (t n) -> p t n", t=T),
                                   ACT.Copy).then_inc(o_moved, 1)

            @block.vector
            def _(dve):
                own = Chain(dve, dve_own)
                for n, (r, t) in enumerate(steps):
                    dve.wait_ge(exped, 1 + 3 * (n + 1))
                    if n >= 2:
                        dve.wait_ge(turned, 2 * (n - 1))
                    s = n % 2
                    dve.tensor_tensor(qe[:, s, :], q[:, t, :], eb[:, s, :], ALU.mult).then_inc(gated, 1)
                    dve.tensor_tensor(ke[:, s, :], k[:, t, :], enb[:, s, :], ALU.mult).then_inc(gated, 1)
                    dve.tensor_tensor(kd[:, r, t, :], k[:, t, :], ed[:, s, :], ALU.mult).then_inc(kd_done, 1)
                dve.wait_ge(made, 1)
                for h in range(GLA_H):
                    dve.wait_ge(inner, h + 1)
                    if h >= 2:
                        dve.wait_ge(o_done, h - 1)
                    for r in range(2):
                        mask = tri[:, 2 * r:2 * r + 1, :].bitcast(U32).to_broadcast([P, T, P])
                        ins = dve.copy_predicated(
                            aT[:, h % 2, 2 * r:2 * r + 2, :], mask,
                            wide[:, h % 2, 2 * r * P:2 * (r + 1) * P].rearrange("p (t n) -> p t n", t=T))
                        if r == 0:
                            own(ins)
                    ins.then_inc(masked, 1)
                    dve.wait_ge(outer, h + 1)
                    for r in range(2):
                        for i, n in enumerate(order[r]):
                            u = 3 * r + i
                            chunk = update(r, i)
                            to = state[:, h % 2, r, i, :]
                            if i == 0:
                                dve.tensor_copy(to, chunk).then_inc(stated, 1)
                            else:
                                dve.wait_ge(stated, 6 * h + u)
                                dve.scalar_tensor_tensor(out=to, in0=state[:, h % 2, r, i - 1, :],
                                                         scalar=decay[:, r, h, n:n + 1], in1=chunk,
                                                         op0=ALU.mult, op1=ALU.add).then_inc(stated, 1)


def gla_out(nc, K, A, o, gate, oT, panels, side_of):
    with stage(nc, K, "gla_out") as st:
        gain = st.sb("gain", [P, GLA_DV])
        squares = st.sb("squares", [P, T, D])
        ms, std, rstd = (st.sb(n, [P, T * GLA_H]) for n in ("ms", "std", "rstd"))
        tp = st.ps("tp", [P, 2 * T, HALF])
        side = side_of(st)
        loaded, squared, ms_done, std_done, gated, turned, hi_done, dve_own = map(
            st.sem, ("loaded", "squared", "ms_done", "std_done", "gated", "turned", "hi_done", "dve_own"))

        def halves(a, n):
            t, h = n // 2, n % 2
            return a[:, 4 * h:4 * h + 4, t * P:(t + 1) * P]

        def bank(n):
            return tp[:, n, :].rearrange("p (k n) -> p k n", k=4)

        with nc.Block(no_gpsimd_drain=True) as block:
            @block.sync
            def _(sp):
                sp.dma_start(gain[:], A.gla_out_norm[0:1, :].partition_broadcast(P)).then_inc(loaded, 16)
                side.sync(sp)
                start_panels(sp, K, panels)

            @block.scalar
            def _(act):
                act.activation(squares[:].rearrange("p t (h d) -> p t h d", h=GLA_H), o[:],
                               ACT.Square).then_inc(squared, 1)
                act.wait_ge(ms_done, 1)
                act.activation(std[:], ms[:], ACT.Sqrt).then_inc(std_done, 1)
                for n in range(2 * T):
                    act.wait_ge(turned, n + 1)
                    act.activation(halves(oT.hi, n), bank(n), ACT.Copy).then_inc(hi_done, 1)

            @block.vector
            def _(dve):
                own = Chain(dve, dve_own)
                dve.wait_ge(squared, 1)
                own(dve.tensor_reduce(ms[:], squares[:].rearrange("p t (h d) -> p (t h) d", h=GLA_H), AX.X,
                                      ALU.add))
                dve.tensor_scalar(ms[:], ms[:], 1.0 / GLA_DV, EPS, ALU.mult, ALU.add).then_inc(ms_done, 1)
                dve.wait_ge(loaded, 16)
                g = gate.rearrange("p t (h d) -> p t h d", h=GLA_H)
                for t in range(T):
                    own(dve.tensor_tensor(g[:, t], g[:, t], gain[:].unsqueeze(1).to_broadcast([P, GLA_H, GLA_DV]),
                                          ALU.mult))
                dve.wait_ge(std_done, 1)
                own(dve.reciprocal(rstd[:], std[:]))
                for t in range(T):
                    r = rstd[:, t * GLA_H:(t + 1) * GLA_H].unsqueeze(2).to_broadcast([P, GLA_H, GLA_DV])
                    own(dve.tensor_tensor(o[:, t], o[:, t], r, ALU.mult))
                    dve.tensor_tensor(o[:, t], o[:, t], g[:, t], ALU.mult).then_inc(gated, 1)
                for n in range(2 * T):
                    dve.wait_ge(hi_done, n + 1)
                    rest_of(dve, halves(oT.lo, n), bank(n), halves(oT.hi, n))
                side.vector(dve)

            @block.tensor
            def _(pe):
                side.tensor(pe)
                for n in range(2 * T):
                    t, h = n // 2, n % 2
                    pe.wait_ge(gated, t + 1)
                    for k in range(4):
                        f = 4 * h + k
                        mm = pe.transpose(tp[:, n, k * P:(k + 1) * P], o[:, t, f // 2, f % 2 * P:(f % 2 + 1) * P],
                                          K.ident[:])
                    mm.then_inc(turned, 1)


def residual(nc, K, lhs, scale=None, following=()):
    panels = take_panels(K, 2)
    with stage(nc, K, "residual") as st:
        w = Parts(st.mem, nc, st.name, [P, PIECES, PIECE])
        ps = st.ps("ps", [P, 4, HALF])
        if scale is not None:
            scaled, factor = (st.sb(n, [P, 2, HALF]) for n in ("scaled", "factor"))
            given = st.ps("given", [P, D])
        hi_done, split_done, piece_used, given_done, factor_done, dve_own = map(
            st.sem, ("hi_done", "split_done", "piece_used", "given_done", "factor_done", "dve_own"))
        with nc.Block(no_gpsimd_drain=True) as block:
            @block.sync
            def _(sp):
                start_panels(sp, K, following, split_done, panels[0])

            @block.tensor
            def _(pe):
                if scale is not None:
                    give(pe, K, given, *scale).then_inc(given_done, 1)
                for n in range(2):
                    for c in range(4):
                        piece = 4 * n + c
                        a = piece % PIECES
                        pe.wait_ge(split_done, piece + 1)
                        for kk in range(2):
                            k = 2 * c + kk
                            for t in range(T):
                                mm = three_passes(pe, ps[:, 2 * n + t, :], lhs, w,
                                                  lambda x: x[:, k, t * P:(t + 1) * P],
                                                  lambda x: x[:, a, kk * HALF:(kk + 1) * HALF],
                                                  start=k == 0, stop=k == KC - 1)
                        mm.then_inc(piece_used, 1)

            @block.scalar
            def _(act):
                for n, i in enumerate(panels):
                    for c in range(4):
                        split_piece(act, K, w, i, c, 4 * n + c, piece_used, hi_done)
                    if n == 0 and scale is not None:
                        act.wait_ge(given_done, 1)
                        act.activation(factor[:].rearrange("p b n -> p (b n)"), given[:],
                                       ACT.Copy).then_inc(factor_done, 1)

            @block.vector
            def _(dve):
                own = Chain(dve, dve_own)

                def add(n):
                    dve.wait_ge(piece_used, 4 * n + 4)
                    if scale is not None:
                        dve.wait_ge(factor_done, 1)
                    for t in range(T):
                        x = K.x[:, t, n * HALF:(n + 1) * HALF]
                        y = ps[:, 2 * n + t, :]
                        if scale is not None:
                            own(dve.tensor_tensor(scaled[:, t, :], y, factor[:, n, :], ALU.mult))
                            y = scaled[:, t, :]
                        own(dve.tensor_tensor(x, x, y, ALU.add))

                for n, i in enumerate(panels):
                    for c in range(4):
                        rest_of_piece(dve, K, w, i, c, 4 * n + c, hi_done, split_done)
                        if n == 1 and c == 2:
                            add(0)
                add(1)


def block_one(nc, K, A):
    gains = A.norm_mix, A.norm_mlp

    def gain(kind, layer):
        return gains[kind][layer:layer + 1, :]

    def wide(w, panels):
        return [(columns(w, n), KC) for n in panels]

    def pairs(layer, numbers):
        w_in, w_out = A.mlp_w_in[layer], A.mlp_w_out[layer]
        return [panel for n in numbers
                for panel in ((columns(w_in, n), KC),
                              (w_out[n * HALF:(n + 1) * HALF, :].rearrange("(k p) n -> p k n", p=P), 4))]

    def conditions(layer, csum):
        return csum, K.c_cols, A.w_ada_2[layer]

    w_qkv, w_o, w_gla = A.attn_w_qkv[0], A.attn_w_o[0], A.gla_w_in[0]
    begin_ring(nc, K)
    setup(nc, K, A, [])
    with ExitStack() as mem:
        def sb(name, shape):
            return mem.enter_context(nc.sbuf_tensor(name, shape, F32))

        hT = Parts(mem, nc, "attn_hT", [P, KC, S])
        norm(nc, K, gain(0, 0), hT=hT, panels=wide(w_qkv, range(3)) + wide(w_o, range(1)))
        qkv = sb("qkv", [P, T, (QK_HEADS + N_KV) * HD])
        qT = sb("qT", [P, N_HEADS // 2, S])
        kT = sb("kT", [P, N_KV, S])
        project(nc, K, hT, ["tokens"] * 3,
                lambda act, n, t, ps: act.activation(qkv[:, t, n * HALF:(n + 1) * HALF], ps, ACT.Copy),
                following=wide(w_o, range(1, 2)) + pairs(0, range(1)))
        rope(nc, K, qkv, qT, kT, A, lambda st: Tables(st, K))
        v0 = QK_HEADS * HD
        attend(nc, K, N_HEADS, HD ** -0.5,
               lambda h: qT[h % 2 * HD:h % 2 * HD + HD, h // 2, :],
               lambda h: kT[h % 2 * HD:h % 2 * HD + HD, h // (N_HEADS // N_KV), :],
               lambda h, k: qkv[:, k, v0 + h // (N_HEADS // N_KV) * HD:v0 + (h // (N_HEADS // N_KV) + 1) * HD],
               hT)
        residual(nc, K, hT, following=pairs(0, range(1, 2)))
    with ExitStack() as conds:
        csum = conds.enter_context(nc.sbuf_tensor("csum0", [P, ADA], F32))
        with ExitStack() as mem:
            hT = Parts(mem, nc, "mlp0_hT", [P, KC, S])
            norm(nc, K, gain(1, 0), hT=hT)
            mlp(nc, K, hT, A.mlp_w_in[0], A.mlp_w_out[0], conditions(0, csum), following=wide(w_gla, range(SLOTS)))
        with ExitStack() as mem:
            def sb(name, shape):
                return mem.enter_context(nc.sbuf_tensor(name, shape, F32))

            q, k = (sb(n, [P, T, HALF]) for n in ("q", "k"))
            v, gate = (sb(n, [P, T, D]) for n in ("v", "gate"))
            logg = sb("logg", [P, T, 2, HALF])

            def evacuate(act, n, t, ps):
                if n == 0:
                    return act.activation(q[:, t, :], ps, ACT.Copy, scale=GLA_DK ** -0.5)
                if n == 1:
                    return act.activation(k[:, t, :], ps, ACT.Copy)
                to, c = (v, n - 2) if n < 4 else (gate, n - 4)
                return act.activation(to[:, t, c * HALF:(c + 1) * HALF], ps, ACT.Copy if n < 4 else ACT.Silu)

            with ExitStack() as inner:
                hT = Parts(inner, nc, "gla_hT", [P, KC, S])
                norm(nc, K, gain(0, 1), hT=hT)
                project(nc, K, hT, ["tokens"] * 6, evacuate, own_panels=wide(w_gla, range(SLOTS, 6)),
                        following=wide(A.gla_w_o[0], range(2)))
                gla_gates(nc, K, A, hT, logg)
            o = logg[:].rearrange("p t r n -> p (t r n)").rearrange("p (t h d) -> p t h d", t=T, h=GLA_H)
            gla_scan(nc, K, q, k, v, logg, o)
            oT = Parts(mem, nc, "oT", [P, KC, S])
            gla_out(nc, K, A, o, gate[:], oT, pairs(1, range(1)), lambda st: Conditions(st, K, csum, A.b_ada_2[0], 0))
            residual(nc, K, oT, following=pairs(1, range(1, 2)))
    with nc.sbuf_tensor("csum1", [P, ADA], F32) as csum:
        with ExitStack() as mem:
            hT = Parts(mem, nc, "mlp1_hT", [P, KC, S])
            norm(nc, K, gain(1, 1), hT=hT)
            mlp(nc, K, hT, A.mlp_w_in[1], A.mlp_w_out[1], conditions(1, csum))
        norm(nc, K, A.final_norm.rearrange("(a n) -> a n", a=1), keep=K.x,
             side_of=lambda st: Conditions(st, K, csum, A.b_ada_2[1], 1))




class Tables:

    def __init__(self, st, K):
        self.K = K
        self.whole = st.sb("whole", [P, T, S], mybir.dt.int32)
        self.few = st.sb("few", [P, TOPK], mybir.dt.int32)
        self.own_sem = st.sem("tables_own")

    def gpsimd(self, pool):
        own = Chain(pool, self.own_sem)
        far = self.K.far
        own(pool.iota(self.whole[:], pattern=[[-P, T], [1, S]], base=0, channel_multiplier=-1))
        own(pool.tensor_copy(far[:], self.whole[:]))
        own(pool.affine_select(out=far[:], in_=far[:], compare_op=ALU.is_ge, fill=MASKED, base=0,
                               pattern=[[P, T], [-1, S]], channel_multiplier=1))
        own(pool.iota(self.few[:], pattern=[[1, TOPK]], base=0, channel_multiplier=0))
        own(pool.tensor_copy(self.K.places[:], self.few[:]))
        own(pool.memset(self.K.zeros[:], 0.0))


class Convolution:

    def __init__(self, st, K, conv_w, b, c, h, hi, lo):
        self.K, self.conv_w, self.b, self.c, self.h, self.hi, self.lo = K, conv_w, b, c, h, hi, lo
        self.rows = st.sb("conv_rows", [CONV_K * 4, P])
        self.w = st.sb("conv_cols", [P, CONV_K, 4])
        self.turned = st.ps("conv_turn", [P, HALF])
        self.z, self.part = (st.sb(n, [P, 4, S]) for n in ("conv_z", "conv_part"))
        self.loaded, self.cols_done, self.cols_moved, self.done, self.hi_done, self.own_sem = map(
            st.sem, ("conv_loaded", "conv_cols_done", "conv_cols_moved", "conv_done", "conv_hi_done",
                     "conv_own"))

    def sync(self, sp):
        sp.dma_start(self.rows[:], self.conv_w).then_inc(self.loaded, 16)

    def tensor(self, pe):
        pe.wait_ge(self.loaded, 16)
        pe.transpose(self.turned[:, 0:12], self.rows[:], self.K.ident[0:12, 0:12]).then_inc(self.cols_done, 1)

    def scalar(self, act):
        act.wait_ge(self.cols_done, 1)
        act.activation(self.w[:].rearrange("p k c -> p (k c)"), self.turned[:, 0:12],
                       ACT.Copy).then_inc(self.cols_moved, 1)

    def gpsimd(self, pool):
        own = Chain(pool, self.own_sem)
        own(pool.tensor_tensor(self.z[:], self.c[:], self.h[:], ALU.mult))
        pool.wait_ge(self.cols_moved, 1)

        def weight(k, n):
            return self.w[:, k, :].unsqueeze(2).to_broadcast([P, 4, n])

        y = self.c
        own(pool.tensor_tensor(y[:], self.z[:], weight(2, S), ALU.mult))
        for back in (1, 2):
            n = S - back
            own(pool.tensor_tensor(self.part[:, :, 0:n], self.z[:, :, 0:n], weight(2 - back, n), ALU.mult))
            own(pool.tensor_tensor(y[:, :, back:S], y[:, :, back:S], self.part[:, :, 0:n], ALU.add))
        pool.tensor_tensor(y[:], y[:], self.b[:], ALU.mult).then_inc(self.done, 1)

    def scalar_end(self, act):
        act.wait_ge(self.done, 1)
        act.activation(self.hi, self.c[:], ACT.Copy).then_inc(self.hi_done, 1)

    def vector(self, dve):
        dve.wait_ge(self.hi_done, 1)
        rest_of(dve, self.lo, self.c[:], self.hi)


def merge(nc, K, y, gates, following):
    panels = take_panels(K, 2)
    with stage(nc, K, "merge") as st:
        w = Parts(st.mem, nc, st.name, [P, PIECES, PIECE])
        wide = st.ps("wide", [P, 2, 4, HALF])
        hi_done, split_done, piece_used, gated, turned, turned_hi, dve_own = map(
            st.sem, ("hi_done", "split_done", "piece_used", "gated", "turned", "turned_hi", "dve_own"))

        def halves(a, n):
            t, h = n // 2, n % 2
            return a[:, 4 * h:4 * h + 4, t * P:(t + 1) * P]

        def bank(n):
            return wide[:, 0, n, :].rearrange("p (k n) -> p k n", k=4)

        with nc.Block(no_gpsimd_drain=True) as block:
            @block.sync
            def _(sp):
                start_panels(sp, K, following, split_done, panels[0])

            @block.tensor
            def _(pe):
                for a in range(2):
                    for k in range(4):
                        piece = 4 * a + k
                        pe.wait_ge(split_done, piece + 1)
                        for t in range(T):
                            for b in range(2):
                                mm = three_passes(pe, wide[:, a, 2 * t + b, :], y, w,
                                                  lambda x: x[:, piece, t * P:(t + 1) * P],
                                                  lambda x: x[:, piece % PIECES, b * HALF:(b + 1) * HALF],
                                                  start=k == 0, stop=k == 3)
                        mm.then_inc(piece_used, 1)
                for n in range(2 * T):
                    t, h = n // 2, n % 2
                    pe.wait_ge(gated, t + 1)
                    for k in range(4):
                        f = (4 * h + k) * P
                        mm = pe.transpose(wide[:, 0, n, k * P:(k + 1) * P], gates[:, 0, t, f:f + P], K.ident[:])
                    mm.then_inc(turned, 1)

            @block.vector
            def _(dve):
                own = Chain(dve, dve_own)

                def gate(a, t):
                    dve.wait_ge(piece_used, 4 * a + 4)
                    own(dve.tensor_tensor(gates[:, a, t, :], gates[:, a, t, :],
                                          wide[:, a, 2 * t:2 * t + 2, :].rearrange("p b n -> p (b n)"),
                                          ALU.mult))

                for a, i in enumerate(panels):
                    for c in range(4):
                        rest_of_piece(dve, K, w, i, c, 4 * a + c, hi_done, split_done)
                        if a == 1 and c >= 2:
                            gate(0, c - 2)
                for t in range(T):
                    gate(1, t)
                    dve.tensor_tensor(gates[:, 0, t, :], gates[:, 0, t, :], gates[:, 1, t, :],
                                      ALU.add).then_inc(gated, 1)
                for n in range(2 * T):
                    dve.wait_ge(turned_hi, n + 1)
                    rest_of(dve, halves(y.lo, n), bank(n), halves(y.hi, n))

            @block.scalar
            def _(act):
                for a, i in enumerate(panels):
                    for c in range(4):
                        split_piece(act, K, w, i, c, 4 * a + c, piece_used, hi_done)
                for n in range(2 * T):
                    act.wait_ge(turned, n + 1)
                    act.activation(halves(y.hi, n), bank(n), ACT.Copy).then_inc(turned_hi, 1)


def peer(nc, K, A, l, h2, h2T, sub_keys, g2):
    VS = 8
    U_LAYER = 16 * 2 * PH
    V_LAYER = U_LAYER * TOPK // VS
    AHEAD = 24
    rows_u = A.expert_u_2.rearrange("l e d -> (l e) d")
    rows_v = A.expert_v_2.rearrange("l e d -> (l e) d")
    EARLY = {8: (0, 1), 9: (2, 3), 10: (4, 5), 11: (6, 7), 12: (8, 9), 13: (10, 11)}
    BY_DVE = range(1, TOPK, 2)
    M = 2 * PH
    panels = take_panels(K, SLOTS)

    def u_row(j):
        return K.ring[:, panels[j // 4] % SLOTS, j % 4 * D:(j % 4 + 1) * D]

    with stage(nc, K, "peer") as st:
        w = Parts(st.mem, nc, st.name, [P, PIECES, PIECE])
        scores = st.sb("scores", [P, T, PH, 2 * NKEYS])
        v_slot = st.sb("v_slot", [P, VS, D])
        now, rest = (st.sb(n, [P, 2 * NKEYS]) for n in ("now", "rest"))
        value = st.sb("value", [P, 2, TOPK])
        place = st.sb("place", [P, 2, TOPK], U32)
        place_f = st.sb("place_f", [P, 2, TOPK])
        sums, left = (st.sb(n, [P, TOPK * TOPK]) for n in ("sums", "left"))
        best = st.sb("best", [P, T, TOPK])
        best_at = st.sb("best_at", [P, TOPK], U32)
        half = st.sb("half", [P, 2, TOPK], U32)
        half_f = st.sb("half_f", [P, 2, TOPK])
        hot = st.sb("hot", [P, 2, TOPK, TOPK])
        key = st.sb("key", [P, 2, TOPK])
        expert_f = st.sb("expert_f", [P, TOPK])
        at_u, at_v = (st.sb(n, [P, T, TOPK], U32) for n in ("at_u", "at_v"))
        shift, total, inverse = (st.sb(n, [P, T]) for n in ("shift", "total", "inverse"))
        e, gate, dots, gelu, weight = (st.sb(n, [P, T, TOPK]) for n in ("e", "gate", "dots", "gelu", "weight"))
        diagonal = [st.sb(f"diagonal{t}", [P, TOPK, P]) for t in range(T)]
        scaled, factor = h2, u_row(1)
        keys = diagonal[0][:]
        keysT = diagonal[1][:, 0:2, :]
        q = diagonal[1][:, 4:8, :].rearrange("p (s t) n -> p s t n", s=2)
        q_ps = st.ps("q_ps", [P, 2, HALF])
        keys_ps = q_ps[:, :, S:S + P]
        scores_ps = st.ps("scores_ps", [P, 2, HALF])
        y = st.ps("y", [P, T, 2, HALF])
        u_in = [st.pool_sem(f"u_in{j}") for j in range(TOPK)]
        v_in = [st.pool_sem(f"v_in{j}") for j in range(VS)]
        (keys_in, hi_done, split_done, q_done, q_moved, keys_moved, scored, scores_moved,
         given_done, factor_done) = map(
            st.sem, ("keys_in", "hi_done", "split_done", "q_done", "q_moved", "keys_moved",
                     "scored", "scores_moved", "given_done", "factor_done"))
        (at_u_ready, at_v_ready, dots_done, shift_done, e_done, gelu_done, weight_done,
         diagonal_ready, v_used, v_by_dve, paced, dve_own) = map(
            st.sem, ("at_u_ready", "at_v_ready", "dots_done", "shift_done", "e_done",
                     "gelu_done", "weight_done", "diagonal_ready", "v_used", "v_by_dve", "paced", "dve_own"))

        def by_row(a):
            return a.rearrange("p (k n) -> p k n", k=KC)

        def by_pe(rows):
            return rows - len([j for j in BY_DVE if j < rows])

        with nc.Block() as block:
            @block.sync
            def _(sp):
                for half_m in range(2):
                    m = slice(half_m * PH, (half_m + 1) * PH)
                    sp.dma_start(keys[:, m, :], sub_keys[half_m * 4:half_m * 4 + 4].rearrange(
                        "h a n d -> n (h a) d")).then_inc(keys_in, 16)

            @block.gpsimd
            def _(pool):
                def gather_u(n, t, j):
                    pool.indirect_dma_start(
                        u_row(j), None, rows_u,
                        bass.IndirectOffsetOnAxis(ap=at_u[:, t, j:j + 1], axis=0)).then_inc(u_in[j], 16)

                def gather_v(t, j):
                    pool.indirect_dma_start(
                        v_slot[:, j % VS, :], None, rows_v,
                        bass.IndirectOffsetOnAxis(ap=at_v[:, t, j:j + 1], axis=0)).then_inc(v_in[j % VS], 16)

                def unit(n, t, last, start=0, start_u=0):
                    pool.wait_ge(at_v_ready, n + 1)
                    if not last:
                        pool.wait_ge(at_u_ready, n + 2)
                    for j in range(TOPK):
                        if j >= start:
                            if last and j - VS in BY_DVE:
                                pool.wait_ge(v_by_dve, BY_DVE.index(j - VS) + 1)
                            else:
                                before = j + 1 - VS
                                if last and before > 0:
                                    before = by_pe(before)
                                pool.wait_ge(v_used, 16 * n + (before + AHEAD))
                            pool.sem_inc(paced, 1)
                            gather_v(t, j)
                        if not last and j >= start_u:
                            pool.wait_ge(dots_done, 16 * n + (j + 1))
                            pool.sem_inc(paced, 1)
                            gather_u(n + 1, 1 - t, j)

                SECOND = 6
                pool.wait_ge(at_u_ready, 1)
                pool.wait_ge(at_v_ready, 1)
                for j in range(TOPK):
                    if j == TOPK - 4:
                        pool.wait_ge(at_u_ready, 2)
                        for i in range(SECOND):
                            pool.wait_ge(dots_done, i + 1)
                            gather_u(1, 1, i)
                    if j % 4 == 0:
                        pool.wait_ge(split_done, j + 4)
                    gather_u(0, 0, j)
                    if j < VS:
                        gather_v(0, j)
                unit(0, 0, False, start=VS, start_u=SECOND)
                with pool.Fori(0, PH - 1) as h:
                    for t in (1, 0):
                        unit(2 * h + 2 - t, t, False)
                unit(M - 1, 1, True)

            @block.vector
            def _(dve):
                own = Chain(dve, dve_own)

                def sixteen(*lists):
                    own.several(*(dve.max(v[:, 0:8], source) for v, _, source, _ in lists))
                    own.several(*(ins for v, place, source, spare in lists
                                  for ins in (dve.max_index(place[:, 0:8], v[:, 0:8], source),
                                              dve.match_replace(spare, v[:, 0:8], source, GONE))))
                    own.several(*(dve.max(v[:, 8:16], spare) for v, _, _, spare in lists))
                    own.several(*(dve.max_index(place[:, 8:16], v[:, 8:16], spare)
                                  for v, place, _, spare in lists))

                def choose(head, t):
                    square = [P, TOPK, TOPK]
                    own(dve.tensor_copy(now[:], scores[:, t, bass.ds(head, 1), :].rearrange("p a n -> p (a n)")))
                    sixteen(*((value[:, a, :], place[:, a, :], now[:, a * NKEYS:(a + 1) * NKEYS],
                               rest[:, a * NKEYS:(a + 1) * NKEYS]) for a in range(2)))
                    own.several(dve.tensor_copy(place_f[:], place[:]),
                                dve.tensor_tensor(sums[:].rearrange("p (a b) -> p a b", b=TOPK),
                                                  value[:, 0, :].unsqueeze(2).to_broadcast(square),
                                                  value[:, 1, :].unsqueeze(1).to_broadcast(square), ALU.add))
                    sixteen((best[:, t, :], best_at[:], sums[:], left[:]))
                    dve.tensor_scalar(shift[:, t:t + 1], best[:, t, 0:1], -1.0, None,
                                      ALU.mult).then_inc(shift_done, 1)
                    own.several(dve.tensor_scalar(half[:, 0, :], best_at[:], 4, None, ALU.logical_shift_right),
                                dve.tensor_scalar(half[:, 1, :], best_at[:], 15, None, ALU.bitwise_and))
                    own(dve.tensor_copy(half_f[:], half[:]))
                    own.several(*(dve.tensor_tensor(hot[:, a], half_f[:, a, :].unsqueeze(2).to_broadcast(square),
                                                    K.places[:].unsqueeze(1).to_broadcast(square), ALU.is_equal)
                                  for a in range(2)))
                    own.several(*(dve.tensor_tensor(hot[:, a], hot[:, a],
                                                    place_f[:, a, :].unsqueeze(1).to_broadcast(square), ALU.mult)
                                  for a in range(2)))
                    own(dve.tensor_reduce(key[:], hot[:], AX.X, ALU.add))
                    own(dve.scalar_tensor_tensor(out=expert_f[:], in0=key[:, 0, :], scalar=float(NKEYS),
                                                 in1=key[:, 1, :], op0=ALU.mult, op1=ALU.add))
                    dve.tensor_scalar(at_u[:, t, :], expert_f[:], K.layer_base[:, 0:1], None,
                                      ALU.add).then_inc(at_u_ready, 1)

                def keep_for_v(n, t):
                    dve.wait_ge(v_used, 16 * n + AHEAD)
                    dve.wait_ge(at_u_ready, n + 2)
                    dve.tensor_copy(at_v[:, t, :], at_u[:, t, :]).then_inc(at_v_ready, 1)

                def dot(n, t, j):
                    dve.wait_ge(u_in[j], l * U_LAYER + 16 * n + 16)
                    dve.tensor_tensor_reduce(u_row(j), u_row(j), h2[:, t, :], 1.0, 0.0, ALU.mult, ALU.add,
                                             dots[:, t, j:j + 1]).then_inc(dots_done, 1)

                def unit(n, t, head=None, start=0, last=False):
                    if head is not None:
                        choose(head, 1 - t)
                    for j in range(start, TOPK):
                        dot(n, t, j)
                    dve.wait_ge(e_done, n + 1)
                    own(dve.reciprocal(inverse[:, t:t + 1], total[:, t:t + 1]))
                    own(dve.tensor_scalar(gate[:, t, :], e[:, t, :], inverse[:, t:t + 1], None, ALU.mult))
                    dve.wait_ge(gelu_done, n + 1)
                    dve.tensor_tensor(weight[:, t, :], gelu[:, t, :], gate[:, t, :],
                                      ALU.mult).then_inc(weight_done, 1)
                    if not last:
                        keep_for_v(n, 1 - t)

                for c in range(M):
                    dve.wait_ge(hi_done, c + 1)
                    a = c % PIECES
                    rest_of(dve, by_row(w.lo[:, a, :]), chunk_of(K, panels[c // 4], c % 4),
                            by_row(w.hi[:, a, :])).then_inc(split_done, 1)
                    if c == 4:
                        dve.wait_ge(scores_moved, 2)
                        choose(0, 0)
                        dve.wait_ge(at_u_ready, 1)
                        dve.tensor_copy(at_v[:, 0, :], at_u[:, 0, :]).then_inc(at_v_ready, 1)
                    if c == 7:
                        choose(0, 1)
                    for j in EARLY.get(c, ()):
                        dot(0, 0, j)
                dve.wait_ge(scores_moved, M)
                unit(0, 0, start=sum(map(len, EARLY.values())))
                own.clear()
                with dve.Fori(0, PH - 1) as h:
                    with own.turn():
                        for t in (1, 0):
                            unit(2 * h + 2 - t, t, head=h + 1)
                unit(M - 1, 1, last=True)

                def give_x(t, sums_of):
                    own(dve.tensor_tensor(scaled[:, t, :], sums_of, factor, ALU.mult))
                    own(dve.tensor_tensor(K.x[:, t, :], K.x[:, t, :], scaled[:, t, :], ALU.add))

                n, also = M - 1, u_row(0)
                dve.wait_ge(dots_done, M * TOPK)
                dve.wait_ge(weight_done, M)
                for i, j in enumerate(BY_DVE):
                    dve.wait_ge(v_in[j % VS], l * V_LAYER + 32 * n + 16 * (j // VS + 1))
                    if i == 0:
                        dve.tensor_scalar(also, v_slot[:, j % VS, :], weight[:, 1, j:j + 1], None,
                                          ALU.mult).then_inc(v_by_dve, 1)
                    else:
                        dve.wait_ge(v_by_dve, i)
                        dve.scalar_tensor_tensor(out=also, in0=v_slot[:, j % VS, :], scalar=weight[:, 1, j:j + 1],
                                                 in1=also, op0=ALU.mult, op1=ALU.add).then_inc(v_by_dve, 1)
                    if i == 4:
                        dve.wait_ge(v_used, 16 * (M - 1) + AHEAD)
                        dve.wait_ge(factor_done, 1)
                        give_x(0, y[:, 0, :, :].rearrange("p b n -> p (b n)"))
                own(dve.tensor_scalar(K.layer_base[:], K.layer_base[:], float(EXPERTS), None, ALU.add))
                dve.wait_ge(v_by_dve, len(BY_DVE))
                dve.wait_ge(v_used, 16 * (M - 1) + by_pe(TOPK) + AHEAD)
                own(dve.tensor_tensor(also, also, y[:, 1, :, :].rearrange("p b n -> p (b n)"), ALU.add))
                give_x(1, also)

            @block.scalar
            def _(act):
                def split(c):
                    if c % 4 == 0:
                        act.wait_ge(K.ring_in[panels[c // 4] % SLOTS], arrived(panels[c // 4]))
                    if c >= PIECES:
                        act.wait_ge(q_done, c - PIECES + 1)
                    act.activation(by_row(w.hi[:, c % PIECES, :]), chunk_of(K, panels[c // 4], c % 4),
                                   ACT.Copy).then_inc(hi_done, 1)

                def move_queries(c):
                    act.wait_ge(q_done, c + 1)
                    act.activation(q[:, c % 2, :, :], q_ps[:, c % 2, 0:S].rearrange("p (t n) -> p t n", t=T),
                                   ACT.Copy).then_inc(q_moved, 1)
                    act.activation(keysT[:, c % 2, :], keys_ps[:, c % 2, :], ACT.Copy).then_inc(keys_moved, 1)

                def move_scores(c):
                    act.wait_ge(scored, c + 1)
                    a = c % 2 * NKEYS
                    act.activation(scores[:, :, c // 2, a:a + NKEYS],
                                   scores_ps[:, c % 2, 0:S].rearrange("p (t n) -> p t n", t=T),
                                   ACT.Copy).then_inc(scores_moved, 1)

                for c in range(3):
                    split(c)
                for c in range(2):
                    move_queries(c)
                split(3)
                for c in range(2):
                    move_scores(c)
                for c in range(4, M + 3):
                    if c < M:
                        split(c)
                    if c >= 5:
                        move_scores(c - 3)
                    if c < M + 2:
                        move_queries(c - 2)
                act.wait_ge(scored, M)

                def gates(n, t):
                    act.wait_ge(shift_done, n + 1)
                    act.activation(e[:, t, :], best[:, t, :], ACT.Exp, bias=shift[:, t:t + 1],
                                   accum_out=total[:, t:t + 1]).then_inc(e_done, 1)

                def unit(n, t, last):
                    if not last:
                        gates(n + 1, 1 - t)
                    act.wait_ge(dots_done, 16 * n + 16)
                    act.activation(gelu[:, t, :], dots[:, t, :], ACT.Gelu_apprx_tanh).then_inc(gelu_done, 1)
                    act.wait_ge(weight_done, n + 1)
                    act.wait_ge(v_used, 16 * n + (AHEAD - 16))
                    for j in range(TOPK):
                        if last and j in BY_DVE:
                            continue
                        act.activation(diagonal[t][:, j, :], K.ident[:], ACT.Copy,
                                       scale=weight[:, t, j:j + 1]).then_inc(diagonal_ready, 1)

                gates(0, 0)
                with act.Fori(0, PH - 1) as h:
                    for t in range(T):
                        unit(2 * h + t, t, False)
                unit(2 * PH - 2, 0, False)
                unit(2 * PH - 1, 1, True)
                act.wait_ge(given_done, 1)
                act.activation(factor, q_ps[:].rearrange("p b n -> p (b n)"), ACT.Copy).then_inc(factor_done, 1)

            @block.tensor
            def _(pe):
                pe.sem_inc(v_used, AHEAD)
                pe.wait_ge(keys_in, 32)

                def project_chunk(c):
                    if c >= 2:
                        pe.wait_ge(q_moved, c - 1)
                        pe.wait_ge(keys_moved, c - 1)
                    pe.transpose(keys_ps[:, c % 2, :], keys[:, c, :], K.ident[:])
                    pe.wait_ge(split_done, c + 1)
                    for k in range(KC):
                        mm = three_passes(pe, q_ps[:, c % 2, 0:S], w, h2T,
                                          lambda x: x[:, c % PIECES, k * P:(k + 1) * P], lambda x: x[:, k, :],
                                          start=k == 0, stop=k == KC - 1)
                    mm.then_inc(q_done, 1)

                def score(c):
                    pe.wait_ge(q_moved, c + 1)
                    pe.wait_ge(keys_moved, c + 1)
                    if c >= 2:
                        pe.wait_ge(scores_moved, c - 1)
                    for t in range(T):
                        mm = pe.matmul(scores_ps[:, c % 2, t * P:(t + 1) * P], q[:, c % 2, t, :],
                                       keysT[:, c % 2, :], start=True, stop=True)
                    mm.then_inc(scored, 1)

                for c in range(2):
                    project_chunk(c)
                for c in range(2):
                    score(c)
                for c in range(2, M + 1):
                    if c < M:
                        project_chunk(c)
                    if c >= 3:
                        score(c - 1)
                give(pe, K, q_ps[:].rearrange("p b n -> p (b n)"), l, g2).then_inc(given_done, 1)
                for t in range(T):
                    for b in range(2):
                        mm = pe.matmul(y[:, t, b, :], K.zeros[:, 0:P], K.zeros[:], start=True, stop=False,
                                       skip_group_check=True)

                def unit(n, t, last=False):
                    for j in range(TOPK):
                        if last and j in BY_DVE:
                            continue
                        pe.wait_ge(diagonal_ready, 16 * n + (by_pe(j + 1) if last else j + 1))
                        pe.wait_ge(v_in[j % VS], l * V_LAYER + 32 * n + 16 * (j // VS + 1))
                        for b in range(2):
                            mm = pe.matmul(y[:, t, b, :], diagonal[t][:, j, :],
                                           v_slot[:, j % VS, b * HALF:(b + 1) * HALF], start=False, stop=False,
                                           skip_group_check=True)
                        mm.then_inc(v_used, 1)

                with pe.Fori(0, PH - 1) as h:
                    for t in range(T):
                        unit(2 * h + t, t)
                unit(M - 2, 0)
                unit(M - 1, 1, last=True)


def block_two(nc, K, A):
    with nc.Fori(0, LAYERS) as l:
        begin_ring(nc, K)

        def layer(w):
            return w[bass.ds(l, 1)]

        def matrix(w):
            return layer(w).rearrange("a k n -> (a k) n")

        SHIFT1, SCALE1, GATE1, SHIFT2, SCALE2, GATE2 = range(6)

        def wide(w, panels):
            return [(columns(w, n), KC) for n in panels]

        w_in, w_out, w_query = (matrix(w) for w in (A.w_in_2, A.w_out_2, A.w_query_2))
        proj = [matrix(w).rearrange("(k p) n -> p k n", p=P) for w in (A.w_attn_proj_2, A.w_conv_proj_2)]
        with ExitStack() as mem:
            hT = Parts(mem, nc, "mix_hT", [P, KC, S])
            norm(nc, K, layer(A.norm1_g_2), modulate=(l, SCALE1, SHIFT1), hT=hT,
                 panels=wide(w_in, range(SLOTS)))
            with ExitStack() as inner:
                def sb(name, shape):
                    return inner.enter_context(nc.sbuf_tensor(name, shape, F32))

                turned = {n: sb(f"mix_{n}", [P, 4, S]) for n in ("q", "k", "b", "c", "h")}
                v = sb("mix_v", [P, T, HALF])
                gates = sb("mix_gates", [P, 2, T, D])
                kinds = ["q", "k", "v", "b", "c", "h", 0, 1, 2, 3]

                def evacuate(act, n, half, ps):
                    kind = kinds[n]
                    if kind == "v":
                        return act.activation(v[:, half, :], ps, ACT.Copy)
                    if kind in turned:
                        return act.activation(turned[kind][:, 2 * half:2 * half + 2, :], ps, ACT.Copy)
                    return act.activation(gates[:, kind // 2, half, kind % 2 * HALF:(kind % 2 + 1) * HALF], ps,
                                          ACT.Sigmoid)

                project(nc, K, hT, ["features" if k in turned else "tokens" for k in kinds], evacuate,
                        own_panels=wide(w_in, range(SLOTS, len(kinds))),
                        following=[(w, 4) for w in proj] + wide(w_out, range(2)))

                def head(a):
                    return lambda h: turned[a][h % 2 * HD:h % 2 * HD + HD, h // 2, :]

                conv_w = layer(A.conv_w_2).rearrange("a k (c p) -> (a k c) p", p=P)
                attend(nc, K, MH, HD ** -0.5, head("q"), head("k"),
                       lambda h, k: v[:, k, h * HD:(h + 1) * HD], hT, far=K.far,
                       side_of=lambda st: Convolution(st, K, conv_w, turned["b"], turned["c"], turned["h"],
                                                      hT.hi[:, 4:8, :], hT.lo[:, 4:8, :]))
                merge(nc, K, hT, gates, following=wide(w_query, range(2)))
            residual(nc, K, hT, scale=(l, GATE1),
                     following=wide(w_query, range(2, 4)))
        with ExitStack() as mem:
            h2 = mem.enter_context(nc.sbuf_tensor("h2", [P, T, D], F32))
            h2T = Parts(mem, nc, "h2T", [P, KC, S])
            norm(nc, K, layer(A.norm2_g_2), modulate=(l, SCALE2, SHIFT2), hT=h2T, keep=h2)
            peer(nc, K, A, l, h2, h2T, layer(A.sub_keys_2).rearrange("l h a n d -> (l h) a n d"), GATE2)



def program(nc, A, out):
    K = Kept()
    K.stages = K.pool_sems = 0
    with ExitStack() as kept:
        def sb(name, shape, dt=F32):
            return kept.enter_context(nc.sbuf_tensor(name, shape, dt))

        K.ring = sb("ring", [P, SLOTS, PANEL])
        K.x = sb("x", [P, T, D])
        K.ident = sb("ident", [P, P])
        K.pick = sb("pick", [P, 6, 6])
        K.select = sb("select", [6, 6, P])
        K.ada = sb("ada", [6, LAYERS * D])
        K.c_cols = sb("c_cols", [P, KC])
        K.layer_base = sb("layer_base", [P, 1])
        K.far = sb("far", [P, T, S])
        K.places = sb("places", [P, TOPK])
        K.zeros = sb("zeros", [P, HALF])
        K.ring_in = [kept.enter_context(nc.semaphore(f"ring_in{n}")) for n in range(SLOTS)]

        block_one(nc, K, A)
        block_two(nc, K, A)
        begin_ring(nc, K)
        norm(nc, K, A.final_g_2.rearrange("(a n) -> a n", a=1), out=out)


_INS = ["x", "norm_mix", "norm_mlp", "attn_w_qkv", "attn_q_norm", "attn_k_norm", "attn_w_o", "gla_w_in",
        "gla_w_gate_up", "gla_b_gate", "gla_out_norm", "gla_w_o", "mlp_w_in", "mlp_w_out", "final_norm",
        "c_2", "norm1_g_2", "norm2_g_2", "w_ada_2", "b_ada_2", "w_in_2", "conv_w_2", "w_attn_proj_2",
        "w_conv_proj_2", "w_out_2", "w_query_2", "sub_keys_2", "expert_u_2", "expert_v_2", "final_g_2"]


def rope_table():
    half = HD // 2
    inv = np.float32(10000.0) ** (-np.arange(0, half, 2, dtype=np.float32) / np.float32(half))
    pos = np.stack([np.arange(S) // 64, np.arange(S) % 64], 1).astype(np.float32)
    ang = pos[:, :, None] * inv[None, None, :]
    cos = np.repeat(np.cos(ang)[:, :, None, :], 2, axis=2).reshape(S, HD)
    sin = (np.sin(ang)[:, :, None, :] * np.array([-1, 1], np.float32)[None, None, :, None]).reshape(S, HD)
    return np.ascontiguousarray(np.stack([cos, sin], 1).astype(np.float32))


def kernel(**inputs):
    import numpy as _np
    import concourse.bacc as _bacc
    from concourse import mybir as _mybir
    from concourse.bass_utils import run_bass_kernel_spmd as _run

    nc = _bacc.Bacc("TRN2", target_bir_lowering=False, num_devices=1)
    A = Kept()
    arrays = {}

    def declare(name, a):
        arrays[f"in_{name}_dram"] = a
        return nc.dram_tensor(f"in_{name}_dram", a.shape, _mybir.dt.from_np(a.dtype), kind="ExternalInput").ap()

    ins = {name: declare(name, _np.ascontiguousarray(inputs[name])) for name in _INS}
    ins["rope_table"] = declare("rope_table", rope_table())
    A.__dict__.update(ins)
    out = nc.dram_tensor("out_0_dram", (1, S, D), _mybir.dt.float32, kind="ExternalOutput").ap()
    program(nc, A, out)
    r = _run(nc, [arrays], core_ids=[0])
    return r.results[0]["out_0_dram"]
```
